# Optimizing a Trainium2 kernel written in Bass

```python
import math
import jax, jax.numpy as jnp
from jax import lax
import numpy as np

D_MODEL = 1024
BATCH = 1
SEQ = 512
DEPTH = 1

HEAD_DIM = 64
BLOCK = 128
RMS_EPS = 1e-6
SUBLN_EPS = 1e-5
A_HEADS = 4
A_QK = A_HEADS * 2 * HEAD_DIM
A_WIDTH = A_HEADS * 2 * HEAD_DIM
B_HEADS = 8
B_KV_HEADS = 2
B_GROUP = B_HEADS // B_KV_HEADS
B_WIDTH = B_HEADS * HEAD_DIM
B_KV = B_KV_HEADS * HEAD_DIM
WINDOW = 128
C_HEADS = 8
C_WIDTH = C_HEADS * HEAD_DIM
N_BRANCH = 3
SPLITS = (A_QK, A_QK, A_WIDTH, A_WIDTH,
          B_WIDTH, B_KV, B_KV, B_WIDTH,
          C_WIDTH, C_WIDTH, C_WIDTH, C_HEADS, C_WIDTH,
          N_BRANCH * D_MODEL)
D_IN = sum(SPLITS)


def rms_norm(x, gain, eps):
    xf = x.astype(jnp.float32)
    y = xf * lax.rsqrt(jnp.mean(xf * xf, axis=-1, keepdims=True) + eps)
    return (y * gain.astype(jnp.float32)).astype(x.dtype)

def alibi_slopes(n_heads):
    return 2.0 ** (-8.0 * jnp.arange(1, n_heads + 1, dtype=jnp.float32) / n_heads)

def diff_attention(q, k, v, lam, slopes):
    B, S, H, _, d = q.shape
    nb = S // BLOCK
    scale = d ** -0.5
    qb = jnp.moveaxis(q.reshape(B, nb, BLOCK, H, 2, d), 1, 0)
    k_pos = jnp.arange(S)

    def one_block(args):
        qblk, start = args
        s = jnp.einsum('bqhmd,bkhmd->bhmqk', qblk, k).astype(jnp.float32) * scale
        dist = (start + jnp.arange(BLOCK))[:, None] - k_pos[None, :]
        bias = jnp.where(dist >= 0, -slopes[:, None, None] * dist.astype(jnp.float32), -jnp.inf)
        p = jax.nn.softmax(s + bias[None, :, None], axis=-1)
        w = p[:, :, 0] - lam * p[:, :, 1]
        return jnp.einsum('bhqk,bkhe->bqhe', w.astype(v.dtype), v)

    out = lax.map(one_block, (qb, jnp.arange(nb) * BLOCK))
    return jnp.moveaxis(out, 0, 1).reshape(B, S, H, v.shape[-1])

def sliding_window_attention(q, k, v, sinks, slopes):
    B, S, HQ, d = q.shape
    KV = k.shape[2]
    G = HQ // KV
    nb = S // BLOCK
    scale = d ** -0.5
    qb = q.reshape(B, nb, BLOCK, KV, G, d)

    def banded(t):
        tb = t.reshape(B, nb, BLOCK, KV, d)
        prev = jnp.concatenate([jnp.zeros_like(tb[:, :1]), tb[:, :-1]], axis=1)
        return jnp.concatenate([prev, tb], axis=2)

    kb, vb = banded(k), banded(v)
    s = jnp.einsum('bnqhgd,bnkhd->bnhgqk', qb, kb).astype(jnp.float32) * scale
    i = jnp.arange(BLOCK)[:, None]
    j = jnp.arange(2 * BLOCK)[None, :]
    dist = i - j + BLOCK
    key_pos = jnp.arange(nb)[:, None, None] * BLOCK + j - BLOCK
    valid = (dist >= 0) & (dist < WINDOW) & (key_pos >= 0)
    bias = -slopes.reshape(KV, G)[:, :, None, None] * dist.astype(jnp.float32)
    s = jnp.where(valid[None, :, None, None], s + bias[None, None], -jnp.inf)
    sink = sinks.astype(jnp.float32).reshape(KV, G)[None, None, :, :, None, None]
    m = jnp.maximum(jnp.max(s, axis=-1, keepdims=True), sink)
    e = jnp.exp(s - m)
    p = e / (jnp.sum(e, axis=-1, keepdims=True) + jnp.exp(sink - m))
    out = jnp.einsum('bnhgqk,bnkhd->bnqhgd', p.astype(v.dtype), vb)
    return out.reshape(B, S, HQ * d)

def forgetting_attention(q, k, v, logf):
    B, S, H, d = q.shape
    nb = S // BLOCK
    scale = d ** -0.5
    c = jnp.cumsum(logf, axis=1)
    c_k = jnp.transpose(c, (0, 2, 1))
    qb = jnp.moveaxis(q.reshape(B, nb, BLOCK, H, d), 1, 0)
    cb = jnp.moveaxis(c.reshape(B, nb, BLOCK, H), 1, 0)
    k_pos = jnp.arange(S)

    def one_block(args):
        qblk, cblk, start = args
        s = jnp.einsum('bqhd,bkhd->bhqk', qblk, k).astype(jnp.float32) * scale
        decay = jnp.transpose(cblk, (0, 2, 1))[:, :, :, None] - c_k[:, :, None, :]
        dist = (start + jnp.arange(BLOCK))[:, None] - k_pos[None, :]
        s = jnp.where((dist >= 0)[None, None], s + decay, -jnp.inf)
        p = jax.nn.softmax(s, axis=-1)
        return jnp.einsum('bhqk,bkhd->bqhd', p.astype(v.dtype), v)

    out = lax.map(one_block, (qb, cb, jnp.arange(nb) * BLOCK))
    return jnp.moveaxis(out, 0, 1).reshape(B, S, H * d)

def first_inputs(seed: int = 0) -> dict:
    key = jax.random.key(seed)
    ks = jax.random.split(key, 16)
    f32 = jnp.float32
    nrm = lambda k, shape: jax.random.normal(k, shape, dtype=f32)
    return {
        "x": nrm(ks[0], (BATCH, SEQ, D_MODEL)),
        "norm_gain": 1.0 + 0.05 * nrm(ks[1], (DEPTH, D_MODEL)),
        "w_in": nrm(ks[2], (DEPTH, D_MODEL, D_IN)) * D_MODEL ** -0.5,
        "b_forget": 0.1 * nrm(ks[3], (DEPTH, C_HEADS)),
        "lambda_q1": 0.1 * nrm(ks[4], (DEPTH, HEAD_DIM)),
        "lambda_k1": 0.1 * nrm(ks[5], (DEPTH, HEAD_DIM)),
        "lambda_q2": 0.1 * nrm(ks[6], (DEPTH, HEAD_DIM)),
        "lambda_k2": 0.1 * nrm(ks[7], (DEPTH, HEAD_DIM)),
        "subln_gain": 1.0 + 0.05 * nrm(ks[8], (DEPTH, 2 * HEAD_DIM)),
        "sinks": 0.5 * nrm(ks[9], (DEPTH, B_HEADS)),
        "w_up_a": nrm(ks[10], (DEPTH, A_WIDTH, D_MODEL)) * A_WIDTH ** -0.5,
        "w_up_b": nrm(ks[11], (DEPTH, B_WIDTH, D_MODEL)) * B_WIDTH ** -0.5,
        "w_up_c": nrm(ks[12], (DEPTH, C_WIDTH, D_MODEL)) * C_WIDTH ** -0.5,
        "w_o": nrm(ks[13], (DEPTH, D_MODEL, D_MODEL)) * D_MODEL ** -0.5,
        "final_gain": 1.0 + 0.05 * nrm(ks[14], (D_MODEL,)),
    }

def first_block(x, norm_gain, w_in, b_forget, lambda_q1, lambda_k1, lambda_q2, lambda_k2,
              subln_gain, sinks, w_up_a, w_up_b, w_up_c, w_o, final_gain):
    B, S, D = x.shape
    offsets = np.cumsum(SPLITS)[:-1].tolist()
    slopes_a = alibi_slopes(A_HEADS)
    slopes_b = alibi_slopes(B_HEADS)
    for l in range(DEPTH):
        h = rms_norm(x, norm_gain[l], RMS_EPS)
        proj = jnp.einsum('bsd,de->bse', h, w_in[l])
        (qa, ka, va, ga, qb, kb, vb, gb,
         qc, kc, vc, fc, gc, gm) = jnp.split(proj, offsets, axis=-1)

        lam_init = 0.8 - 0.6 * math.exp(-0.3 * l)
        lam = (jnp.exp(jnp.sum(lambda_q1[l].astype(jnp.float32) * lambda_k1[l].astype(jnp.float32)))
               - jnp.exp(jnp.sum(lambda_q2[l].astype(jnp.float32) * lambda_k2[l].astype(jnp.float32)))
               + lam_init)
        ya = diff_attention(qa.reshape(B, S, A_HEADS, 2, HEAD_DIM),
                            ka.reshape(B, S, A_HEADS, 2, HEAD_DIM),
                            va.reshape(B, S, A_HEADS, 2 * HEAD_DIM), lam, slopes_a)
        ya = (rms_norm(ya, subln_gain[l], SUBLN_EPS) * (1.0 - lam_init)).reshape(B, S, A_WIDTH)

        yb = sliding_window_attention(qb.reshape(B, S, B_HEADS, HEAD_DIM),
                                      kb.reshape(B, S, B_KV_HEADS, HEAD_DIM),
                                      vb.reshape(B, S, B_KV_HEADS, HEAD_DIM),
                                      sinks[l], slopes_b)

        logf = jax.nn.log_sigmoid(fc.astype(jnp.float32) + b_forget[l].astype(jnp.float32))
        yc = forgetting_attention(qc.reshape(B, S, C_HEADS, HEAD_DIM),
                                  kc.reshape(B, S, C_HEADS, HEAD_DIM),
                                  vc.reshape(B, S, C_HEADS, HEAD_DIM), logf)

        ua = jnp.einsum('bse,ed->bsd', ya * jax.nn.silu(ga), w_up_a[l])
        ub = jnp.einsum('bse,ed->bsd', yb * jax.nn.silu(gb), w_up_b[l])
        uc = jnp.einsum('bse,ed->bsd', yc * jax.nn.silu(gc), w_up_c[l])
        gates = jax.nn.sigmoid(gm.reshape(B, S, N_BRANCH, D))
        merged = gates[:, :, 0] * ua + gates[:, :, 1] * ub + gates[:, :, 2] * uc
        x = x + jnp.einsum('bsd,de->bse', merged, w_o[l])
    return rms_norm(x, final_gain, RMS_EPS)


D_MIX = D_MODEL
RG_WIDTH = 3 * D_MIX // 8
HG_WIDTH = 3 * D_MIX // 8
SC_WIDTH = D_MIX - RG_WIDTH - HG_WIDTH
RG_HEADS = RG_WIDTH // HEAD_DIM
HG_HEADS = HG_WIDTH // HEAD_DIM
RG_CONV = 4
SC_CONV = 3
FFN_CONV = 3
RG_C = 8.0
HG_CHUNK = 64
D_FF = 2816
PLE_DIM = 256
EPS = 1e-6
PROJ_SIZES = [RG_WIDTH, RG_WIDTH,
              HG_WIDTH, HG_WIDTH, HG_WIDTH, HG_WIDTH,
              SC_WIDTH, SC_WIDTH, SC_WIDTH]
N_PROJ = sum(PROJ_SIZES)
PROJ_SPLITS = [int(s) for s in np.cumsum(PROJ_SIZES)[:-1]]


def rmsnorm(x, gain):
    xf = x.astype(jnp.float32)
    y = xf * lax.rsqrt(jnp.mean(xf * xf, axis=-1, keepdims=True) + EPS)
    return (y * gain.astype(jnp.float32)).astype(x.dtype)

def head_rmsnorm(y, gain):
    b, t, w = y.shape
    yh = y.reshape(b, t, w // HEAD_DIM, HEAD_DIM)
    yh = yh * lax.rsqrt(jnp.mean(yh * yh, axis=-1, keepdims=True) + EPS)
    return yh.reshape(b, t, w) * gain.astype(jnp.float32)

def causal_dwconv(x, w):
    k = w.shape[0]
    return lax.conv_general_dilated(
        x, w[:, None, :].astype(x.dtype), window_strides=(1,), padding=[(k - 1, 0)],
        dimension_numbers=('NWC', 'WIO', 'NWC'), feature_group_count=x.shape[-1])

def _linear_combine(c1, c2):
    a1, b1 = c1
    a2, b2 = c2
    return a1 * a2, a2 * b1 + b2

def rglru_group(u_in, gate_in, conv_w, conv_b, w_r, b_r, w_i, b_i, lam, gain):
    b, t, _ = u_in.shape
    u = (causal_dwconv(u_in, conv_w) + conv_b.astype(u_in.dtype)).astype(jnp.float32)
    uh = u.reshape(b, t, RG_HEADS, HEAD_DIM)
    r = jax.nn.sigmoid(jnp.einsum('btnd,nde->btne', uh, w_r.astype(jnp.float32))
                       + b_r.astype(jnp.float32)).reshape(b, t, RG_WIDTH)
    ig = jax.nn.sigmoid(jnp.einsum('btnd,nde->btne', uh, w_i.astype(jnp.float32))
                        + b_i.astype(jnp.float32)).reshape(b, t, RG_WIDTH)
    log_a = -RG_C * r * jax.nn.softplus(-lam.astype(jnp.float32))
    a = jnp.exp(log_a)
    beta = jnp.sqrt(-jnp.expm1(2.0 * log_a))
    _, h = lax.associative_scan(_linear_combine, (a, beta * ig * u), axis=1)
    return head_rmsnorm(h * jax.nn.gelu(gate_in.astype(jnp.float32)), gain)

def hgrn2_group(q, f_raw, v, g, lb, gain):
    b, t, _ = q.shape
    nc = t // HG_CHUNK
    qf = jax.nn.silu(q.astype(jnp.float32)) * HEAD_DIM ** -0.5
    f = lb + (1.0 - lb) * jax.nn.sigmoid(f_raw.astype(jnp.float32))
    log_f = jnp.log(f)
    k = 1.0 - f

    def to_chunks(u):
        return u.reshape(b, nc, HG_CHUNK, HG_HEADS, HEAD_DIM).transpose(1, 0, 3, 2, 4)

    mask = jnp.tril(jnp.ones((HG_CHUNK, HG_CHUNK), dtype=bool))[:, :, None]

    def step(S, inp):
        qc, kc, vc, lfc = inp
        G = jnp.cumsum(lfc, axis=2)
        o_inter = jnp.einsum('bhtk,bhkv->bhtv', qc * jnp.exp(G), S)
        diff = G[:, :, :, None, :] - G[:, :, None, :, :]
        decay = jnp.where(mask, jnp.exp(jnp.minimum(diff, 0.0)), 0.0)
        scores = jnp.einsum('bhtk,bhsk,bhtsk->bhts', qc, kc, decay)
        o_intra = jnp.einsum('bhts,bhsv->bhtv', scores, vc)
        G_last = G[:, :, -1:, :]
        S_new = (jnp.exp(G_last[:, :, 0, :])[..., None] * S
                 + jnp.einsum('bhsk,bhsv->bhkv', kc * jnp.exp(G_last - G), vc))
        return S_new, o_inter + o_intra

    S0 = jnp.zeros((b, HG_HEADS, HEAD_DIM, HEAD_DIM), jnp.float32)
    _, o = lax.scan(step, S0, (to_chunks(qf), to_chunks(k),
                               to_chunks(v.astype(jnp.float32)), to_chunks(log_f)))
    o = o.transpose(1, 0, 3, 2, 4).reshape(b, t, HG_WIDTH)
    return head_rmsnorm(o, gain) * jax.nn.silu(g.astype(jnp.float32))

def shortconv_group(bg, cg, v, conv_w, gain):
    y = bg * causal_dwconv(cg * v, conv_w)
    return head_rmsnorm(y.astype(jnp.float32), gain)

def conv_ffn(h, w_up, conv_w, w_down):
    gu = causal_dwconv(h @ w_up, conv_w)
    g, u = jnp.split(gu, 2, axis=-1)
    return (jax.nn.silu(g) * u) @ w_down

def second_inputs(seed: int = 0) -> dict:
    key = jax.random.key(seed)
    ks = jax.random.split(key, 24)
    n = jax.random.normal
    f32 = jnp.float32
    u = jax.random.uniform(ks[10], (DEPTH, RG_WIDTH), f32, 0.9, 0.999)
    a0 = u ** (1.0 / RG_C)
    rg_lambda = jnp.log(a0) - jnp.log1p(-a0)
    return {
        'x': n(ks[0], (BATCH, SEQ, D_MODEL), f32),
        'p': n(ks[1], (DEPTH, BATCH, SEQ, PLE_DIM), f32),
        'norm_mix_gain': 1.0 + 0.02 * n(ks[2], (DEPTH, D_MODEL), f32),
        'w_in': n(ks[3], (DEPTH, D_MODEL, N_PROJ), f32) * D_MODEL ** -0.5,
        'rg_conv_w': n(ks[4], (DEPTH, RG_CONV, RG_WIDTH), f32) * RG_CONV ** -0.5,
        'rg_conv_b': 0.01 * n(ks[5], (DEPTH, RG_WIDTH), f32),
        'rg_w_r': n(ks[6], (DEPTH, RG_HEADS, HEAD_DIM, HEAD_DIM), f32) * HEAD_DIM ** -0.5,
        'rg_b_r': 0.01 * n(ks[7], (DEPTH, RG_HEADS, HEAD_DIM), f32),
        'rg_w_i': n(ks[8], (DEPTH, RG_HEADS, HEAD_DIM, HEAD_DIM), f32) * HEAD_DIM ** -0.5,
        'rg_b_i': 0.01 * n(ks[9], (DEPTH, RG_HEADS, HEAD_DIM), f32),
        'rg_lambda': rg_lambda,
        'hg_lower_bounds': 0.1 * n(ks[11], (DEPTH, HG_WIDTH), f32),
        'sc_conv_w': n(ks[12], (DEPTH, SC_CONV, SC_WIDTH), f32) * SC_CONV ** -0.5,
        'mix_out_gain': 1.0 + 0.02 * n(ks[13], (DEPTH, D_MIX), f32),
        'w_out': n(ks[14], (DEPTH, D_MIX, D_MODEL), f32) * D_MIX ** -0.5,
        'norm_ffn_gain': 1.0 + 0.02 * n(ks[15], (DEPTH, D_MODEL), f32),
        'ffn_w_up': n(ks[16], (DEPTH, D_MODEL, 2 * D_FF), f32) * D_MODEL ** -0.5,
        'ffn_conv_w': n(ks[17], (DEPTH, FFN_CONV, 2 * D_FF), f32) * FFN_CONV ** -0.5,
        'ffn_w_down': n(ks[18], (DEPTH, D_FF, D_MODEL), f32) * D_FF ** -0.5,
        'ple_w_proj': n(ks[19], (DEPTH, PLE_DIM, D_MODEL), f32) * PLE_DIM ** -0.5,
        'ple_w_gate': n(ks[20], (DEPTH, D_MODEL, D_MODEL), f32) * D_MODEL ** -0.5,
        'final_norm_gain': 1.0 + 0.02 * n(ks[21], (D_MODEL,), f32),
    }

def second_block(x, p, norm_mix_gain, w_in, rg_conv_w, rg_conv_b, rg_w_r, rg_b_r, rg_w_i, rg_b_i,
              rg_lambda, hg_lower_bounds, sc_conv_w, mix_out_gain, w_out, norm_ffn_gain,
              ffn_w_up, ffn_conv_w, ffn_w_down, ple_w_proj, ple_w_gate, final_norm_gain):
    dt = x.dtype
    sm = jax.nn.softmax(hg_lower_bounds.astype(jnp.float32), axis=0)
    lower_bound = jnp.cumsum(sm, axis=0) - sm[0:1]
    for i in range(DEPTH):
        h = rmsnorm(x, norm_mix_gain[i])
        z = h @ w_in[i]
        a_u, a_gate, b_q, b_f, b_v, b_g, c_b, c_c, c_v = jnp.split(z, PROJ_SPLITS, axis=-1)
        g_a, g_b, g_c = jnp.split(mix_out_gain[i], [RG_WIDTH, RG_WIDTH + HG_WIDTH])
        y_a = rglru_group(a_u, a_gate, rg_conv_w[i], rg_conv_b[i], rg_w_r[i], rg_b_r[i],
                          rg_w_i[i], rg_b_i[i], rg_lambda[i], g_a)
        y_b = hgrn2_group(b_q, b_f, b_v, b_g, lower_bound[i], g_b)
        y_c = shortconv_group(c_b, c_c, c_v, sc_conv_w[i], g_c)
        y = jnp.concatenate([y_a, y_b, y_c], axis=-1).astype(dt)
        x = x + y @ w_out[i]
        x = x + conv_ffn(rmsnorm(x, norm_ffn_gain[i]), ffn_w_up[i], ffn_conv_w[i], ffn_w_down[i])
        gate = jax.nn.sigmoid((x @ ple_w_gate[i]).astype(jnp.float32))
        x = x + (gate * (p[i] @ ple_w_proj[i]).astype(jnp.float32)).astype(dt)
    return rmsnorm(x, final_norm_gain)


def setup_inputs(seed=0):
    out = dict(first_inputs(seed))
    for name, value in second_inputs(seed + 1).items():
        if name != "x":
            out[name + "_2"] = value
    return out


def reference(
    x, norm_gain, w_in, b_forget, lambda_q1, lambda_k1, lambda_q2, lambda_k2, subln_gain, sinks,
    w_up_a, w_up_b, w_up_c, w_o, final_gain, p_2, norm_mix_gain_2, w_in_2, rg_conv_w_2,
    rg_conv_b_2, rg_w_r_2, rg_b_r_2, rg_w_i_2, rg_b_i_2, rg_lambda_2, hg_lower_bounds_2,
    sc_conv_w_2, mix_out_gain_2, w_out_2, norm_ffn_gain_2, ffn_w_up_2, ffn_conv_w_2,
    ffn_w_down_2, ple_w_proj_2, ple_w_gate_2, final_norm_gain_2,
):
    x = first_block(
        x, norm_gain, w_in, b_forget, lambda_q1, lambda_k1, lambda_q2, lambda_k2, subln_gain,
        sinks, w_up_a, w_up_b, w_up_c, w_o, final_gain,
    )
    return second_block(
        x, p_2, norm_mix_gain_2, w_in_2, rg_conv_w_2, rg_conv_b_2, rg_w_r_2, rg_b_r_2, rg_w_i_2,
        rg_b_i_2, rg_lambda_2, hg_lower_bounds_2, sc_conv_w_2, mix_out_gain_2, w_out_2,
        norm_ffn_gain_2, ffn_w_up_2, ffn_conv_w_2, ffn_w_down_2, ple_w_proj_2, ple_w_gate_2,
        final_norm_gain_2,
    )


_drawn_inputs = setup_inputs


def setup_inputs(seed=0):
    import zlib

    import numpy as np

    out = dict(_drawn_inputs(seed))
    spreads = {}
    factors = {'b_forget': 4.293,
     'lambda_k1': 5.141,
     'lambda_q2': 5.392,
     'subln_gain': 3.149,
     'sinks': 5.693,
     'rg_b_r_2': 23.66,
     'rg_b_i_2': 8.0,
     'mix_out_gain_2': 4.162,
     'norm_ffn_gain_2': 4.993,
     'final_norm_gain_2': 8.078}
    for name, (base, spread) in spreads.items():
        noise = np.random.default_rng([zlib.crc32(name.encode()), seed]).standard_normal(out[name].shape)
        drawn = base * np.exp(spread * noise) if base else spread * noise
        out[name] = __import__('jax').numpy.asarray(drawn.astype(out[name].dtype))
    for name, factor in factors.items():
        out[name] = (out[name] * factor).astype(out[name].dtype)
    return out
```

```python
import math
from contextlib import ExitStack

import numpy as np

import concourse.bass as bass
from concourse import mybir

F32 = mybir.dt.float32
F32R = mybir.dt.float32r
U8 = mybir.dt.uint8
ALU = mybir.AluOpType
ACT = mybir.ActivationFunctionType
AXX = mybir.AxisListType.X

P = 128
T = 512
KD = 8
BLK = 8
NEG = -1.0e30
LOWEST = -3.0e38
LEVELS = [1, 2, 4, 8, 16, 32, 64]
NPAIR = 22

QA, KA, VA, GA, QB, KB, VB, GB, QC, KC, VC, FC, GC, GM = (
    0, 512, 1024, 1536, 2048, 2560, 2688, 2816, 3328, 3840, 4352, 4864, 4872, 5384)
AU, AG, BQ, BF, BV, BG, CB, CC, CV = 0, 384, 768, 1152, 1536, 1920, 2304, 2560, 2816

VEC = {}


def _vec_table():
    at = 0
    for name, n in [("norm_gain", 8), ("final_gain", 8), ("mix_norm", 8), ("subln", 1), ("sinks", 8),
                    ("b_forget", 1), ("lam_vec", 256), ("rg_cw", 12), ("rg_cb", 3), ("rg_br", 3), ("rg_bi", 3),
                    ("rg_lam", 3), ("hg_lb", 3), ("sc_cw", 6), ("mix_gain", 8), ("ffn_norm", 8), ("ffn_cw", 132),
                    ("final2", 8)]:
        VEC[name] = (at, n)
        at += n
    return at


NVEC = _vec_table()


def plan_units():
    units = []

    def fm(name, col, width=P, nk=KD):
        units.append([(name, k, col, width) for k in range(nk)])

    def tm(name, col, nb, per):
        for k in range(0, KD, per):
            units.append([(name, kk, col + P * e, P) for kk in range(k, k + per) for e in range(nb)])

    fm("win", FC, 8)
    for c in (KC, QC):
        for t in range(4):
            fm("win", c + P * t)
    tm("win", VC, 4, 2)
    for c in (KA, QA):
        for t in range(4):
            fm("win", c + P * t)
    tm("win", VA, 4, 2)
    fm("win", KB)
    fm("win", VB)
    for t in range(4):
        fm("win", QB + P * t)
    for t in range(4):
        fm("win", GC + P * t)
    for d in range(3):
        for j in range(3):
            fm("win", GM + 1024 * j + P * d)
    for c in (GA, GB):
        for t in range(4):
            fm("win", c + P * t)
    for d in range(8):
        if d >= 3:
            for j in range(3):
                fm("win", GM + 1024 * j + P * d)
        units.append([(n, k, P * d, P) for n in ("up_c", "up_a") for k in range(4)])
        units.append([("up_b", k, P * d, P) for k in range(4)])
    for d in range(8):
        fm("wo", P * d)
    for c in (AU, BF, BQ):
        for t in range(3):
            fm("win2", c + P * t)
    tm("win2", BV, 3, 2)
    for c, n in ((AG, 3), (BG, 3), (CC, 2), (CV, 2), (CB, 2)):
        for t in range(n):
            fm("win2", c + P * t)
    for d in range(8):
        fm("wout", P * d)
    for j in range(NPAIR):
        fm("ffn_up", P * j)
        fm("ffn_up", 2816 + P * j)
    for d in range(8):
        for k in range(0, NPAIR, 8):
            units.append([("ffn_dn", kk, P * d, P) for kk in range(k, min(k + 8, NPAIR))])
    units.append([("ple_p", k, P * d, P) for d in range(4) for k in range(2)])
    units.append([("ple_p", k, P * d, P) for d in range(4, 8) for k in range(2)])
    for d in range(8):
        fm("ple_g", P * d)
    return units


class Queue:

    def __init__(self, sem):
        self.sem, self.n, self.items, self.seen = sem, 0, [], {}

    def wait(self, toks):
        for tok in toks:
            if isinstance(tok, list):
                self.wait(tok)
            elif tok is not None and self.seen.get(tok[0].name, 0) < tok[1]:
                self.seen[tok[0].name] = tok[1]
                self.items.append(tok)

    def __call__(self, fn, toks=(), inc=True):
        self.wait(toks)
        self.n += inc
        self.items.append((fn, inc))
        return (self.sem, self.n)

    @property
    def last(self):
        return (self.sem, self.n)

    def replay(self, eng):
        for a, b in self.items:
            if callable(a):
                ins = a(eng)
                if b is True:
                    ins.then_inc(self.sem, 1)
                elif b:
                    ins.then_inc(b, 16)
            else:
                eng.wait_ge(a, b)


class Buf:

    def __init__(self, ap):
        self.ap, self.free = ap, []


class Ring:
    def __init__(self, aps):
        self.bufs, self.i = [Buf(a[:, :]) for a in aps], 0

    def next(self):
        b = self.bufs[self.i % len(self.bufs)]
        self.i += 1
        return b


def build(nc, wall, xT, pT, vec, cst, cu8, rgw, out):
    units = plan_units()
    with ExitStack() as ctx:
        base = 16512
        place = {}

        def at(name, shape, dt, off):
            return nc.alloc_sbuf_tensor_at(name, shape, dt, offset=off)

        class Area:
            def __init__(self, start):
                self.p = start

            def __call__(self, name, cols, dt=F32, size=4):
                t = at(name, [P, cols], dt, self.p)
                place[name] = self.p
                self.p += (cols * size + 63) // 64 * 64
                assert self.p <= 229368, (name, self.p)
                return t

        NR = NS = 3
        LOOK = 2
        ar = Area(base)
        raw = [ar(f"raw{i}", BLK * P) for i in range(NR)]
        whi = [ar(f"whi{i}", BLK * P, F32R) for i in range(NS)]
        wlo = [ar(f"wlo{i}", BLK * P, F32R) for i in range(NS)]
        CST = ar("cst", 128 * 4 + 512 + 256 + 512)
        CU8 = ar("cu8", 7 * 256 + 512, U8, 1)
        VECS = ar("vecs", NVEC)
        SM = ar("sm", 96)
        HH = ar("HH", KD * T, F32R)
        HL = ar("HL", KD * T, F32R)
        arena = ar.p
        ident = CST[:, 0:128]
        ones = CST[:, 128:256]
        bdones = CST[:, 256:384]
        maskC = CST[:, 384:512]
        DA = CST[:, 512:1024]
        DB = CST[:, 1024:1280]
        m64 = CST[:, 1280:1792]

        def lvmask(l):
            return CU8[:, 256 * l:256 * l + 256]

        dgmask = CU8[:, 7 * 256:7 * 256 + 512]

        def v(name, i=0, n=1):
            o = VEC[name][0] + i
            return VECS[:, o:o + n]

        pb = [ctx.enter_context(nc.psum_tensor(f"pb{i}", [P, T], F32)) for i in range(8)]

        def sem(name):
            return ctx.enter_context(nc.semaphore(name))

        PE, AC, DV, PO, SP = (Queue(sem(n)) for n in ("s_pe", "s_ac", "s_dv", "s_po", "s_sp"))

        def act(o, i, f=ACT.Copy, w=(), bias=None, scale=1.0, accum=None):
            kw = {}
            if bias is not None:
                kw["bias"] = bias
            if accum is not None:
                kw["accum_out"] = accum
            return AC(lambda e: e.activation(o, i, f, scale=scale, **kw), w)

        def tt(o, a, b, op, w=(), q=None):
            return (q or DV)(lambda e: e.tensor_tensor(o, a, b, op), w)

        def ts(o, a, s1, s2=None, op0=ALU.mult, op1=None, w=(), q=None):
            if op1 is None:
                return (q or DV)(lambda e: e.tensor_scalar(o, a, s1, None, op0), w)
            return (q or DV)(lambda e: e.tensor_scalar(o, a, s1, s2, op0, op1), w)

        def stt(o, a, s, b, op0, op1, w=()):
            return DV(lambda e: e.scalar_tensor_tensor(out=o, in0=a, scalar=s, in1=b, op0=op0, op1=op1), w)

        def addmax(o, a, b, mx, w=()):
            return DV(lambda e: e.tensor_tensor_reduce(o, a, b, 1.0, LOWEST, ALU.add, ALU.max, mx), w)

        def recip(o, a, w=()):
            return DV(lambda e: e.reciprocal(o, a), w)

        def vcopy(o, a, w=(), q=None):
            return (q or DV)(lambda e: e.tensor_copy(o, a), w)

        def scan(o, d0, d1, w=()):
            return DV(lambda e: e.tensor_tensor_scan(o, d0, d1, 0.0, ALU.mult, ALU.add), w)

        def mm(o, l, r, start=True, stop=True, w=(), inc=False, skip=False):
            return PE(lambda e: e.matmul(o, l, r, start=start, stop=stop, skip_group_check=skip), w, inc)

        def tp(o, i, w=(), inc=False):
            return PE(lambda e: e.transpose(o, i, ident), w, inc)

        dma_n = {}

        def dma(q, o, i, s, w=()):
            q.wait(w)
            q.items.append((lambda e: e.dma_start(o, i), s))
            dma_n[s.name] = dma_n.get(s.name, 0) + 16
            return (s, dma_n[s.name])

        def split(src, hi, lo, w, q=None):
            a = act(hi, src, w=w)
            b = tt(lo, src, hi.bitcast(F32), ALU.subtract, [a, *w], q or PO)
            return [a, b]

        s_raw = [sem(f"s_raw{i}") for i in range(NR)]
        offs = np.concatenate([[0], np.cumsum([sum(b[3] for b in u) for u in units])])

        class Stream:
            def __init__(self):
                self.loaded, self.done, self.parts = {}, {}, {}
                self.u, self.b, self.next_split = -1, 0, 0

            def load(self, u):
                if u < len(units):
                    n = int(offs[u + 1] - offs[u])
                    self.loaded[u] = dma(SP, raw[u % NR][:, 0:n], wall[:, int(offs[u]):int(offs[u + 1])],
                                         s_raw[u % NR], [self.parts.get(u - NR)])

            def prepare(self, upto):
                while self.next_split <= min(upto, len(units) - 1):
                    u = self.next_split
                    n = int(offs[u + 1] - offs[u])
                    self.parts[u] = split(raw[u % NR][:, 0:n], whi[u % NS][:, 0:n], wlo[u % NS][:, 0:n],
                                          [self.loaded[u], self.done.get(u - NS)])
                    self.load(u + NR)
                    self.next_split += 1

            def take(self, want, n=1):
                if self.u < 0 or self.b == len(units[self.u]):
                    self.u, self.b = self.u + 1, 0
                    self.prepare(self.u + LOOK)
                u = units[self.u]
                assert u[self.b][:3] == want, (u[self.b], want)
                width = u[self.b][3]
                o = width * self.b
                self.b += n
                hi, lo = whi[self.u % NS], wlo[self.u % NS]
                return hi[:, o:o + width * n], lo[:, o:o + width * n], self.parts[self.u], self.b == len(u)

        ws = Stream()

        def proj(o, name, col, xh, xl, xtok, free, nk=KD, width=P, k0=0, ktot=None):
            ktot = ktot or nk
            for k in range(nk):
                hi, lo, parts, end = ws.take((name, k, col))
                hi, lo = hi[:, 0:width], lo[:, 0:width]
                mm(o, hi, xh[k], start=k0 + k == 0, stop=False, w=[free, parts[0], xtok[k]])
                mm(o, hi, xl[k], start=False, stop=False)
                t = mm(o, lo, xh[k], start=False, stop=k0 + k == ktot - 1, w=[parts[1]], inc=end or k == nk - 1)
                if end:
                    ws.done[ws.u] = t
            return t

        def proj_tokens(os, name, col, nb, xh, xl, xtok, between=None):
            toks = [None] * 4
            for k in range(KD):
                hi, lo, parts, end = ws.take((name, k, col), nb)
                for m in range(4):
                    xs = slice(P * m, P * m + P)
                    o = os[m].ap[:, 0:nb * P]
                    mm(o, xh[k][:, xs], hi, start=k == 0, stop=False, w=[os[m].free, parts, xtok[k]])
                    mm(o, xh[k][:, xs], lo, start=False, stop=False)
                    toks[m] = mm(o, xl[k][:, xs], hi, start=False, stop=k == KD - 1, inc=True)
                if end:
                    ws.done[ws.u] = toks[3]
                if between and k % 2:
                    between()
            return toks

        s_c = [sem(f"s_c{i}") for i in range(4)]
        s_x = [sem(f"s_x{i}") for i in range(4)]
        X = at("X", [P, KD * T], F32, arena)

        def xk(k):
            return X[:, T * k:T * k + T]

        xtok0 = []
        for i in range(4):
            tok = dma(AC, X[:, 2 * T * i:2 * T * i + 2 * T].rearrange("p (k t) -> p k t", k=2),
                      xT[2 * P * i:2 * P * i + 2 * P, :].rearrange("(k p) t -> p k t", p=P), s_x[i])
            xtok0 += [tok, tok]
        for u in range(NR):
            ws.load(u)
        tvec = dma(AC, VECS[:, :], vec, s_c[0])
        tcst = dma(AC, CST[:, :], cst, s_c[1])
        eps6 = SM[:, 0:1]
        eps5 = SM[:, 1:2]
        one = SM[:, 2:3]
        teps = [DV(lambda e: e.memset(eps6, 1e-6)), DV(lambda e: e.memset(eps5, 1e-5)),
                DV(lambda e: e.memset(one, 1.0))]

        hh = [HH[:, T * k:T * k + T] for k in range(KD)]
        hl = [HL[:, T * k:T * k + T] for k in range(KD)]

        main = Ring([b[:, :] for b in pb[0:4]])
        S = Ring([b[:, :] for b in pb[4:6]])
        TB = Ring([pb[6][:, :]])
        YB = Ring([pb[7][:, :]])

        a1 = Area(arena)
        qA = [a1(f"qA{t}", T) for t in range(4)]
        kA = [a1(f"kA{t}", T) for t in range(4)]
        vA = [a1(f"vA{m}", T) for m in range(4)]
        qC = [a1(f"qC{t}", T) for t in range(4)]
        kC = [a1(f"kC{t}", T) for t in range(4)]
        vC = [a1(f"vC{m}", T) for m in range(4)]
        qB = [a1(f"qB{t}", T) for t in range(4)]
        kB = a1("kB", T)
        vB = a1("vB", T)
        exB = [a1(f"exB{t}", T, F32R) for t in range(4)]
        GMs = [a1(f"gms{i}", T) for i in range(9)]
        work0 = a1.p
        Pr = Ring([a1(f"P{i}", T) for i in range(6)])
        PTr = Ring([a1(f"PT{i}", T) for i in range(3)])
        Br = Ring([a1(f"B{i}", T) for i in range(2)])
        Nr = Ring([a1(f"N{i}", T) for i in range(2)])
        Wr = Ring([a1(f"W{i}", T) for i in range(3)])
        STt = a1("stat", 8 * 16)
        Sr = Ring([STt[:, 16 * i:16 * i + 16] for i in range(8)])
        cT = at("cT", [P, T], F32, Wr.bufs and place["W2"])
        CQ = a1("CQ", 32)
        THr = Ring([a1(f"th{i}", T) for i in range(3)])

        MF = at("maskf", [P, 7 * 256 + 512], F32, place["gms4"])
        tcu8 = dma(AC, MF[:, :], cu8, s_c[2])
        tcu8 = vcopy(CU8[:, :], MF[:, :], [tcu8], PO)

        w = Wr.next()
        sqb = [Buf(qC[0][:, :]), Buf(qC[1][:, :])]
        acc = qC[2][:, :]
        tacc = None
        for k in range(KD):
            b = sqb[k % 2] if k else Buf(acc)
            t = act(b.ap, xk(k), ACT.Square, [xtok0[k], b.free])
            if k:
                tacc = tt(acc, acc, b.ap, ALU.add, [t, tacc or tsq0])
                b.free = [tacc]
            else:
                tsq0 = t
        bank = TB.next()
        t = mm(bank.ap, ones, acc, w=[tacc, tcst], inc=True)
        rst = qC[3][:, :]
        t = act(rst, bank.ap, ACT.Ln, [t, teps], bias=eps6, scale=1.0 / 1024)
        bank.free = [t]
        t = act(rst, rst, ACT.Exp, [t], scale=-0.5)
        htok = []
        tmp = [Buf(kC[0][:, :]), Buf(kC[1][:, :])]
        for k in range(KD):
            b = tmp[k % 2]
            t1 = stt(b.ap, xk(k), v("norm_gain", k), rst, ALU.mult, ALU.mult, [t, tvec, b.free, xtok0[k]])
            sp = split(b.ap, hh[k], hl[k], [t1], DV)
            b.free = sp
            htok.append(sp)
        first_free = [AC.last, DV.last, PE.last]

        background = []

        def step(n=1):
            for _ in range(n):
                while background:
                    try:
                        next(background[0])
                        break
                    except StopIteration:
                        background.pop(0)

        def drain_background():
            while background:
                step()

        def pipeline(us):
            n = len(us)
            us[0].pre()
            for i in range(n + 3):
                if i + 1 < n:
                    us[i + 1].pre()
                if i < n:
                    us[i].scores()
                if 0 <= i - 1 < n:
                    us[i - 1].normal()
                if 0 <= i - 2 < n:
                    us[i - 2].turn()
                if 0 <= i - 3 < n:
                    us[i - 3].values()
                yield

        class Unit:

            def pre(self):
                pass

            def softmax(self, bank, tscore, bias, tbias, width, col, sink=None):
                st, p = self.st, Pr.next()
                t = addmax(p.ap[:, 0:width], bank.ap[:, 0:width], bias, st.ap[:, col:col + 1],
                           [tscore, tbias, p.free, st.free if col == 0 else None])
                bank.free = [t]
                self.addt = t
                nm = st.ap[:, col + 1:col + 2]
                if sink is None:
                    t = ts(nm, st.ap[:, col:col + 1], -1.0, w=[t])
                else:
                    t = ts(nm, st.ap[:, col:col + 1], sink, -1.0, ALU.max, ALU.mult, [t])
                t2 = act(p.ap[:, 0:width], p.ap[:, 0:width], ACT.Exp, [t], bias=nm,
                         accum=st.ap[:, col + 2:col + 3])
                return p, t2, t

            def turn(self):
                bank, self.pt = TB.next(), PTr.next()
                n = self.width // P
                for j in range(n):
                    t = tp(bank.ap[:, P * j:P * j + P], self.p.ap[:, P * j:P * j + P],
                           [self.tp, bank.free], inc=j == n - 1)
                self.p.free = [t]
                self.tpt = act(self.pt.ap[:, 0:self.width], bank.ap[:, 0:self.width], w=[t, self.pt.free])
                bank.free = [self.tpt]

        def finish_values(unit, o, lhs, tv, last):
            n = unit.width // P
            for j in range(n):
                t = mm(o, lhs(j), unit.pt.ap[:, P * j:P * j + P], start=j == 0, stop=j == n - 1,
                       w=[unit.tpt, tv, last], inc=j == n - 1)
            unit.pt.free = [t]
            return t

        tok = {}

        class UnitC(Unit):
            def __init__(self, h, i):
                self.h, self.i, self.t, self.r = h, i, h // 2, 64 * (h % 2)
                self.width = P * (i + 1)

            def pre(self):
                if self.i == 0:
                    bank, nb = TB.next(), Nr.next()
                    t = mm(bank.ap, ident[0:8, self.h:self.h + 1].to_broadcast([8, P]), cT[0:8, :],
                           w=[tok["c"], bank.free], inc=True)
                    UnitC.neg = nb
                    UnitC.tneg = act(nb.ap, bank.ap, w=[t, nb.free], scale=-1.0)
                    bank.free = [UnitC.tneg]
                self.nb, self.tn = UnitC.neg, UnitC.tneg

            def scores(self):
                i, r = self.i, self.r
                bank = S.next()
                ts_ = mm(bank.ap[:, 0:self.width], qC[self.t][r:r + 64, P * i:P * i + P],
                         kC[self.t][r:r + 64, 0:self.width], w=[tok["qC"], tok["kC"], bank.free], inc=True)
                tok["scoreC", self.t] = ts_
                bb = Br.next()
                cq = CQ[:, 8 * i + self.h:8 * i + self.h + 1]
                tb = [stt(bb.ap[:, P * i:P * i + P], self.nb.ap[:, P * i:P * i + P], cq, maskC, ALU.add, ALU.add,
                          [self.tn, tok["cq"], bb.free])]
                if i:
                    tb.append(ts(bb.ap[:, 0:P * i], self.nb.ap[:, 0:P * i], cq, op0=ALU.add))
                self.nb.free = tb
                self.st = Sr.next()
                self.p, self.te, _ = self.softmax(bank, ts_, bb.ap[:, 0:self.width], tb, self.width, 0)
                bb.free = [self.addt]

            def normal(self):
                st = self.st.ap
                t = recip(st[:, 3:4], st[:, 2:3], [self.te])
                self.tp = ts(self.p.ap[:, 0:self.width], self.p.ap[:, 0:self.width], st[:, 3:4], w=[t])
                self.st.free = [self.tp]

            def values(self):
                if self.i == 0 and self.r == 0:
                    UnitC.y = YB.next()
                y, r, i = UnitC.y, self.r, self.i
                t = finish_values(self, y.ap[r:r + 64, P * i:P * i + P],
                                  lambda j: vC[j][:, 64 * self.h:64 * self.h + 64], tok["vC"], y.free)
                if self.r and i == 3:
                    tok["yC", self.t] = vcopy(qC[self.t][:, :], y.ap, [t, tok["scoreC", self.t]])
                    y.free = [tok["yC", self.t]]

        class UnitA(Unit):
            def __init__(self, h, i):
                self.h, self.i = h, i
                self.width = P * (i + 1)

            def pre(self):
                if self.i == 0:
                    UnitA.nb = Br.next()
                    UnitA.tn = ts(UnitA.nb.ap, DA, 2.0 ** (-2 * (self.h + 1)), w=[UnitA.nb.free])
                self.nb, self.tn = UnitA.nb, UnitA.tn

            def scores(self):
                i = self.i
                self.st = Sr.next()
                self.ps, self.tes = [], []
                for m in range(2):
                    r = 64 * m
                    bank = S.next()
                    t = mm(bank.ap[:, 0:self.width], qA[self.h][r:r + 64, P * i:P * i + P],
                           kA[self.h][r:r + 64, 0:self.width], w=[tok["qA"], tok["kA"], bank.free], inc=True)
                    tok["scoreA", self.h] = t
                    p, te, _ = self.softmax(bank, t, self.nb.ap[:, 384 - P * i:512], self.tn, self.width, 4 * m)
                    self.ps.append(p)
                    self.tes.append(te)
                self.nb.free = [self.addt]

            def normal(self):
                st, wd = self.st.ap, self.width
                p0, p1 = self.ps
                a = recip(st[:, 3:4], st[:, 2:3], [self.tes[0]])
                b = recip(st[:, 7:8], st[:, 6:7], [self.tes[1]])
                b = ts(p1.ap[:, 0:wd], p1.ap[:, 0:wd], st[:, 7:8], lam, ALU.mult, ALU.mult, [b, tok["lam"]])
                self.tp = stt(p0.ap[:, 0:wd], p0.ap[:, 0:wd], st[:, 3:4], p1.ap[:, 0:wd], ALU.mult, ALU.subtract,
                              [a, b])
                self.p = p0
                p1.free = [self.tp]
                self.st.free = [self.tp]

            def values(self):
                h, i = self.h, self.i
                if i == 0:
                    UnitA.y = YB.next()
                y = UnitA.y
                t = finish_values(self, y.ap[:, P * i:P * i + P], lambda j: vA[j][:, P * h:P * h + P],
                                  tok["vA"], y.free)
                if i == 3:
                    dst = qA[h][:, :]
                    t = vcopy(dst, y.ap, [t, tok["scoreA", h]])
                    y.free = [t]
                    sq = Wr.next()
                    ts_ = act(sq.ap, dst, ACT.Square, [t, sq.free])
                    bank = TB.next()
                    tm_ = mm(bank.ap, ones, sq.ap, w=[ts_, bank.free], inc=True)
                    t2 = act(sq.ap, bank.ap, ACT.Ln, [tm_], bias=eps5, scale=1.0 / 128)
                    bank.free = [t2]
                    t2 = act(sq.ap, sq.ap, ACT.Exp, [t2], scale=-0.5)
                    tok["yA", h] = stt(dst, dst, subg, sq.ap, ALU.mult, ALU.mult, [t2, tok["subg"]])
                    sq.free = [tok["yA", h]]

        class UnitB(Unit):
            def __init__(self, t, s, i):
                self.t, self.r, self.i, self.h = t, 64 * s, i, t + 4 * s
                self.j0 = max(i - 1, 0)
                self.width = P * (i + 1 - self.j0)

            def pre(self):
                if self.i == 0:
                    UnitB.nb = Br.next()
                    UnitB.tn = ts(UnitB.nb.ap[:, 0:256], DB, 2.0 ** -(self.h + 1), w=[UnitB.nb.free])
                self.nb, self.tn = UnitB.nb, UnitB.tn

            def scores(self):
                i, r = self.i, self.r
                self.st = Sr.next()
                bank = S.next()
                t = mm(bank.ap[:, 0:self.width], qB[self.t][r:r + 64, P * i:P * i + P],
                       kB[r:r + 64, P * self.j0:P * i + P], w=[tok["qB"], tok["kB"], bank.free], inc=True)
                tok["scoreB", self.t] = t
                self.p, self.te, tm_ = self.softmax(bank, t, self.nb.ap[:, 256 - self.width:256], self.tn,
                                                    self.width, 0, v("sinks", self.h))
                self.nb.free = [self.addt]
                st = self.st.ap
                self.te2 = act(st[:, 4:5], v("sinks", self.h), ACT.Exp, [tm_], bias=st[:, 1:2])

            def normal(self):
                st, wd = self.st.ap, self.width
                t = tt(st[:, 5:6], st[:, 2:3], st[:, 4:5], ALU.add, [self.te, self.te2])
                t = recip(st[:, 3:4], st[:, 5:6], [t])
                self.tp = ts(self.p.ap[:, 0:wd], self.p.ap[:, 0:wd], st[:, 3:4], w=[t])
                self.st.free = [self.tp]

            def values(self):
                if self.i == 0 and self.r == 0:
                    UnitB.y = YB.next()
                y, r, i = UnitB.y, self.r, self.i
                t = finish_values(self, y.ap[r:r + 64, P * i:P * i + P],
                                  lambda j: vB[:, P * (self.j0 + j) + r:P * (self.j0 + j) + r + 64], tok["vB"],
                                  y.free)
                if self.r and i == 3:
                    tok["yB", self.t] = vcopy(qB[self.t][:, :], y.ap, [t, tok["scoreB", self.t]])
                    y.free = [tok["yB", self.t]]

        lam, subg = SM[:, 8:9], SM[:, 9:10]
        lam_init = 0.8 - 0.6 * math.exp(-0.3 * 0)
        lv = VEC["lam_vec"][0]
        scr = THr.bufs[0].ap
        tl = []
        for j in range(2):
            tl.append(DV(lambda e, j=j: e.tensor_tensor_reduce(
                scr[:, 64 * j:64 * j + 64], VECS[:, lv + 128 * j:lv + 128 * j + 64],
                VECS[:, lv + 128 * j + 64:lv + 128 * j + 128], 1.0, 0.0, ALU.mult, ALU.add,
                SM[:, 10 + j:11 + j]), [tvec]))
        t = act(SM[:, 12:14], SM[:, 10:12], ACT.Exp, tl)
        t = tt(SM[:, 14:15], SM[:, 12:13], SM[:, 13:14], ALU.subtract, [t])
        tok["lam"] = ts(lam, SM[:, 14:15], lam_init, op0=ALU.add, w=[t])
        tok["subg"] = ts(subg, v("subln"), 1.0 - lam_init, w=[tvec])

        def fm_tile(col, dst, scale=None, on=None, w=()):
            b = main.next()
            t = proj(b.ap, "win", col, hh, hl, htok, b.free)
            if on is DV:
                t = vcopy(dst, b.ap, [t, *w]) if scale is None else ts(dst, b.ap, scale, w=[t, *w])
            else:
                t = act(dst, b.ap, w=[t, *w], scale=scale or 1.0)
            b.free = [t]
            return t

        b = main.next()
        t = proj(b.ap[0:8, :], "win", FC, hh, hl, htok, b.free, width=8)
        fx, fn, fa = (GMs[i][0:8, :] for i in range(3))
        t1 = ts(fx, b.ap[0:8, :], VECS[0:8, VEC["b_forget"][0]:VEC["b_forget"][0] + 1], op0=ALU.add, w=[t, tvec])
        b.free = [t1]
        t2 = ts(fn, fx, 0.0, op0=ALU.min, w=[t1])
        t3 = stt(fa, fn, -2.0, fx, ALU.mult, ALU.add, [t2])
        t4 = act(fa, fa, ACT.Exp, [t3], scale=-1.0)
        t4 = act(fa, fa, ACT.Ln, [t4, teps], bias=one[0:8, :])
        t5 = tt(fn, fn, fa, ALU.subtract, [t4])
        tok["c"] = scan(cT[0:8, :], ones[0:8, 0:1].to_broadcast([8, T]), fn, [t5])
        tk = [fm_tile(KC + P * t, kC[t][:, :], on=DV, w=[first_free]) for t in range(4)]
        bank = TB.next()
        for m in range(4):
            t = mm(bank.ap[:, 8 * m:8 * m + 8], cT[0:8, P * m:P * m + P], ident[0:8, 0:8],
                   w=[tok["c"], bank.free], inc=m == 3)
        tok["cq"] = vcopy(CQ[:, :], bank.ap[:, 0:32], [t])
        bank.free = [tok["cq"]]
        tq = [fm_tile(QC + P * t, qC[t][:, :], 0.125, on=DV, w=[first_free]) for t in range(4)]
        tok["kC"], tok["qC"] = tk[-1], tq[-1]
        bs = [main.next() for _ in range(4)]
        tm4 = proj_tokens(bs, "win", VC, 4, hh, hl, htok)
        for m in range(4):
            tok["vC"] = act(vC[m][:, :], bs[m].ap, w=[tm4[m]])
            bs[m].free = [tok["vC"]]
        background.append(pipeline([UnitC(h, i) for h in range(8) for i in range(4)]))

        def slot():
            step(3)

        xfree = [first_free]
        for t in range(4):
            tok["kA"] = fm_tile(KA + P * t, kA[t][:, :], w=xfree)
            slot()
        for t in range(4):
            tok["qA"] = fm_tile(QA + P * t, qA[t][:, :], 0.125, w=xfree)
            slot()
        bs = [main.next() for _ in range(4)]
        tm4 = proj_tokens(bs, "win", VA, 4, hh, hl, htok, slot)
        for m in range(4):
            tok["vA"] = act(vA[m][:, :], bs[m].ap, w=[tm4[m]])
            bs[m].free = [tok["vA"]]
        background.append(pipeline([UnitA(h, i) for h in range(4) for i in range(4)]))
        tok["kB"] = fm_tile(KB, kB[:, :])
        slot()
        vt = THr.next()
        t = fm_tile(VB, vt.ap, w=[tl])
        slot()
        bank = TB.next()
        for m in range(4):
            t2 = tp(bank.ap[:, P * m:P * m + P], vt.ap[:, P * m:P * m + P], [t, bank.free], inc=m == 3)
        vt.free = [t2]
        tok["vB"] = act(vB[:, :], bank.ap, w=[t2])
        bank.free = [tok["vB"]]
        for t in range(4):
            tok["qB"] = fm_tile(QB + P * t, qB[t][:, :], 0.125)
            slot()
        background.append(pipeline([UnitB(t, s, i) for t in range(4) for s in range(2) for i in range(4)]))

        def gate_tile(col, y, ty, hi, lo):
            b = main.next()
            t = proj(b.ap, "win", col, hh, hl, htok, b.free)
            th = THr.next()
            t1 = act(th.ap, b.ap, ACT.Tanh, [t, th.free], scale=0.5)
            t1 = stt(th.ap, th.ap, 1.0, b.ap, ALU.add, ALU.mult, [t1])
            b.free = [t1]
            t1 = stt(th.ap, th.ap, 0.5, y, ALU.mult, ALU.mult, [t1, ty()])
            sp = split(th.ap, hi, lo, [t1])
            th.free = sp
            return sp

        def alias(name, like):
            return at(name, [P, T], F32R, place[like])

        ygh, ygl = {}, {}
        for t in range(4):
            ygh["c", t], ygl["c", t] = alias(f"ychi{t}", f"kC{t}"), alias(f"yclo{t}", f"qC{t}")
            ygh["a", t], ygl["a", t] = alias(f"yahi{t}", f"kA{t}"), alias(f"yalo{t}", f"qA{t}")
            ygh["b", t], ygl["b", t] = exB[t], alias(f"yblo{t}", f"qB{t}")
        ygt = {}

        def need(key):
            while key not in tok:
                step()
            return tok[key]

        for t in range(4):
            need(("yC", t))
            ygt["c", t] = gate_tile(GC + P * t, qC[t][:, :], lambda t=t: tok["yC", t], ygh["c", t][:, :],
                                    ygl["c", t][:, :])
            slot()
        gmt = {}

        def gm_tile(d, j, buf, free=()):
            b = main.next()
            t = proj(b.ap, "win", GM + 1024 * j + P * d, hh, hl, htok, b.free)
            gmt[d, j] = (act(buf, b.ap, ACT.Tanh, [t, *free], scale=0.5), buf)
            b.free = [gmt[d, j][0]]

        for d in range(3):
            for j in range(3):
                gm_tile(d, j, GMs[3 * d + j][:, :], [tcu8])
                slot()
        for t in range(4):
            need(("yA", t))
            ygt["a", t] = gate_tile(GA + P * t, qA[t][:, :], lambda t=t: tok["yA", t], ygh["a", t][:, :],
                                    ygl["a", t][:, :])
            slot()
        for t in range(4):
            need(("yB", t))
            ygt["b", t] = gate_tile(GB + P * t, qB[t][:, :], lambda t=t: tok["yB", t], ygh["b", t][:, :],
                                    ygl["b", t][:, :])
            slot()
        drain_background()
        att_free = [AC.last, DV.last, PE.last, PO.last]

        MH = at("MH", [P, KD * T], F32R, work0)
        ML = at("ML", [P, KD * T], F32R, work0 + 4 * KD * T)
        mh = [MH[:, T * k:T * k + T] for k in range(KD)]
        ml = [ML[:, T * k:T * k + T] for k in range(KD)]
        assert work0 + 8 * KD * T <= place["stat"]
        mtok = []
        Gr = Ring([g[:, :] for g in GMs])
        for d in range(8):
            if d >= 3:
                for j in range(3):
                    g = Gr.next()
                    gm_tile(d, j, g.ap, [g.free])
                    gmt[d, j] += (g,)
            else:
                for j in range(3):
                    gmt[d, j] += (Gr.next(),)
            prev = None
            for n, j in (("c", 2), ("a", 0), ("b", 1)):
                b = main.next()
                t = proj(b.ap, "up_" + n, P * d, [ygh[n, k][:, :] for k in range(4)],
                         [ygl[n, k][:, :] for k in range(4)], [ygt[n, k] for k in range(4)], b.free, nk=4)
                tg, gb, g = gmt[d, j]
                t = stt(gb, gb, 1.0, b.ap, ALU.add, ALU.mult, [t, tg])
                b.free = [t]
                if prev is not None:
                    t2 = tt(gb, gb, prev[0], ALU.add, [t, prev[1]])
                    prev[2].free = [t2]
                    t = t2
                prev = (gb, t, g)
            gb, t, g = prev
            a = act(mh[d], gb, w=[t, att_free], scale=0.5)
            l = stt(ml[d], gb, 0.5, mh[d].bitcast(F32), ALU.mult, ALU.subtract, [a])
            g.free = [a, l]
            mtok.append([a, l])
        up_free = [PE.last]
        s_x2 = [sem(f"s_xr{i}") for i in range(2)]
        xr = []
        for i in range(2):
            tok_ = dma(SP, X[:, 4 * T * i:4 * T * i + 4 * T].rearrange("p (k t) -> p k t", k=4),
                       xT[4 * P * i:4 * P * i + 4 * P, :].rearrange("(k p) t -> p k t", p=P), s_x2[i], up_free)
            xr += [tok_] * 4

        fg, mg = (lambda k: v("final_gain", k)), (lambda k: v("mix_norm", k))
        gg = SM[:, 16:24]
        tgg = tt(gg, v("final_gain", 0, 8), v("mix_norm", 0, 8), ALU.mult, [tvec])
        gA = [g[:, :] for g in GMs]
        acc1, acc2 = gA[0], gA[1]
        sq = Ring(gA[2:6])
        gm_free = [DV.last, AC.last]
        ty = []
        ta1 = ta2 = None
        for d in range(8):
            b = main.next()
            t = proj(b.ap, "wo", P * d, mh, ml, mtok, b.free)
            t = tt(xk(d), b.ap, xk(d), ALU.add, [t, xr[d]])
            b.free = [t]
            ty.append(t)
            o1, o2 = (Buf(acc1), Buf(acc2)) if d == 0 else (sq.next(), sq.next())
            t1 = act(o1.ap, xk(d), ACT.Square, [t, o1.free, gm_free])
            t2 = act(o2.ap, xk(d), ACT.Square, [t, o2.free, gm_free], scale=fg(d))
            if d:
                ta1 = tt(acc1, acc1, o1.ap, ALU.add, [t1, ta1])
                ta2 = tt(acc2, acc2, o2.ap, ALU.add, [t2, ta2])
                o1.free, o2.free = [ta1], [ta2]
            else:
                ta1, ta2 = t1, t2
        b1_free = [PE.last]
        bk1, bk2 = S.next(), S.next()
        t1 = mm(bk1.ap, ones, acc1, w=[ta1, bk1.free], inc=True)
        t2 = mm(bk2.ap, ones, acc2, w=[ta2, bk2.free], inc=True)
        r1, r2, r3 = gA[6], gA[7], gA[8]
        t = act(r1, bk1.ap, ACT.Ln, [t1], bias=eps6, scale=1.0 / 1024)
        bk1.free = [t]
        tr1 = act(r1, r1, ACT.Exp, [t], scale=-0.5)
        t = tt(r3, r1, r1, ALU.mult, [tr1])
        t = tt(r2, bk2.ap, r3, ALU.mult, [t, t2])
        bk2.free = [t]
        t = act(r2, r2, ACT.Ln, [t], bias=eps6, scale=1.0 / 1024)
        t = act(r2, r2, ACT.Exp, [t], scale=-0.5)
        tr = tt(r3, r1, r2, ALU.mult, [t])
        tmpr = Ring(gA[2:6])
        sqfree = [DV.last, AC.last]
        htok = []
        for k in range(KD):
            b = tmpr.next()
            t = stt(b.ap, xk(k), gg[:, k:k + 1], r3, ALU.mult, ALU.mult, [tr, tgg, b.free, sqfree])
            sp = split(b.ap, hh[k], hl[k], [t], DV)
            b.free = sp
            htok.append(sp)
        txb = []
        for k in range(KD):
            txb.append(stt(xk(k), xk(k), fg(k), r1, ALU.mult, ALU.mult, [tr1, htok[k]]))
        n2_free = [AC.last, DV.last]

        a2 = Area(arena + 4 * KD * T)
        fence = [AC.last, DV.last, PO.last, PE.last]
        U3, A3, B3, G3 = (a2(n, 3 * T) for n in ("U3", "A3", "B3", "G3"))
        q3, k3, g64, g512, E3, kh, qh, hv, gs = (
            a2(n, 3 * T) for n in ("q3", "k3", "g64", "g512", "E3", "kh", "qh", "hv", "gs"))
        ST = [a2(f"ST{p}", 2 * T) for p in range(3)]
        sch = [a2(f"sch{t}", T, F32R) for t in range(2)]
        scl = [a2(f"scl{t}", T, F32R) for t in range(2)]
        ZP = [a2(f"zp{i}", T + 16) for i in range(2)]
        RGW = a2("RGW", 6 * P)
        s_rw = sem("s_rw")
        trw = dma(SP, RGW[:, :], rgw, s_rw, fence)

        def c3(x, t):
            return x[:, T * t:T * t + T]

        main = Ring([b.ap for b in main.bufs[:]])
        for b in main.bufs:
            b.free = fence
        m3 = Ring([pb[i][:, :] for i in (0, 1, 2)])
        x4 = Ring([pb[i][:, :] for i in (3, 4)])
        ob = [Buf(pb[i][:, :]) for i in (5, 6, 7)]
        for b in [*m3.bufs, *x4.bufs, *ob]:
            b.free = fence

        def tile2(col):
            b = m3.next()
            return b, proj(b.ap, "win2", col, hh, hl, htok, b.free)

        tzp = [DV(lambda e, z=z: e.memset(z[:, 0:16], 0.0), fence) for z in ZP]
        zr = Ring(ZP)
        for b in zr.bufs:
            b.free = [tzp]

        tu = []
        for t in range(3):
            b, tk_ = tile2(AU + P * t)
            z = zr.next()
            tz = act(z.ap[:, 16:16 + T], b.ap, w=[tk_, z.free])
            b.free = [tz]
            u = c3(U3, t)
            cw = VEC["rg_cw"][0] + 4 * t
            tt_ = ts(u, z.ap[:, 16:16 + T], VECS[:, cw + 3:cw + 4], v("rg_cb", t), ALU.mult, ALU.add, [tz])
            for j in range(3):
                tt_ = stt(u, z.ap[:, 13 + j:13 + j + T], VECS[:, cw + j:cw + j + 1], u, ALU.mult, ALU.add, [tt_])
            z.free = [tt_]
            tu.append(tt_)

        tsp = {}

        def rg_const():
            sl, nn = SM[:, 24:27], SM[:, 27:30]
            la = v("rg_lam", 0, 3)
            t = ts(nn, la, 0.0, op0=ALU.min, w=[tvec])
            t1 = stt(sl, nn, -2.0, la, ALU.mult, ALU.add, [t])
            t1 = act(sl, sl, ACT.Exp, [t1], scale=-1.0)
            t1 = act(sl, sl, ACT.Ln, [t1], bias=one)
            t1 = tt(sl, sl, nn, ALU.subtract, [t1])
            tsp["sp8"] = ts(SM[:, 30:33], sl, 8.0, w=[t1])
            tsp["hb"] = ts(SM[:, 33:39], v("rg_br", 0, 6), 0.5)
            lb = v("hg_lb", 0, 3)
            t = tt(SM[:, 39:42], lb, lb, ALU.subtract)
            t = act(SM[:, 39:42], SM[:, 39:42], ACT.Exp, [t])
            t = recip(SM[:, 42:45], SM[:, 39:42], [t])
            t = tt(SM[:, 39:42], SM[:, 39:42], SM[:, 42:45], ALU.mult, [t])
            t = tt(SM[:, 45:48], SM[:, 39:42], SM[:, 39:42], ALU.subtract, [t])
            tsp["lb"] = ts(SM[:, 48:51], SM[:, 45:48], -1.0, 1.0, ALU.mult, ALU.add, [t])

        rg_const()
        lbv, olb = SM[:, 45:48], SM[:, 48:51]

        def rg_steps():
            tr_, ti_ = [], []
            for t in range(3):
                for g, dst, lst in ((0, A3, tr_), (1, B3, ti_)):
                    b = x4.next()
                    tm_ = mm(b.ap, RGW[:, P * (2 * t + g):P * (2 * t + g) + P], c3(U3, t),
                             w=[tu[t], trw, b.free], inc=True)
                    ta = act(c3(dst, t), b.ap, ACT.Tanh, [tm_, tsp["hb"]],
                             bias=SM[:, 33 + 3 * g + t:34 + 3 * g + t], scale=0.5)
                    b.free = [ta]
                    lst.append(ts(c3(dst, t), c3(dst, t), 0.5, 0.5, ALU.mult, ALU.add, [ta]))
                yield
            for t in range(3):
                a, bb, u, g = c3(A3, t), c3(B3, t), c3(U3, t), c3(G3, t)
                s8 = SM[:, 30 + t:31 + t]
                t1 = act(g, a, ACT.Tanh, [tr_[t], tsp["sp8"]], scale=s8)
                n8 = SM[:, 51 + t:52 + t]
                t0 = ts(n8, s8, -1.0, w=[tsp["sp8"]])
                t2 = act(a, a, ACT.Exp, [t1, t0], scale=n8)
                t3 = tt(bb, bb, u, ALU.mult, [ti_[t]])
                t4 = ts(u, g, 1.0, op0=ALU.add, w=[t1, t3])
                t4 = recip(u, u, [t4])
                t4 = stt(g, g, 2.0, u, ALU.mult, ALU.mult, [t4])
                tr_[t], ti_[t] = [t2], [t3, t4]
                yield
            t = act(G3[:, :], G3[:, :], ACT.Sqrt, [ti_[0], ti_[1], ti_[2]])
            for i in range(3):
                t1 = tt(c3(B3, i), c3(B3, i), c3(G3, i), ALU.mult, [t])
                tok["rg", i] = scan(c3(U3, i), c3(A3, i), c3(B3, i), [t1, tr_[i]])
                yield

        background.append(rg_steps())

        tg = []
        for t in range(3):
            b, tk_ = tile2(BF + P * t)
            e = c3(E3, t)
            t1 = act(e, b.ap, ACT.Exp, [tk_, fence], scale=-1.0)
            b.free = [t1]
            t1 = ts(e, e, 1.0, op0=ALU.add, w=[t1])
            t1 = recip(e, e, [t1])
            t1 = ts(e, e, olb[:, t:t + 1], lbv[:, t:t + 1], ALU.mult, ALU.add, [t1, tsp["lb"]])
            t2 = ts(c3(k3, t), e, -1.0, 1.0, ALU.mult, ALU.add, [t1])
            t1 = ts(e, e, 2.0 ** -63, op0=ALU.max, w=[t1, t2])
            tg.append(t1)
            step()
        tlf = act(E3[:, :], E3[:, :], ACT.Ln, tg)
        tG = []
        for t in range(3):
            tG.append(scan(c3(g64, t), m64, c3(E3, t), [tlf]))
            tG.append(scan(c3(g512, t), ones[:, 0:1].to_broadcast([P, T]), c3(E3, t), [tlf]))
        tq = []
        qt = Ring([c3(gs, 0), c3(gs, 1)])
        for t in range(3):
            b, tk_ = tile2(BQ + P * t)
            x_ = qt.next()
            t1 = act(x_.ap, b.ap, ACT.Tanh, [tk_, fence, x_.free], scale=0.5)
            t1 = stt(x_.ap, x_.ap, 1.0, b.ap, ALU.add, ALU.mult, [t1])
            b.free = [t1]
            tq.append(ts(c3(q3, t), x_.ap, 0.5 * 0.125, w=[t1]))
            x_.free = [tq[-1]]
            step()
        bs = [*m3.bufs, x4.next()]
        tm4 = proj_tokens(bs, "win2", BV, 3, hh, hl, htok)
        thv = []
        for m in range(4):
            t = act(hv[:, 384 * m:384 * m + 384], bs[m].ap[:, 0:384], w=[tm4[m]])
            bs[m].free = [t]
            thv.append(t)
        tst = [PO(lambda e, s=s: e.memset(s[:, :], 0.0), fence) for s in ST]

        def blocks(x, h):
            return x[:, :].rearrange("p (b two r) -> p b two r", two=2, r=h)

        def hgrn_steps():
            first = [True, True, True]
            merged = [[t] for t in tst]
            kfree, qfree = [], []

            def factors(h, src, tsrc):
                nonlocal kfree, qfree
                g = blocks(src, h)
                d = blocks(E3, h)
                nb = 3 * T // (2 * h)
                mid = g[:, :, 0, h - 1:h].to_broadcast([P, nb, h])
                w = [tsrc, kfree, qfree, tlf, tG]
                t = [tt(d[:, :, 0, :], mid, g[:, :, 0, :], ALU.subtract, w),
                     tt(d[:, :, 1, :], g[:, :, 1, :], mid, ALU.subtract, w)]
                t = act(E3[:, :], E3[:, :], ACT.Exp, t)
                tk_ = tt(kh[:, :], k3[:, :], E3[:, :], ALU.mult, [t, kfree, fence])
                tq_ = tt(blocks(qh, h)[:, :, 1, :], blocks(q3, h)[:, :, 1, :], d[:, :, 1, :], ALU.mult,
                         [t, qfree, tq, fence])
                return tk_, tq_

            for h, src in ((256, g512), (128, g512)):
                tk_, tq_ = factors(h, src, tG)
                yield
                last = []
                for hd in range(6):
                    p, r = hd // 2, 64 * (hd % 2)
                    x0 = T * p
                    pairs = [(0, 2, 2), (1, 2, 2)] if h == 256 else [(0, 1, 1), (2, 3, 1)]
                    bank = x4.next()
                    off = 0
                    for s, t0, n in pairs:
                        t = mm(bank.ap[:, off:off + P * n], kh[r:r + 64, x0 + P * s:x0 + P * s + P],
                               qh[r:r + 64, x0 + P * t0:x0 + P * (t0 + n)], w=[tk_, tq_, bank.free],
                               inc=True)
                        off += P * n
                    last.append(t)
                    yield
                    sc = offr.next()
                    tc = act(sc.ap[:, 0:off], bank.ap[:, 0:off], w=[t, sc.free])
                    bank.free = [tc]
                    off = 0
                    for s, t0, n in pairs:
                        o = ob[p].ap[r:r + 64, P * t0:P * (t0 + n)]
                        t = mm(o, hv[:, 384 * s + 64 * hd:384 * s + 64 * hd + 64], sc.ap[:, off:off + P * n],
                               start=first_o[hd], stop=False, w=[tc, thv, ob[p].free], inc=True, skip=True)
                        first_o[hd] = False
                        off += P * n
                    sc.free = [t]
                kfree, qfree = [last], [last]
            for l, h in reversed(list(enumerate(LEVELS))):
                tk_, tq_ = factors(h, g64 if h < 64 else g512, tG)
                yield
                last = []
                for hd in range(6):
                    p, r = hd // 2, 64 * (hd % 2)
                    bank = x4.next()
                    for m in range(4):
                        x0 = T * p + P * m
                        up = qh[r:r + 64, x0:x0 + P].rearrange("p (b two r) -> p b two r", two=2, r=h)[:, :, 1, :]
                        t = mm(bank.ap[:, 64 * m:64 * m + 64], kh[r:r + 64, x0:x0 + P], up,
                               w=[tk_, tq_, bank.free], inc=m == 3)
                    last.append(t)
                    dst = ST[p][:, T * (hd % 2):T * (hd % 2) + T].rearrange(
                        "p (b two r) -> p b two r", two=2, r=h)[:, :, 1, :]
                    msk = lvmask(l).rearrange("p (b r) -> p b r", r=h)
                    src = bank.ap[:, 0:256].rearrange("p (b r) -> p b r", r=h)
                    t = DV(lambda e, dst=dst, msk=msk, src=src: e.copy_predicated(dst, msk, src),
                           [t, merged[p], tcu8])
                    merged[p] = [t]
                    bank.free = [t]
                    if hd % 2:
                        yield
                kfree, qfree = [last], [last]
            for hd in range(6):
                p, r = hd // 2, 64 * (hd % 2)
                bank = x4.next()
                for m in range(4):
                    x0 = T * p + P * m
                    t = mm(bank.ap[:, P * m:P * m + P], k3[r:r + 64, x0:x0 + P], q3[r:r + 64, x0:x0 + P],
                           w=[tq, tg, bank.free], inc=m == 3)
                dst = ST[p][:, T * (hd % 2):T * (hd % 2) + T]
                t = DV(lambda e, dst=dst, src=bank.ap: e.copy_predicated(dst, dgmask, src), [t, merged[p], tcu8])
                merged[p] = [t]
                bank.free = [t]
                if hd % 2:
                    yield
            for hd in range(6):
                p, r = hd // 2, 64 * (hd % 2)
                for m in range(4):
                    t = mm(ob[p].ap[r:r + 64, P * m:P * m + P],
                           hv[:, 384 * m + 64 * hd:384 * m + 64 * hd + 64],
                           ST[p][:, T * (hd % 2) + P * m:T * (hd % 2) + P * m + P], start=False, stop=m == 3,
                           w=[merged[p]], inc=m == 3, skip=True)
                tok["ho", p] = t
                if hd % 2:
                    yield

        first_o = [True] * 6
        offr = Ring([a2(f"off{i}", T) for i in range(2)])
        for b in offr.bufs:
            b.free = fence
        background.append(hgrn_steps())

        YMH, YML = {}, {}
        ytok = {}

        def headnorm(src, dst, gain, tsrc, scale_bank, extra=None, textra=(), dsplit=None, sq=None, w=()):
            tq_ = act(sq.ap, src, ACT.Square, [tsrc, sq.free])
            bank = scale_bank
            tm_ = mm(bank.ap, bdones, sq.ap, w=[tq_, bank.free], inc=True)
            t1 = act(sq.ap, bank.ap, ACT.Ln, [tm_], bias=eps6, scale=1.0 / 64)
            bank.free = [t1]
            t1 = act(sq.ap, sq.ap, ACT.Exp, [t1], scale=-0.5)
            t1 = stt(dst, src, gain, sq.ap, ALU.mult, ALU.mult, [t1, tsrc, *w])
            if extra is not None:
                t1 = tt(dst, dst, extra, ALU.mult, [t1, *textra])
            sq.free = [t1]
            return t1

        a3g = []
        for t in range(3):
            b, tk_ = tile2(AG + P * t)
            need(("rg", t))
            g, a_, u = c3(G3, t), c3(A3, t), c3(U3, t)
            t0 = tok["rg", t]
            t1 = act(a_, b.ap, ACT.Square, [tk_, t0])
            t1 = ts(a_, a_, 0.044715, 1.0, ALU.mult, ALU.add, [t1])
            t1 = tt(a_, a_, b.ap, ALU.mult, [t1])
            t1 = act(a_, a_, ACT.Tanh, [t1], scale=0.7978845608028654)
            t1 = stt(g, a_, 1.0, b.ap, ALU.add, ALU.mult, [t1, t0])
            b.free = [t1]
            t1 = stt(u, u, 0.5, g, ALU.mult, ALU.mult, [t1])
            a3g.append(t1)
            step(4)
        tgs = []
        for t in range(3):
            b, tk_ = tile2(BG + P * t)
            g = c3(gs, t)
            x_ = c3(G3, t)
            t1 = act(x_, b.ap, ACT.Tanh, [tk_, a3g], scale=0.5)
            t1 = stt(x_, x_, 1.0, b.ap, ALU.add, ALU.mult, [t1])
            b.free = [t1]
            tgs.append(ts(g, x_, 0.5, w=[t1, tq]))
            step(4)
        rgh = [at(f"rgh{t}", [P, T], F32R, place["A3"] + 4 * T * t) for t in range(3)]
        rgl = [at(f"rgl{t}", [P, T], F32R, place["B3"] + 4 * T * t) for t in range(3)]
        sqr = Ring([c3(G3, t) for t in range(3)])
        for b in sqr.bufs:
            b.free = [tgs]
        for t in range(3):
            u = c3(U3, t)
            t1 = headnorm(u, u, v("mix_gain", t), a3g[t], x4.next(), sq=sqr.next())
            ytok[t] = split(u, rgh[t][:, :], rgl[t][:, :], [t1, a3g])
        rg_free = [ytok[0], ytok[1], ytok[2]]
        cz, cb_ = [], []
        cc = []
        for t in range(2):
            b, tk_ = tile2(CC + P * t)
            d = c3(G3, t)
            t1 = act(d, b.ap, w=[tk_, rg_free])
            b.free = [t1]
            cc.append(t1)
            step(4)
        for t in range(2):
            b, tk_ = tile2(CV + P * t)
            z = zr.next()
            t1 = tt(z.ap[:, 16:16 + T], b.ap, c3(G3, t), ALU.mult, [tk_, cc[t], z.free])
            b.free = [t1]
            y = c3(U3, t)
            cw = VEC["sc_cw"][0] + 3 * t
            t1 = ts(y, z.ap[:, 16:16 + T], VECS[:, cw + 2:cw + 3], w=[t1, rg_free])
            for j in range(2):
                t1 = stt(y, z.ap[:, 14 + j:14 + j + T], VECS[:, cw + j:cw + j + 1], y, ALU.mult, ALU.add, [t1])
            z.free = [t1]
            cz.append(t1)
            step(4)
        for t in range(2):
            b, tk_ = tile2(CB + P * t)
            y = c3(U3, t)
            t1 = tt(y, b.ap, y, ALU.mult, [tk_, cz[t]])
            b.free = [t1]
            step(4)
            sq_ = Buf(c3(G3, t))
            t1 = headnorm(y, y, v("mix_gain", 6 + t), t1, x4.next(), sq=sq_, w=[])
            ytok[6 + t] = split(y, sch[t][:, :], scl[t][:, :], [t1, fence])
        drain_background()
        hgh = [at(f"hgh{t}", [P, T], F32R, place["kh"] + 4 * T * t) for t in range(3)]
        hgl = [at(f"hgl{t}", [P, T], F32R, place["qh"] + 4 * T * t) for t in range(3)]
        hfree = [PE.last]
        for p in range(3):
            y = c3(E3, p)
            sq_ = Buf(c3(g64, p))
            t1 = headnorm(ob[p].ap, y, v("mix_gain", 3 + p), [tok["ho", p], hfree], x4.next(),
                          extra=c3(gs, p), textra=[tgs], sq=sq_, w=[hfree])
            ytok[3 + p] = split(y, hgh[p][:, :], hgl[p][:, :], [t1, hfree], DV)
        mixh = [*rgh, *hgh, *sch]
        mixl = [*rgl, *hgl, *scl]
        mix_free = [AC.last, DV.last, PO.last]

        main = Ring([pb[i][:, :] for i in range(8)])
        for b in main.bufs:
            b.free = [mix_free, hfree]

        def norm_stats(sqbufs, accb, rst, w0):
            state = {"t": None}

            def add(k, src, t):
                o = Buf(accb) if k == 0 else sqbufs.next()
                t1 = act(o.ap, src, ACT.Square, [t, o.free, *w0])
                if k:
                    t1 = tt(accb, accb, o.ap, ALU.add, [t1, state["t"]])
                    o.free = [t1]
                state["t"] = t1

            def end(bank):
                t = mm(bank.ap, ones, accb, w=[state["t"], bank.free], inc=True)
                t = act(rst, bank.ap, ACT.Ln, [t, *w0], bias=eps6, scale=1.0 / 1024)
                bank.free = [t]
                return act(rst, rst, ACT.Exp, [t], scale=-0.5)

            return add, end

        E = [c3(E3, 0), c3(E3, 1), c3(E3, 2), c3(gs, 0), c3(gs, 1), c3(gs, 2)]
        add, end = norm_stats(Ring(E[2:4]), E[0], E[1], [mix_free])
        tx1 = []
        for d in range(8):
            b = main.next()
            t = proj(b.ap, "wout", P * d, [m[:, :] for m in mixh], [m[:, :] for m in mixl],
                     [ytok[k] for k in range(8)], b.free)
            t = tt(xk(d), b.ap, xk(d), ALU.add, [t, txb[d]])
            b.free = [t]
            tx1.append(t)
            add(d, xk(d), t)
        wout_free = [PE.last]
        trs = end(main.next())
        tmpr = Ring(E[4:6])
        htok = []
        for k in range(KD):
            b = tmpr.next()
            t = stt(b.ap, xk(k), v("ffn_norm", k), E[1], ALU.mult, ALU.mult, [trs, tx1[k], b.free, mix_free])
            sp = split(b.ap, hh[k], hl[k], [t, wout_free], DV)
            b.free = sp
            htok.append(sp)
        fence2 = [AC.last, DV.last, PO.last, PE.last]

        a3 = Area(arena + 4 * KD * T)
        FH = [a3(f"fh{j}", T, F32R) for j in range(NPAIR)]
        FL = [a3(f"fl{j}", T, F32R) for j in range(NPAIR)]
        ffn_work = a3.p
        zf = [a3(f"zf{i}", T + 16) for i in range(4)]
        CVr = Ring([a3(f"cv{i}", T) for i in range(6)])
        for b in CVr.bufs:
            b.free = fence2
        tzf = [DV(lambda e, z=z: e.memset(z[:, 0:16], 0.0), fence2) for z in zf]
        zfr = Ring(zf)
        for b in zfr.bufs:
            b.free = [tzf]
        ftok = []

        def conv_tile(col, cwi):
            b = main.next()
            t = proj(b.ap, "ffn_up", col, hh, hl, htok, b.free)
            z, o = zfr.next(), CVr.next()
            tz = act(z.ap[:, 16:16 + T], b.ap, w=[t, z.free])
            cw = VEC["ffn_cw"][0] + 3 * cwi
            t = ts(o.ap, z.ap[:, 16:16 + T], VECS[:, cw + 2:cw + 3], w=[tz, o.free])
            b.free = [tz]
            for j in range(2):
                t = stt(o.ap, z.ap[:, 14 + j:14 + j + T], VECS[:, cw + j:cw + j + 1], o.ap, ALU.mult, ALU.add,
                        [t, tz])
            z.free = [t]
            return o, t

        for j in range(NPAIR):
            g, tg_ = conv_tile(P * j, j)
            th = CVr.next()
            t1 = act(th.ap, g.ap, ACT.Tanh, [tg_, th.free], scale=0.5)
            t1 = stt(g.ap, th.ap, 1.0, g.ap, ALU.add, ALU.mult, [t1])
            th.free = [t1]
            u, tu_ = conv_tile(2816 + P * j, NPAIR + j)
            t1 = stt(u.ap, u.ap, 0.5, g.ap, ALU.mult, ALU.mult, [tu_, t1])
            g.free = [t1]
            sp = split(u.ap, FH[j][:, :], FL[j][:, :], [t1, fence2])
            u.free = sp
            ftok.append(sp)
        up_done = [AC.last, DV.last, PO.last, PE.last]
        PR = at("PR", [P, 2 * T], F32, ffn_work)
        PH = at("PH", [P, 2 * T], F32R, ffn_work + 8 * T)
        PL = at("PL", [P, 2 * T], F32R, ffn_work + 16 * T)
        s_p = sem("s_p")
        tp_ = dma(SP, PR[:, :].rearrange("p (k t) -> p k t", k=2), pT.rearrange("(k p) t -> p k t", p=P), s_p,
                  up_done)
        psp = split(PR[:, :], PH[:, :], PL[:, :], [tp_, up_done], DV)
        tx2 = []
        gtok = []
        for d in range(8):
            b = main.next()
            for k0 in range(0, NPAIR, 8):
                n = min(8, NPAIR - k0)
                for k in range(k0, k0 + n):
                    hi, lo, parts, e_ = ws.take(("ffn_dn", k, P * d))
                    mm(b.ap, hi, FH[k][:, :], start=k == 0, stop=False, w=[b.free, parts[0], ftok[k]])
                    mm(b.ap, hi, FL[k][:, :], start=False, stop=False)
                    t = mm(b.ap, lo, FH[k][:, :], start=False, stop=k == NPAIR - 1, w=[parts[1]],
                           inc=e_ or k == NPAIR - 1)
                    if e_:
                        ws.done[ws.u] = t
            t = tt(xk(d), b.ap, xk(d), ALU.add, [t, tx1[d]])
            b.free = [t]
            tx2.append(t)
            gtok.append(split(xk(d), hh[d], hl[d], [t, up_done]))
        dn_free = [PE.last]
        a4 = Area(arena + 4 * KD * T)
        PP = [a4(f"pp{d}", T) for d in range(8)]
        t4r = Ring([a4(f"t4{i}", T) for i in range(4)])
        sq4 = Ring([a4(f"sq4{i}", T) for i in range(2)])
        acc4, rs4 = a4("acc4", T)[:, :], a4("rs4", T)[:, :]
        tpp = []
        ph = [c3(PH, k) for k in range(2)]
        pl = [c3(PL, k) for k in range(2)]
        for d in range(8):
            b = main.next()
            t = proj(b.ap, "ple_p", P * d, ph, pl, [psp, psp], b.free, nk=2)
            t = act(PP[d][:, :], b.ap, w=[t, dn_free])
            b.free = [t]
            tpp.append(t)
        add, end = norm_stats(sq4, acc4, rs4, [dn_free])
        tx3 = []
        for d in range(8):
            b = main.next()
            t = proj(b.ap, "ple_g", P * d, hh, hl, gtok, b.free)
            x_ = t4r.next()
            t1 = act(x_.ap, b.ap, ACT.Tanh, [t, x_.free, dn_free], scale=0.5)
            b.free = [t1]
            t1 = stt(x_.ap, x_.ap, 1.0, PP[d][:, :], ALU.add, ALU.mult, [t1, tpp[d]])
            t1 = stt(xk(d), x_.ap, 0.5, xk(d), ALU.mult, ALU.add, [t1, tx2[d], gtok[d]])
            x_.free = [t1]
            tx3.append(t1)
            add(d, xk(d), t1)
        trs = end(main.next())
        s_o = [sem(f"s_o{i}") for i in range(2)]
        ends = {}
        for d in range(8):
            t = stt(xk(d), xk(d), v("final2", d), rs4, ALU.mult, ALU.mult, [trs, tx3[d]])
            ends[d % 2] = dma(SP, out[P * d:P * d + P, :], xk(d), s_o[d % 2], [t])
        SP.wait(list(ends.values()))
        assert ws.u == len(units) - 1 and ws.b == len(units[-1])

        block = ctx.enter_context(nc.Block())

        @block.sync
        def _(eng):
            SP.replay(eng)

        @block.scalar
        def _(eng):
            AC.replay(eng)

        @block.vector
        def _(eng):
            DV.replay(eng)

        @block.gpsimd
        def _(eng):
            PO.replay(eng)

        @block.tensor
        def _(eng):
            PE.replay(eng)


def constants():
    p = np.arange(P)[:, None]
    c = np.arange(T)[None, :]
    ident = np.eye(P, dtype=np.float32)
    ones = np.ones((P, P), np.float32)
    bd = np.kron(np.eye(2), np.ones((64, 64))).astype(np.float32)
    mask = np.where(p >= np.arange(P)[None, :], 0.0, NEG).astype(np.float32)
    da = np.where(p - (c - 384) >= 0, -(p - (c - 384)), NEG).astype(np.float32)
    cb = np.arange(256)[None, :]
    dist = p - cb + P
    db = np.where((dist >= 0) & (dist < P), -dist, NEG).astype(np.float32)
    m64 = np.broadcast_to((np.arange(T) % 64 != 0).astype(np.float32), (P, T))
    cst = np.concatenate([ident, ones, bd, mask, da, db, m64], 1).astype(np.float32)
    s = np.arange(P)[:, None]
    u8 = []
    for h in LEVELS:
        t = np.arange(P).reshape(-1, 2, h)[:, 1, :].ravel()[None, :]
        m = (s // (2 * h) == t // (2 * h)) & (s % (2 * h) < h)
        u8.append(np.tile(m, (1, 4)))
    u8.append(np.tile(np.eye(P, dtype=bool), (1, 4)))
    return np.ascontiguousarray(cst), np.ascontiguousarray(np.concatenate(u8, 1).astype(np.float32))


def kernel(**inputs):
    import numpy as _np
    import concourse.bacc as _bacc
    from concourse import mybir as _mybir
    from concourse.bass_utils import run_bass_kernel_spmd as _run

    g = {k: _np.asarray(a) for k, a in inputs.items()}
    heads = [h for t in range(4) for h in (t, t + 4)]
    perm = _np.concatenate([_np.arange(64 * h, 64 * h + 64) for h in heads])
    win = g["w_in"][0].copy()
    win[:, QB:QB + 512] = g["w_in"][0][:, QB + perm]
    win[:, GB:GB + 512] = g["w_in"][0][:, GB + perm]
    mats = {"win": win, "up_a": g["w_up_a"][0], "up_b": g["w_up_b"][0][perm], "up_c": g["w_up_c"][0],
            "wo": g["w_o"][0], "win2": g["w_in_2"][0], "wout": g["w_out_2"][0], "ffn_up": g["ffn_w_up_2"][0],
            "ffn_dn": g["ffn_w_down_2"][0], "ple_p": g["ple_w_proj_2"][0], "ple_g": g["ple_w_gate_2"][0]}
    wall = _np.concatenate([mats[n][P * k:P * k + P, c:c + w] for u in plan_units() for n, k, c, w in u], 1)

    def cols(a):
        return a.reshape(-1, P).T

    def rep(a):
        return _np.tile(a.reshape(1, -1), (P, 1))

    bf = _np.tile(g["b_forget"][0], P // 8).reshape(P, 1)
    cwr = g["rg_conv_w_2"][0].reshape(4, 3, P).transpose(2, 1, 0).reshape(P, 12)
    cws = g["sc_conv_w_2"][0].reshape(3, 2, P).transpose(2, 1, 0).reshape(P, 6)
    cwf = g["ffn_conv_w_2"][0].reshape(3, 44, P).transpose(2, 1, 0).reshape(P, 132)
    vec = _np.concatenate([
        cols(g["norm_gain"][0]), cols(g["final_gain"]), cols(g["norm_mix_gain_2"][0]), cols(g["subln_gain"][0]),
        rep(g["sinks"][0]), bf, rep(g["lambda_q1"][0]), rep(g["lambda_k1"][0]), rep(g["lambda_q2"][0]),
        rep(g["lambda_k2"][0]), cwr, cols(g["rg_conv_b_2"][0]), cols(g["rg_b_r_2"][0].ravel()),
        cols(g["rg_b_i_2"][0].ravel()), cols(g["rg_lambda_2"][0]), cols(g["hg_lower_bounds_2"][0]), cws,
        cols(g["mix_out_gain_2"][0]), cols(g["norm_ffn_gain_2"][0]), cwf, cols(g["final_norm_gain_2"])], 1)
    rgw = _np.zeros((P, 6 * P), _np.float32)
    for t in range(3):
        for j, n in enumerate(("rg_w_r_2", "rg_w_i_2")):
            for s in range(2):
                o = P * (2 * t + j) + 64 * s
                rgw[64 * s:64 * s + 64, o:o + 64] = g[n][0, 2 * t + s]
    cst, cu8 = constants()
    arrays = {"wall": wall, "xT": g["x"][0].T, "pT": g["p_2"][0, 0].T, "vec": vec, "cst": cst, "cu8": cu8,
              "rgw": rgw}
    nc = _bacc.Bacc("TRN2", target_bir_lowering=False, num_devices=1)
    aps = []
    for n, a in arrays.items():
        arrays[n] = _np.ascontiguousarray(a)
        aps.append(nc.dram_tensor(f"in_{n}", a.shape, _mybir.dt.from_np(a.dtype), kind="ExternalInput").ap())
    out = nc.dram_tensor("outT", (1024, T), _mybir.dt.float32, kind="ExternalOutput").ap()
    build(nc, *aps, out)
    r = _run(nc, [{f"in_{n}": a for n, a in arrays.items()}], core_ids=[0])
    return r.results[0]["outT"].T.reshape(1, T, 1024)
```

```python
import math
from contextlib import ExitStack

import numpy as np

import concourse.bass as bass
from concourse import mybir

F32 = mybir.dt.float32
F32R = mybir.dt.float32r
U8 = mybir.dt.uint8
ALU = mybir.AluOpType
ACT = mybir.ActivationFunctionType
AXX = mybir.AxisListType.X

P = 128
T = 512
KD = 8
BLK = 4
NEG = -1.0e30
LOWEST = -3.0e38
LEVELS = [4, 8, 16, 32, 64]
MASKS = len(LEVELS) * 256 + 512
MIDDLE = 21.84
DEEP = 3
WK = [3, 4, 5, 0, 1, 2, 6, 7]
NW = 6
NPAIR = 22

QA, KA, VA, GA, QB, KB, VB, GB, QC, KC, VC, FC, GC, GM = (
    0, 512, 1024, 1536, 2048, 2560, 2688, 2816, 3328, 3840, 4352, 4864, 4872, 5384)
AU, AG, BQ, BF, BV, BG, CB, CC, CV = 0, 384, 768, 1152, 1536, 1920, 2304, 2560, 2816

VEC = {}


def _vec_table():
    at = 0
    for name, n in [("norm_gain", 8), ("final_gain", 8), ("mix_norm", 8), ("subln", 1), ("sinks", 8),
                    ("b_forget", 1), ("lam_vec", 256), ("rg_cw", 12), ("rg_cb", 3), ("rg_br", 3), ("rg_bi", 3),
                    ("rg_lam", 3), ("hg_lb", 3), ("sc_cw", 6), ("mix_gain", 8), ("ffn_norm", 8), ("ffn_cw", 132),
                    ("final2", 8)]:
        VEC[name] = (at, n)
        at += n
    return at


NVEC = _vec_table()


def plan_units():
    units = []

    def fm(name, col, width=P, nk=KD):
        units.append([(name, k, col, width) for k in range(nk)])

    def tm(name, col, nb):
        for k in range(KD):
            units.append([(name, k, col + P * e, P) for e in range(nb)])

    fm("win", FC, 8)
    for c in (KC, QC):
        for t in range(4):
            fm("win", c + P * t)
    tm("win", VC, 4)
    for c in (KA, QA):
        for t in range(4):
            fm("win", c + P * t)
    tm("win", VA, 4)
    fm("win", KB)
    fm("win", VB)
    for t in range(4):
        fm("win", QB + P * t)
    for t in range(4):
        fm("win", GC + P * t)
    for d in range(3):
        for j in range(3):
            fm("win", GM + 1024 * j + P * d)
    for c in (GA, GB):
        for t in range(4):
            fm("win", c + P * t)
    for d in range(8):
        if d >= 3:
            for j in range(3):
                fm("win", GM + 1024 * j + P * d)
        units.append([(n, k, P * d, P) for n in ("up_c", "up_a") for k in range(4)])
        units.append([("up_b", k, P * d, P) for k in range(4)])
    for d in range(8):
        fm("wo", P * d)
    for c in (BF, BQ):
        for t in range(3):
            fm("win2", c + P * t)
    tm("win2", BV, 3)
    for c, n in ((AU, 3), (CC, 2), (CV, 2), (BG, 3), (AG, 3), (CB, 2)):
        for t in range(n):
            fm("win2", c + P * t)
    for ks in (WK[:NW], WK[NW:]):
        for d in range(3):
            units.append([("wout", k, P * d, P) for k in ks])
    for d in range(3, 8):
        units.append([("wout", k, P * d, P) for k in WK])
    for j in range(NPAIR):
        fm("ffn_up", P * j)
        fm("ffn_up", 2816 + P * j)
    for d in range(8):
        for k in range(0, NPAIR, 8):
            units.append([("ffn_dn", kk, P * d, P) for kk in range(k, min(k + 8, NPAIR))])
    units.append([("ple_p", k, P * d, P) for d in range(4) for k in range(2)])
    units.append([("ple_p", k, P * d, P) for d in range(4, 8) for k in range(2)])
    for d in range(8):
        fm("ple_g", P * d)
    return [u[i:i + BLK] for u in units for i in range(0, len(u), BLK)]


class Queue:

    def __init__(self, sem):
        self.sem, self.n, self.items, self.seen = sem, 0, [], {}

    def wait(self, toks):
        for tok in toks:
            if isinstance(tok, list):
                self.wait(tok)
            elif tok is not None and self.seen.get(tok[0].name, 0) < tok[1]:
                self.seen[tok[0].name] = tok[1]
                self.items.append(tok)

    def __call__(self, fn, toks=(), inc=True):
        self.wait(toks)
        self.n += inc
        self.items.append((fn, inc))
        return (self.sem, self.n)

    @property
    def last(self):
        return (self.sem, self.n)

    def replay(self, eng):
        for a, b in self.items:
            if callable(a):
                ins = a(eng)
                if b is True:
                    ins.then_inc(self.sem, 1)
                elif b:
                    ins.then_inc(b, 16)
            else:
                eng.wait_ge(a, b)


class Buf:

    def __init__(self, ap):
        self.ap, self.free = ap, []


class Ring:
    def __init__(self, aps):
        self.bufs, self.i = [Buf(a[:, :]) for a in aps], 0

    def next(self):
        b = self.bufs[self.i % len(self.bufs)]
        self.i += 1
        return b


def build(nc, wall, xT, pT, vec, cst, cu8, rgw, out):
    units = plan_units()
    with ExitStack() as ctx:
        base = 16512
        place = {}

        def at(name, shape, dt, off):
            return nc.alloc_sbuf_tensor_at(name, shape, dt, offset=off)

        class Area:
            def __init__(self, start):
                self.p = start

            def __call__(self, name, cols, dt=F32, size=4):
                t = at(name, [P, cols], dt, self.p)
                place[name] = self.p
                self.p += (cols * size + 63) // 64 * 64
                assert self.p <= 229368, (name, self.p)
                return t

        NR = NS = 6
        LOOK = 4
        ar = Area(base)
        raw = [ar(f"raw{i}", BLK * P) for i in range(NR)]
        whi = [ar(f"whi{i}", BLK * P, F32R) for i in range(NS)]
        wlo = [ar(f"wlo{i}", BLK * P, F32R) for i in range(NS)]
        CST = ar("cst", 128 * 4 + 512 + 256 + 512)
        CU8 = ar("cu8", MASKS, U8, 1)
        VECS = ar("vecs", NVEC)
        SM = ar("sm", 96)
        HH = ar("HH", KD * T, F32R)
        HL = ar("HL", KD * T, F32R)
        arena = ar.p
        ident = CST[:, 0:128]
        ones = CST[:, 128:256]
        bdones = CST[:, 256:384]
        maskC = CST[:, 384:512]
        DA = CST[:, 512:1024]
        DB = CST[:, 1024:1280]
        m64 = CST[:, 1280:1792]

        def lvmask(l):
            return CU8[:, 256 * l:256 * l + 256]

        b4mask = CU8[:, 256 * len(LEVELS):MASKS]

        def v(name, i=0, n=1):
            o = VEC[name][0] + i
            return VECS[:, o:o + n]

        pb = [ctx.enter_context(nc.psum_tensor(f"pb{i}", [P, T], F32)) for i in range(8)]

        def sem(name):
            return ctx.enter_context(nc.semaphore(name))

        PE, AC, DV, PO, SP = (Queue(sem(n)) for n in ("s_pe", "s_ac", "s_dv", "s_po", "s_sp"))

        def act(o, i, f=ACT.Copy, w=(), bias=None, scale=1.0, accum=None):
            kw = {}
            if bias is not None:
                kw["bias"] = bias
            if accum is not None:
                kw["accum_out"] = accum
            return AC(lambda e: e.activation(o, i, f, scale=scale, **kw), w)

        def tables(name):
            AC(lambda e: e.preload_act_table_set(name), inc=False)

        LNEXP, EXPTANH = "natural_log_exp_and_others", "exp_and_others"

        def tt(o, a, b, op, w=(), q=None):
            return (q or DV)(lambda e: e.tensor_tensor(o, a, b, op), w)

        def ts(o, a, s1, s2=None, op0=ALU.mult, op1=None, w=(), q=None):
            if op1 is None:
                return (q or DV)(lambda e: e.tensor_scalar(o, a, s1, None, op0), w)
            return (q or DV)(lambda e: e.tensor_scalar(o, a, s1, s2, op0, op1), w)

        def stt(o, a, s, b, op0, op1, w=()):
            return DV(lambda e: e.scalar_tensor_tensor(out=o, in0=a, scalar=s, in1=b, op0=op0, op1=op1), w)

        def addmax(o, a, b, mx, w=()):
            return DV(lambda e: e.tensor_tensor_reduce(o, a, b, 1.0, LOWEST, ALU.add, ALU.max, mx), w)

        def recip(o, a, w=()):
            return DV(lambda e: e.reciprocal(o, a), w)

        def vcopy(o, a, w=(), q=None):
            return (q or DV)(lambda e: e.tensor_copy(o, a), w)

        def scan(o, d0, d1, w=()):
            return DV(lambda e: e.tensor_tensor_scan(o, d0, d1, 0.0, ALU.mult, ALU.add), w)

        def mm(o, l, r, start=True, stop=True, w=(), inc=False, skip=False):
            return PE(lambda e: e.matmul(o, l, r, start=start, stop=stop, skip_group_check=skip), w, inc)

        def tp(o, i, w=(), inc=False):
            return PE(lambda e: e.transpose(o, i, ident), w, inc)

        dma_n = {}

        def dma(q, o, i, s, w=()):
            q.wait(w)
            q.items.append((lambda e: e.dma_start(o, i), s))
            dma_n[s.name] = dma_n.get(s.name, 0) + 16
            return (s, dma_n[s.name])

        def split(src, hi, lo, w, q=None):
            a = act(hi, src, w=w)
            b = tt(lo, src, hi.bitcast(F32), ALU.subtract, [a, *w], q or PO)
            return [a, b]

        def gain_split(src, gain, hi, lo, w):
            a = act(hi, src, w=w, scale=gain)
            b = stt(lo, src, gain, hi.bitcast(F32), ALU.mult, ALU.subtract, [a, *w])
            return [a, b]

        s_raw = [sem(f"s_raw{i}") for i in range(NR)]
        offs = np.concatenate([[0], np.cumsum([sum(b[3] for b in u) for u in units])])

        class Stream:
            def __init__(self):
                self.loaded, self.done, self.parts = {}, {}, {}
                self.u, self.b, self.next_split = -1, 0, 0

            def load(self, u):
                if u < len(units):
                    n = int(offs[u + 1] - offs[u])
                    self.loaded[u] = dma(SP, raw[u % NR][:, 0:n], wall[:, int(offs[u]):int(offs[u + 1])],
                                         s_raw[u % NR], [self.parts.get(u - NR)])

            def prepare(self, upto):
                while self.next_split <= min(upto, len(units) - 1):
                    u = self.next_split
                    n = int(offs[u + 1] - offs[u])
                    self.parts[u] = split(raw[u % NR][:, 0:n], whi[u % NS][:, 0:n], wlo[u % NS][:, 0:n],
                                          [self.loaded[u], self.done.get(u - NS)])
                    self.load(u + NR)
                    self.next_split += 1

            def take(self, want, n=1):
                if self.u < 0 or self.b == len(units[self.u]):
                    self.u, self.b = self.u + 1, 0
                    self.prepare(self.u + LOOK)
                u = units[self.u]
                assert u[self.b][:3] == want, (u[self.b], want)
                width = u[self.b][3]
                o = width * self.b
                self.b += n
                hi, lo = whi[self.u % NS], wlo[self.u % NS]
                return hi[:, o:o + width * n], lo[:, o:o + width * n], self.parts[self.u], self.b == len(u)

        ws = Stream()

        def proj(o, name, col, xh, xl, xtok, free, ks=range(KD), width=P, first=True, last=True, between=None):
            for i, k in enumerate(ks):
                hi, lo, parts, end = ws.take((name, k, col))
                hi, lo = hi[:, 0:width], lo[:, 0:width]
                mm(o, hi, xh[k], start=first and i == 0, stop=False, w=[free, parts[0], xtok[k]])
                mm(o, hi, xl[k], start=False, stop=False)
                t = mm(o, lo, xh[k], start=False, stop=last and i == len(ks) - 1, w=[parts[1]],
                       inc=end or i == len(ks) - 1)
                if end:
                    ws.done[ws.u] = t
                if between:
                    between(i)
            return t

        def proj_tokens(os, name, col, nb, xh, xl, xtok, between=None):
            toks = [None] * 4
            for k in range(KD):
                hi, lo, parts, end = ws.take((name, k, col), nb)
                for m in range(4):
                    xs = slice(P * m, P * m + P)
                    o = os[m].ap[:, 0:nb * P]
                    mm(o, xh[k][:, xs], hi, start=k == 0, stop=False, w=[os[m].free, parts, xtok[k]])
                    mm(o, xh[k][:, xs], lo, start=False, stop=False)
                    toks[m] = mm(o, xl[k][:, xs], hi, start=False, stop=k == KD - 1, inc=True)
                if end:
                    ws.done[ws.u] = toks[3]
                if between:
                    between(k)
            return toks

        s_c = [sem(f"s_c{i}") for i in range(4)]
        s_x = [sem(f"s_x{i}") for i in range(KD)]
        X = at("X", [P, KD * T], F32, arena)

        def xk(k):
            return X[:, T * k:T * k + T]

        tables(LNEXP)
        tvec = dma(AC, VECS[:, :], vec, s_c[0])
        xtok0 = []
        for k in range(KD):
            xtok0.append(dma((AC, SP)[k % 2], xk(k), xT[P * k:P * k + P, :], s_x[k]))
        for u in range(NR):
            ws.load(u)
        tcst = dma(AC, CST[:, :], cst, s_c[1])
        eps6 = SM[:, 0:1]
        eps5 = SM[:, 1:2]
        one = SM[:, 2:3]
        teps = [DV(lambda e: e.memset(eps6, 1e-6)), DV(lambda e: e.memset(eps5, 1e-5)),
                DV(lambda e: e.memset(one, 1.0))]

        hh = [HH[:, T * k:T * k + T] for k in range(KD)]
        hl = [HL[:, T * k:T * k + T] for k in range(KD)]

        main = Ring([b[:, :] for b in pb[0:4]])
        S = Ring([b[:, :] for b in pb[4:6]])
        TB = Ring([pb[6][:, :]])
        YB = Ring([pb[7][:, :]])

        a1 = Area(arena)
        qA = [a1(f"qA{t}", T) for t in range(4)]
        kA = [a1(f"kA{t}", T) for t in range(4)]
        vA = [a1(f"vA{m}", T) for m in range(4)]
        qC = [a1(f"qC{t}", T) for t in range(4)]
        kC = [a1(f"kC{t}", T) for t in range(4)]
        vC = [a1(f"vC{m}", T) for m in range(4)]
        qB = [a1(f"qB{t}", T) for t in range(4)]
        kB = a1("kB", T)
        vB = a1("vB", T)
        exB = [a1(f"exB{t}", T, F32R) for t in range(4)]
        GMs = [a1(f"gms{i}", T) for i in range(9)]
        work0 = a1.p
        Pr = Ring([a1(f"P{i}", T) for i in range(6)])
        PTr = Ring([a1(f"PT{i}", T) for i in range(3)])
        Br = Ring([a1(f"B{i}", T) for i in range(2)])
        Nr = Ring([a1(f"N{i}", T) for i in range(2)])
        Wr = Ring([a1(f"W{i}", T) for i in range(3)])
        STt = a1("stat", 8 * 16)
        Sr = Ring([STt[:, 16 * i:16 * i + 16] for i in range(8)])
        CQ = a1("CQ", 32)
        THr = Ring([a1(f"th{i}", T) for i in range(3)])
        cT = a1("cT", T)
        MH = at("MH", [P, KD * T], F32R, work0)
        ML = at("ML", [P, KD * T], F32R, work0 + 4 * KD * T)
        mh = [MH[:, T * k:T * k + T] for k in range(KD)]
        ml = [ML[:, T * k:T * k + T] for k in range(KD)]
        assert work0 + 8 * KD * T <= place["stat"]

        MF = at("maskf", [P, MASKS], F32, place["gms4"])
        tcu8 = dma(AC, MF[:, :], cu8, s_c[2])

        rst, rst8, rcol = qB[3][:, :], qB[2][:, :], SM[:, 56:60]
        acc, *sqs = (at(f"sq0{i}", [P, T], F32, place[f"exB{i}"])[:, :] for i in range(3))
        sqb = Ring(sqs)
        ptok = []
        tacc = None
        for k in range(KD):
            b = sqb.next() if k else Buf(acc)
            ptok.append(gain_split(xk(k), v("norm_gain", k), mh[k], ml[k], [xtok0[k], tvec]))
            if 1 <= k <= LOOK + 1:
                ws.prepare(k - 1)
            t = tt(b.ap, xk(k), xk(k), ALU.mult, [xtok0[k], b.free], PO)
            if k:
                tacc = tt(acc, acc, b.ap, ALU.add, [t, tacc])
                b.free = [tacc]
            else:
                tacc = t
        htok = []

        def first_norm():
            bank = TB.next()
            tables(LNEXP)
            t = mm(bank.ap, ones, acc, w=[tacc, tcst], inc=True)
            t = act(rst, bank.ap, ACT.Ln, [t, teps], bias=eps6, scale=1.0 / 1024)
            bank.free = [t]
            t = act(rst, rst, ACT.Exp, [t], scale=-0.5)
            t8 = ts(rst8, rst, 0.125, w=[t])
            return t, t8

        def norm_columns():
            bank = TB.next()
            for m in range(4):
                tm_ = mm(bank.ap[:, m:m + 1], rst[0:1, P * m:P * m + P], ones[0:1, 0:1], w=[trst, bank.free],
                         inc=m == 3)
            tc = vcopy(rcol, bank.ap[:, 0:4], [tm_])
            bank.free = [tc]
            return tc

        def first_normed():
            tmp = Ring([b.ap for b in sqb.bufs])
            for k in range(KD):
                b = tmp.next()
                t1 = stt(b.ap, xk(k), v("norm_gain", k), rst, ALU.mult, ALU.mult, [trst, tacc, b.free])
                sp = split(b.ap, hh[k], hl[k], [t1])
                b.free = sp
                htok.append(sp)
            return [AC.last, DV.last, PO.last]

        background = []

        def step(n=1):
            for _ in range(n):
                while background:
                    try:
                        next(background[0])
                        break
                    except StopIteration:
                        background.pop(0)

        def drain_background():
            while background:
                step()

        def pipeline(us):
            n = len(us)
            us[0].pre()
            for i in range(n + 5):
                if 0 <= i - DEEP < n:
                    us[i - DEEP].turn()
                if i + 1 < n:
                    us[i + 1].pre()
                if i < n:
                    us[i].scores()
                if 0 <= i - 1 < n:
                    us[i - 1].normal()
                if 0 <= i - DEEP - 1 < n:
                    us[i - DEEP - 1].values()
                if 0 <= i - DEEP - 2 < n:
                    us[i - DEEP - 2].late()
                yield

        class Unit:

            def pre(self):
                pass

            def late(self):
                pass

            def softmax(self, bank, tscore, bias, tbias, width, col, sink=None):
                st, p = self.st, Pr.next()
                t = addmax(p.ap[:, 0:width], bank.ap[:, 0:width], bias, st.ap[:, col:col + 1],
                           [tscore, tbias, p.free, st.free if col == 0 else None])
                bank.free = [t]
                self.addt = t
                nm = st.ap[:, col + 1:col + 2]
                if sink is None:
                    t = ts(nm, st.ap[:, col:col + 1], -1.0, w=[t])
                else:
                    t = ts(nm, st.ap[:, col:col + 1], sink, -1.0, ALU.max, ALU.mult, [t])
                t2 = act(p.ap[:, 0:width], p.ap[:, 0:width], ACT.Exp, [t], bias=nm,
                         accum=st.ap[:, col + 2:col + 3])
                return p, t2, t

            def turn(self):
                bank, self.pt = TB.next(), PTr.next()
                n = self.width // P
                for j in range(n):
                    t = tp(bank.ap[:, P * j:P * j + P], self.p.ap[:, P * j:P * j + P],
                           [self.tp, bank.free], inc=j == n - 1)
                self.p.free = [t]
                self.tpt = act(self.pt.ap[:, 0:self.width], bank.ap[:, 0:self.width], w=[t, self.pt.free])
                bank.free = [self.tpt]

        def finish_values(unit, o, lhs, tv, last):
            n = unit.width // P
            for j in range(n):
                t = mm(o, lhs(j), unit.pt.ap[:, P * j:P * j + P], start=j == 0, stop=j == n - 1,
                       w=[unit.tpt, tv, last], inc=j == n - 1)
            unit.pt.free = [t]
            return t

        tok = {}

        class UnitC(Unit):
            def __init__(self, h, i):
                self.h, self.i, self.t, self.r = h, i, h // 2, 64 * (h % 2)
                self.width = P * (i + 1)

            def pre(self):
                if self.i == 0:
                    bank, nb = TB.next(), Nr.next()
                    t = mm(bank.ap, ident[0:8, self.h:self.h + 1].to_broadcast([8, P]), cT[0:8, :],
                           w=[tok["c"], bank.free], inc=True)
                    UnitC.neg = nb
                    UnitC.tneg = act(nb.ap, bank.ap, w=[t, nb.free], scale=-1.0)
                    bank.free = [UnitC.tneg]
                self.nb, self.tn = UnitC.neg, UnitC.tneg

            def scores(self):
                i, r = self.i, self.r
                bank = S.next()
                ts_ = mm(bank.ap[:, 0:self.width], qC[self.t][r:r + 64, P * i:P * i + P],
                         kC[self.t][r:r + 64, 0:self.width], w=[tok["qC"], tok["kC"], bank.free], inc=True)
                tok["scoreC", self.t] = ts_
                bb = Br.next()
                cq = CQ[:, 8 * i + self.h:8 * i + self.h + 1]
                tb = [stt(bb.ap[:, P * i:P * i + P], self.nb.ap[:, P * i:P * i + P], cq, maskC, ALU.add, ALU.add,
                          [self.tn, tok["cq"], bb.free])]
                if i:
                    tb.append(ts(bb.ap[:, 0:P * i], self.nb.ap[:, 0:P * i], cq, op0=ALU.add))
                self.nb.free = tb
                self.st = Sr.next()
                self.p, self.te, _ = self.softmax(bank, ts_, bb.ap[:, 0:self.width], tb, self.width, 0)
                bb.free = [self.addt]

            def normal(self):
                st = self.st.ap
                t = recip(st[:, 3:4], st[:, 2:3], [self.te])
                self.tp = ts(self.p.ap[:, 0:self.width], self.p.ap[:, 0:self.width], st[:, 3:4], w=[t])
                self.st.free = [self.tp]

            def values(self):
                if self.i == 0 and self.r == 0:
                    UnitC.y = YB.next()
                y, r, i = UnitC.y, self.r, self.i
                t = finish_values(self, y.ap[r:r + 64, P * i:P * i + P],
                                  lambda j: vC[j][:, 64 * self.h:64 * self.h + 64], tok["vC"], y.free)
                if self.r and i == 3:
                    tok["yC", self.t] = vcopy(qC[self.t][:, :], y.ap, [t, tok["scoreC", self.t]])
                    y.free = [tok["yC", self.t]]

        class UnitA(Unit):
            def __init__(self, h, i):
                self.h, self.i = h, i
                self.width = P * (i + 1)

            def pre(self):
                if self.i == 0:
                    UnitA.nb = Br.next()
                    UnitA.tn = ts(UnitA.nb.ap, DA, 2.0 ** (-2 * (self.h + 1)), w=[UnitA.nb.free])
                self.nb, self.tn = UnitA.nb, UnitA.tn

            def scores(self):
                i = self.i
                self.st = Sr.next()
                self.ps, self.tes = [], []
                for m in range(2):
                    r = 64 * m
                    bank = S.next()
                    t = mm(bank.ap[:, 0:self.width], qA[self.h][r:r + 64, P * i:P * i + P],
                           kA[self.h][r:r + 64, 0:self.width], w=[tok["qA"], tok["kA"], bank.free], inc=True)
                    tok["scoreA", self.h] = t
                    p, te, _ = self.softmax(bank, t, self.nb.ap[:, 384 - P * i:512], self.tn, self.width, 4 * m)
                    self.ps.append(p)
                    self.tes.append(te)
                self.nb.free = [self.addt]

            def normal(self):
                st, wd = self.st.ap, self.width
                p0, p1 = self.ps
                a = recip(st[:, 3:4], st[:, 2:3], [self.tes[0]])
                b = recip(st[:, 7:8], st[:, 6:7], [self.tes[1]])
                b = ts(p1.ap[:, 0:wd], p1.ap[:, 0:wd], st[:, 7:8], lam, ALU.mult, ALU.mult, [b, tok["lam"]])
                self.tp = stt(p0.ap[:, 0:wd], p0.ap[:, 0:wd], st[:, 3:4], p1.ap[:, 0:wd], ALU.mult, ALU.subtract,
                              [a, b])
                self.p = p0
                p1.free = [self.tp]
                self.st.free = [self.tp]

            def values(self):
                h, i = self.h, self.i
                if i == 0:
                    UnitA.y = YB.next()
                y = UnitA.y
                t = finish_values(self, y.ap[:, P * i:P * i + P], lambda j: vA[j][:, P * h:P * h + P],
                                  tok["vA"], y.free)
                if i == 3:
                    dst = qA[h][:, :]
                    t = vcopy(dst, y.ap, [t, tok["scoreA", h]])
                    y.free = [t]
                    self.sq = Wr.next()
                    self.tsq = act(self.sq.ap, dst, ACT.Square, [t, self.sq.free])

            def late(self):
                h = self.h
                if self.i == 3:
                    sq, ts_, dst = self.sq, self.tsq, qA[h][:, :]
                    bank = TB.next()
                    tables(LNEXP)
                    tm_ = mm(bank.ap, ones, sq.ap, w=[ts_, bank.free], inc=True)
                    t2 = act(sq.ap, bank.ap, ACT.Ln, [tm_], bias=eps5, scale=1.0 / 128)
                    bank.free = [t2]
                    t2 = act(sq.ap, sq.ap, ACT.Exp, [t2], scale=-0.5)
                    tok["yA", h] = stt(dst, dst, subg, sq.ap, ALU.mult, ALU.mult, [t2, tok["subg"]])
                    sq.free = [tok["yA", h]]

        class UnitB(Unit):
            def __init__(self, t, s, i):
                self.t, self.r, self.i, self.h = t, 64 * s, i, t + 4 * s
                self.j0 = max(i - 1, 0)
                self.width = P * (i + 1 - self.j0)

            def pre(self):
                if self.i == 0:
                    UnitB.nb = Br.next()
                    UnitB.tn = ts(UnitB.nb.ap[:, 0:256], DB, 2.0 ** -(self.h + 1), w=[UnitB.nb.free])
                self.nb, self.tn = UnitB.nb, UnitB.tn

            def scores(self):
                i, r = self.i, self.r
                self.st = Sr.next()
                bank = S.next()
                t = mm(bank.ap[:, 0:self.width], qB[self.t][r:r + 64, P * i:P * i + P],
                       kB[r:r + 64, P * self.j0:P * i + P], w=[tok["qB"], tok["kB"], bank.free], inc=True)
                tok["scoreB", self.t] = t
                self.p, self.te, tm_ = self.softmax(bank, t, self.nb.ap[:, 256 - self.width:256], self.tn,
                                                    self.width, 0, v("sinks", self.h))
                self.nb.free = [self.addt]
                st = self.st.ap
                self.te2 = act(st[:, 4:5], v("sinks", self.h), ACT.Exp, [tm_], bias=st[:, 1:2])

            def normal(self):
                st, wd = self.st.ap, self.width
                t = tt(st[:, 5:6], st[:, 2:3], st[:, 4:5], ALU.add, [self.te, self.te2])
                t = recip(st[:, 3:4], st[:, 5:6], [t])
                self.tp = ts(self.p.ap[:, 0:wd], self.p.ap[:, 0:wd], st[:, 3:4], w=[t])
                self.st.free = [self.tp]

            def values(self):
                if self.i == 0 and self.r == 0:
                    UnitB.y = YB.next()
                y, r, i = UnitB.y, self.r, self.i
                t = finish_values(self, y.ap[r:r + 64, P * i:P * i + P],
                                  lambda j: vB[:, P * (self.j0 + j) + r:P * (self.j0 + j) + r + 64], tok["vB"],
                                  y.free)
                if self.r and i == 3:
                    tok["yB", self.t] = vcopy(qB[self.t][:, :], y.ap, [t, tok["scoreB", self.t]])
                    y.free = [tok["yB", self.t]]

        def slot(i):
            if i in (1, 4, 7):
                step()

        lam, subg = SM[:, 8:9], SM[:, 9:10]
        lam_init = 0.8 - 0.6 * math.exp(-0.3 * 0)
        lv = VEC["lam_vec"][0]
        scr = THr.bufs[0].ap
        tl = []
        for j in range(2):
            tl.append(DV(lambda e, j=j: e.tensor_tensor_reduce(
                scr[:, 64 * j:64 * j + 64], VECS[:, lv + 128 * j:lv + 128 * j + 64],
                VECS[:, lv + 128 * j + 64:lv + 128 * j + 128], 1.0, 0.0, ALU.mult, ALU.add,
                SM[:, 10 + j:11 + j]), [tvec]))
        t = act(SM[:, 12:14], SM[:, 10:12], ACT.Exp, tl)
        t = tt(SM[:, 14:15], SM[:, 12:13], SM[:, 13:14], ALU.subtract, [t])
        tok["lam"] = ts(lam, SM[:, 14:15], lam_init, op0=ALU.add, w=[t])
        tok["subg"] = ts(subg, v("subln"), 1.0 - lam_init, w=[tvec])

        def fm_tile(col, dst, scale=None, on=None, w=()):
            b = main.next()
            t = proj(b.ap, "win", col, hh, hl, htok, b.free, between=slot)
            if on is DV:
                t = vcopy(dst, b.ap, [t, *w]) if scale is None else ts(dst, b.ap, scale, w=[t, *w])
            else:
                t = act(dst, b.ap, w=[t, *w], scale=scale or 1.0)
            b.free = [t]
            return t

        def first_tile(col, width=P):
            b = main.next()
            t = proj(b.ap[0:width, :], "win", col, mh, ml, ptok, b.free, width=width)
            return b, t

        b, t = first_tile(FC, 8)
        trst, trst8 = first_norm()
        fx, fn, fa = (GMs[i][0:8, :] for i in range(3))
        t1 = tt(fx, b.ap[0:8, :], rst[0:8, :], ALU.mult, w=[t, trst])
        b.free = [t1]
        t1 = ts(fx, fx, VECS[0:8, VEC["b_forget"][0]:VEC["b_forget"][0] + 1], op0=ALU.add, w=[t1, tvec])
        t2 = ts(fn, fx, 0.0, op0=ALU.min, w=[t1])
        t3 = stt(fa, fn, -2.0, fx, ALU.mult, ALU.add, [t2])
        t4 = act(fa, fa, ACT.Exp, [t3], scale=-1.0)
        t4 = act(fa, fa, ACT.Ln, [t4, teps], bias=one[0:8, :])
        t5 = tt(fn, fn, fa, ALU.subtract, [t4])
        tok["c"] = scan(cT[0:8, :], ones[0:8, 0:1].to_broadcast([8, T]), fn, [t5])
        for c, dst, r, name in ((KC, kC, rst, "kC"), (QC, qC, rst8, "qC")):
            for t in range(4):
                b, tk = first_tile(c + P * t)
                tok[name] = tt(dst[t][:, :], b.ap, r, ALU.mult, [tk, trst8])
                b.free = [tok[name]]
                if c == KC and t == 0:
                    trc = norm_columns()
                if c == KC and t == 1:
                    bank = TB.next()
                    for m in range(4):
                        tk = mm(bank.ap[:, 8 * m:8 * m + 8], cT[0:8, P * m:P * m + P], ident[0:8, 0:8],
                                w=[tok["c"], bank.free], inc=m == 3)
                    tok["cq"] = vcopy(CQ[:, :], bank.ap[:, 0:32], [tk])
                    bank.free = [tok["cq"]]
            if c == KC:
                first_free = first_normed()
        bs = [main.next() for _ in range(4)]
        tm4 = proj_tokens(bs, "win", VC, 4, mh, ml, ptok)
        for m in range(4):
            tok["vC"] = act(vC[m][:, :], bs[m].ap, w=[tm4[m], trc], scale=rcol[:, m:m + 1])
            bs[m].free = [tok["vC"]]
        work_free = [tm4]
        for r in (Pr, PTr, Br, Nr, Wr):
            for b in r.bufs:
                b.free = [work_free]
        background.append(pipeline([UnitC(h, i) for h in range(8) for i in range(4)]))

        xfree = [first_free, tok["qC"]]
        for t in range(4):
            tok["kA"] = fm_tile(KA + P * t, kA[t][:, :], w=xfree)
        for t in range(4):
            tok["qA"] = fm_tile(QA + P * t, qA[t][:, :], 0.125, w=xfree)
        bs = [main.next() for _ in range(4)]
        tm4 = proj_tokens(bs, "win", VA, 4, hh, hl, htok, lambda k: step(1 + k % 2))
        for m in range(4):
            tok["vA"] = act(vA[m][:, :], bs[m].ap, w=[tm4[m]])
            bs[m].free = [tok["vA"]]
        background.append(pipeline([UnitA(h, i) for h in range(4) for i in range(4)]))
        tok["kB"] = fm_tile(KB, kB[:, :])
        vt = THr.next()
        t = fm_tile(VB, vt.ap, w=[tl])
        bank = TB.next()
        for m in range(4):
            t2 = tp(bank.ap[:, P * m:P * m + P], vt.ap[:, P * m:P * m + P], [t, bank.free], inc=m == 3)
        vt.free = [t2]
        tok["vB"] = act(vB[:, :], bank.ap, w=[t2])
        bank.free = [tok["vB"]]
        for t in range(4):
            tok["qB"] = fm_tile(QB + P * t, qB[t][:, :], 0.125, w=xfree)
        background.append(pipeline([UnitB(t, s, i) for t in range(4) for s in range(2) for i in range(4)]))

        def gate_tile(col, y, ty, hi, lo):
            b = main.next()
            t = proj(b.ap, "win", col, hh, hl, htok, b.free, between=slot)
            th = THr.next()
            t1 = act(th.ap, b.ap, ACT.Tanh, [t, th.free], scale=0.5)
            t1 = stt(th.ap, th.ap, 1.0, b.ap, ALU.add, ALU.mult, [t1])
            b.free = [t1]
            t1 = stt(th.ap, th.ap, 0.5, y, ALU.mult, ALU.mult, [t1, ty()])
            sp = split(th.ap, hi, lo, [t1])
            th.free = sp
            return sp

        def alias(name, like):
            return at(name, [P, T], F32R, place[like])

        ygh, ygl = {}, {}
        for t in range(4):
            ygh["c", t], ygl["c", t] = alias(f"ychi{t}", f"kC{t}"), alias(f"yclo{t}", f"qC{t}")
            ygh["a", t], ygl["a", t] = alias(f"yahi{t}", f"kA{t}"), alias(f"yalo{t}", f"qA{t}")
            ygh["b", t], ygl["b", t] = exB[t], alias(f"yblo{t}", f"qB{t}")
        ygt = {}

        def need(key):
            while key not in tok:
                step()
            return tok[key]

        for t in range(4):
            need(("yC", t))
            ygt["c", t] = gate_tile(GC + P * t, qC[t][:, :], lambda t=t: tok["yC", t], ygh["c", t][:, :],
                                    ygl["c", t][:, :])
        gmt = {}

        def gm_tile(d, j, buf, free=()):
            b = main.next()
            t = proj(b.ap, "win", GM + 1024 * j + P * d, hh, hl, htok, b.free, between=slot)
            gmt[d, j] = (act(buf, b.ap, ACT.Tanh, [t, *free], scale=0.5), buf)
            b.free = [gmt[d, j][0]]

        tcu8 = vcopy(CU8[:, :], MF[:, :], [tcu8], PO)
        for d in range(3):
            for j in range(3):
                gm_tile(d, j, GMs[3 * d + j][:, :], [tcu8])
        for t in range(4):
            need(("yA", t))
            ygt["a", t] = gate_tile(GA + P * t, qA[t][:, :], lambda t=t: tok["yA", t], ygh["a", t][:, :],
                                    ygl["a", t][:, :])
        for t in range(4):
            need(("yB", t))
            ygt["b", t] = gate_tile(GB + P * t, qB[t][:, :], lambda t=t: tok["yB", t], ygh["b", t][:, :],
                                    ygl["b", t][:, :])
        drain_background()
        att_free = [AC.last, DV.last, PE.last, PO.last]

        tsp = {}

        def rg_const():
            sl, nn = SM[:, 24:27], SM[:, 27:30]
            la = v("rg_lam", 0, 3)
            t = ts(nn, la, 0.0, op0=ALU.min, w=[tvec])
            t1 = stt(sl, nn, -2.0, la, ALU.mult, ALU.add, [t])
            t1 = act(sl, sl, ACT.Exp, [t1], scale=-1.0)
            t1 = act(sl, sl, ACT.Ln, [t1], bias=one)
            t1 = tt(sl, sl, nn, ALU.subtract, [t1])
            t1 = ts(SM[:, 30:33], sl, 8.0, w=[t1])
            tsp["sp8"] = [t1, ts(SM[:, 51:54], SM[:, 30:33], -1.0, w=[t1])]
            tsp["hb"] = ts(SM[:, 33:39], v("rg_br", 0, 6), 0.5)
            lb = v("hg_lb", 0, 3)
            t = tt(SM[:, 39:42], lb, lb, ALU.subtract)
            t = act(SM[:, 39:42], SM[:, 39:42], ACT.Exp, [t])
            t = recip(SM[:, 42:45], SM[:, 39:42], [t])
            t = tt(SM[:, 39:42], SM[:, 39:42], SM[:, 42:45], ALU.mult, [t])
            t = tt(SM[:, 45:48], SM[:, 39:42], SM[:, 39:42], ALU.subtract, [t])
            tsp["lb"] = ts(SM[:, 48:51], SM[:, 45:48], -1.0, 1.0, ALU.mult, ALU.add, [t])

        lbv, olb = SM[:, 45:48], SM[:, 48:51]

        rg_const()

        mtok = []
        Gr = Ring([g[:, :] for g in GMs])
        for d in range(8):
            if d >= 3:
                for j in range(3):
                    g = Gr.next()
                    gm_tile(d, j, g.ap, [g.free])
                    gmt[d, j] += (g,)
            else:
                for j in range(3):
                    gmt[d, j] += (Gr.next(),)
            prev = None
            for n, j in (("c", 2), ("a", 0), ("b", 1)):
                b = main.next()
                t = proj(b.ap, "up_" + n, P * d, [ygh[n, k][:, :] for k in range(4)],
                         [ygl[n, k][:, :] for k in range(4)], [ygt[n, k] for k in range(4)], b.free,
                         range(4))
                tg, gb, g = gmt[d, j]
                t = stt(gb, gb, 1.0, b.ap, ALU.add, ALU.mult, [t, tg])
                b.free = [t]
                if prev is not None:
                    t2 = tt(gb, gb, prev[0], ALU.add, [t, prev[1]])
                    prev[2].free = [t2]
                    t = t2
                prev = (gb, t, g)
            gb, t, g = prev
            a = act(mh[d], gb, w=[t, att_free], scale=0.5)
            l = stt(ml[d], gb, 0.5, mh[d].bitcast(F32), ALU.mult, ALU.subtract, [a])
            g.free = [a, l]
            mtok.append([a, l])
        up_free = [PE.last]
        s_x2 = [sem(f"s_xr{i}") for i in range(2)]
        xr = []
        for i in range(2):
            tok_ = dma(SP, X[:, 4 * T * i:4 * T * i + 4 * T].rearrange("p (k t) -> p k t", k=4),
                       xT[4 * P * i:4 * P * i + 4 * P, :].rearrange("(k p) t -> p k t", p=P), s_x2[i], up_free)
            xr += [tok_] * 4

        a2 = Area(arena + 4 * KD * T)
        U3, A3, B3, G3 = (a2(n, 3 * T) for n in ("U3", "A3", "B3", "G3"))
        r1, r3, r6 = (a2(n, T)[:, :] for n in ("R1", "R3", "R6"))
        q3, k3, g64, g512 = (a2(n, 3 * T) for n in ("q3", "k3", "g64", "g512"))
        Es = [a2(f"E{i}", 3 * T) for i in range(2)]
        QH = [a2(f"QH{i}", 3 * T // 2) for i in range(2)]
        hv, gs = (a2(n, 3 * T) for n in ("hv", "gs"))
        ST = [a2(f"ST{p}", 2 * T) for p in range(3)]
        sch = [a2(f"sch{t}", T, F32R) for t in range(2)]
        scl = [a2(f"scl{t}", T, F32R) for t in range(2)]
        ZP = [a2(f"zp{i}", T + 16) for i in range(2)]
        offr = Ring([a2(f"off{i}", T) for i in range(2)])
        RGW = at("RGW", [P, 6 * P], F32, place["cst"] + 512 * 4)

        def c3(x, t):
            return x[:, T * t:T * t + T]

        fg = lambda k: v("final_gain", k)
        gg = SM[:, 16:24]
        tgg = tt(gg, v("final_gain", 0, 8), v("mix_norm", 0, 8), ALU.mult, [tvec])
        acc1, acc2, r2 = c3(U3, 0), c3(U3, 1), c3(U3, 2)
        sq = Ring([c3(A3, i) for i in range(3)] + [c3(B3, i) for i in range(3)])
        w0 = [up_free, DV.last, AC.last, PO.last]
        ty, htok = [], []
        ta1 = ta2 = None
        for d in range(8):
            b = main.next()
            t = proj(b.ap, "wo", P * d, mh, ml, mtok, b.free)
            t = tt(xk(d), b.ap, xk(d), ALU.add, [t, xr[d]])
            b.free = [t]
            ty.append(t)
            htok.append(gain_split(xk(d), gg[:, d:d + 1], hh[d], hl[d], [t, tgg, up_free]))
            o1, o2 = (Buf(acc1), Buf(acc2)) if d == 0 else (sq.next(), sq.next())
            t1 = act(o1.ap, xk(d), ACT.Square, [t, o1.free, w0])
            t2 = act(o2.ap, xk(d), ACT.Square, [t, o2.free, w0], scale=fg(d))
            if d:
                ta1 = tt(acc1, acc1, o1.ap, ALU.add, [t1, ta1])
                ta2 = tt(acc2, acc2, o2.ap, ALU.add, [t2, ta2])
                o1.free, o2.free = [ta1], [ta2]
            else:
                ta1, ta2 = t1, t2
        fence = [AC.last, DV.last, PO.last, PE.last]
        s_rw = sem("s_rw")
        trw = dma(SP, RGW[:, :], rgw, s_rw, fence)

        m3 = Ring([pb[i][:, :] for i in (0, 1, 2)])
        x5 = Ring([pb[i][:, :] for i in (3, 4, 5, 6, 7)])
        x4 = Ring([pb[i][:, :] for i in (3, 4)])
        ob = [Buf(pb[i][:, :]) for i in (5, 6, 7)]
        for b in [*m3.bufs, *x5.bufs]:
            b.free = fence
        for i in range(2):
            x4.bufs[i] = x5.bufs[i]
        ob = x5.bufs[2:]

        heads_bg, gates_bg = [], []
        ticks = [0]

        def advance(gens):
            while gens:
                try:
                    next(gens[0])
                    return
                except StopIteration:
                    gens.pop(0)

        def tick(i=1):
            if i % 2:
                ticks[0] += 1
                if ticks[0] % 2:
                    advance(gates_bg)
                advance(heads_bg)

        def tile2(col, between=tick, ring=None):
            b = (ring or m3).next()
            return b, proj(b.ap, "win2", col, hh, hl, htok, b.free, between=between)

        def both_norms():
            bk1, bk2 = x5.next(), x5.next()
            tables(LNEXP)
            t1 = mm(bk1.ap, ones, acc1, w=[ta1, bk1.free], inc=True)
            t2 = mm(bk2.ap, ones, acc2, w=[ta2, bk2.free], inc=True)
            t = act(r1, bk1.ap, ACT.Ln, [t1, w0], bias=eps6, scale=1.0 / 1024)
            bk1.free = [t]
            tr1 = act(r1, r1, ACT.Exp, [t], scale=-0.5)
            t = tt(r3, r1, r1, ALU.mult, [tr1, w0])
            t = tt(r2, bk2.ap, r3, ALU.mult, [t, t2])
            bk2.free = [t]
            t = act(r2, r2, ACT.Ln, [t], bias=eps6, scale=1.0 / 1024)
            t = act(r2, r2, ACT.Exp, [t], scale=-0.5)
            tr = tt(r3, r1, r2, ALU.mult, [t])
            tr6 = tt(r6, r3, r3, ALU.mult, [tr], PO)
            return tr1, tr, tr6

        def both_columns():
            bank = x5.next()
            for m in range(4):
                tm_ = mm(bank.ap[:, m:m + 1], r3[0:1, P * m:P * m + P], ones[0:1, 0:1], w=[tr3, bank.free],
                         inc=m == 3)
            tc = vcopy(rcol2, bank.ap[:, 0:4], [tm_])
            bank.free = [tc]
            return tc

        rcol2 = SM[:, 60:64]
        tzp = [DV(lambda e, z=z: e.memset(z[:, 0:16], 0.0), fence) for z in ZP]
        zr = Ring(ZP)
        for b in zr.bufs:
            b.free = [tzp]
        tst = [PO(lambda e, s=s: e.memset(s[:, :], 0.0), fence) for s in ST]
        up_mid, down_mid = SM[:, 64:65], SM[:, 65:66]
        tmid = [PO(lambda e: e.memset(up_mid, MIDDLE)), PO(lambda e: e.memset(down_mid, -MIDDLE))]

        E3 = Es[0]
        tg = []
        pend = []
        for t in range(3):
            pend.append(tile2(BF + P * t, None))
            if t == 0:
                tr1, tr3, tr6 = both_norms()
        for t in range(3):
            b, tk_ = pend[t]
            e = c3(E3, t)
            t1 = tt(e, b.ap, r3, ALU.mult, [tk_, tr3, fence])
            b.free = [t1]
            tg.append(act(e, e, ACT.Exp, [t1], scale=-1.0))
        tq = []
        qt = Ring([c3(gs, i) for i in range(3)])
        for t in range(3):
            b, tk_ = tile2(BQ + P * t, None, x5)
            if t == 0:
                trc2 = both_columns()
            qt.bufs[t].free = tt(qt.bufs[t].ap, b.ap, r3, ALU.mult, [tk_, fence])
            b.free = [qt.bufs[t].free]
            e = c3(E3, t)
            t1 = ts(e, e, 1.0, op0=ALU.add, w=[tg[t]])
            t1 = recip(e, e, [t1])
            t1 = ts(e, e, olb[:, t:t + 1], lbv[:, t:t + 1], ALU.mult, ALU.add, [t1, tsp["lb"]])
            t2 = ts(c3(k3, t), e, -1.0, 1.0, ALU.mult, ALU.add, [t1, fence])
            t1 = ts(e, e, 2.0 ** -63, op0=ALU.max, w=[t1, t2])
            tg[t] = act(e, e, ACT.Ln, [t1])
        tlf = tg
        tG = []
        for t in range(3):
            tG.append(scan(c3(g64, t), m64, c3(E3, t), [tlf[t], fence]))
            tG.append(scan(c3(g512, t), ones[:, 0:1].to_broadcast([P, T]), c3(E3, t), [tlf[t], fence]))
        for t in range(3):
            x_, q_ = qt.bufs[t], c3(q3, t)
            t2 = act(q_, x_.ap, ACT.Tanh, [x_.free, fence], scale=0.5)
            t1 = stt(q_, q_, 1.0, x_.ap, ALU.add, ALU.mult, [t2])
            tq.append(ts(q_, q_, 0.5 * 0.125, w=[t1]))
        thv = []

        def blocks(x, h):
            return x[:, :].rearrange("p (b two r) -> p b two r", two=2, r=h)

        def hgrn_steps():
            merged = [[t] for t in tst]
            efree = [[tG], []]
            nth = [0]

            def factors(h, src):
                i = nth[0] % 2
                nth[0] += 1
                E, qh = Es[i], QH[i]
                g, d = blocks(src, h), blocks(E, h)
                nb = 3 * T // (2 * h)
                mid = g[:, :, 0, h - 1:h].to_broadcast([P, nb, h])
                w = [tG, efree[i], fence]
                t1 = tt(d[:, :, 0, :], mid, g[:, :, 0, :], ALU.subtract, w)
                t2 = tt(d[:, :, 1, :], g[:, :, 1, :], mid, ALU.subtract, w)
                t = act(E[:, :], E[:, :], ACT.Exp, [t1, t2])
                k_ = blocks(k3, h)
                tk_ = tt(d[:, :, 0, :], d[:, :, 0, :], k_[:, :, 0, :], ALU.mult, [t], PO)
                qv = qh[:, :].rearrange("p (b r) -> p b r", r=h)
                tq_ = tt(qv, blocks(q3, h)[:, :, 1, :], d[:, :, 1, :], ALU.mult, [t, tq, efree[i], fence])
                return h, i, [tk_, tq_]

            def base():
                i = nth[0] % 2
                nth[0] += 1
                E = Es[i]
                g = g64[:, :].rearrange("p (b r) -> p b r", r=4)
                d = E[:, :].rearrange("p (b r) -> p b r", r=4)
                mid = g[:, :, 1:2].to_broadcast([P, 3 * P, 4])
                t = tt(d, g, mid, ALU.subtract, [tG, efree[i]])
                t1 = act(g64[:, :], E[:, :], ACT.Exp, [t, tmid], bias=up_mid)
                t2 = act(E[:, :], E[:, :], ACT.Exp, [t, t1, tmid], bias=down_mid, scale=-1.0)
                tq_ = tt(g64[:, :], g64[:, :], q3[:, :], ALU.mult, [t1, tq])
                tk_ = tt(E[:, :], E[:, :], k3[:, :], ALU.mult, [t2], PO)
                return 0, i, [tk_, tq_]

            def scores_near(part):
                h, i, tf = part
                l = LEVELS.index(h)
                E, qv = Es[i], QH[i]
                msk = lvmask(l).rearrange("p (b r) -> p b r", r=h)
                for hd in range(6):
                    p, r = hd // 2, 64 * (hd % 2)
                    bank = x5.next()
                    for m in range(4):
                        x0 = T * p + P * m
                        t = mm(bank.ap[:, 64 * m:64 * m + 64], E[r:r + 64, x0:x0 + P],
                               qv[r:r + 64, x0 // 2:x0 // 2 + 64], w=[tf, bank.free], inc=m == 3)
                    dst = ST[p][:, T * (hd % 2):T * (hd % 2) + T].rearrange(
                        "p (b two r) -> p b two r", two=2, r=h)[:, :, 1, :]
                    src = bank.ap[:, 0:256].rearrange("p (b r) -> p b r", r=h)
                    tc = DV(lambda e, dst=dst, msk=msk, src=src: e.copy_predicated(dst, msk, src),
                            [t, merged[p], tcu8])
                    merged[p] = [tc]
                    bank.free = [tc]
                    if hd % 2:
                        yield
                efree[i] = [t]

            def scores_base(part):
                _, i, tf = part
                E = Es[i]
                for hd in range(6):
                    p, r = hd // 2, 64 * (hd % 2)
                    bank = x5.next()
                    for m in range(4):
                        x0 = T * p + P * m
                        t = mm(bank.ap[:, P * m:P * m + P], E[r:r + 64, x0:x0 + P], g64[r:r + 64, x0:x0 + P],
                               w=[tf, bank.free], inc=m == 3)
                    dst = ST[p][:, T * (hd % 2):T * (hd % 2) + T]
                    tc = DV(lambda e, dst=dst, src=bank.ap: e.copy_predicated(dst, b4mask, src),
                            [t, merged[p], tcu8])
                    merged[p] = [tc]
                    bank.free = [tc]
                    yield
                efree[i] = [t]

            def near_values():
                for hd in range(6):
                    p, r = hd // 2, 64 * (hd % 2)
                    for m in range(4):
                        t = mm(ob[p].ap[r:r + 64, P * m:P * m + P],
                               hv[:, 384 * m + 64 * hd:384 * m + 64 * hd + 64],
                               ST[p][:, T * (hd % 2) + P * m:T * (hd % 2) + P * m + P], start=m == 0, stop=False,
                               w=[merged[p], thv, ob[p].free], inc=m == 3, skip=True)
                    if hd % 2:
                        yield

            def far(part, last):
                h, i, tf = part
                E, qv = Es[i], QH[i]
                late = []
                for hd in range(6):
                    p, r = hd // 2, 64 * (hd % 2)
                    x0 = T * p
                    pairs = [(0, 0, 2, 2), (1, 0, 2, 2)] if h == 256 else [(0, 0, 1, 1), (2, 1, 3, 1)]
                    bank = x4.next()
                    off = 0
                    for s, c0, t0, n in pairs:
                        t = mm(bank.ap[:, off:off + P * n], E[r:r + 64, x0 + P * s:x0 + P * s + P],
                               qv[r:r + 64, x0 // 2 + P * c0:x0 // 2 + P * (c0 + n)], w=[tf, bank.free],
                               inc=True)
                        off += P * n
                    sc = offr.next()
                    tc = act(sc.ap[:, 0:off], bank.ap[:, 0:off], w=[t, sc.free, fence])
                    bank.free = [tc]
                    late.append((hd, p, r, pairs, sc, tc))
                    if len(late) > 1:
                        far_values(*late.pop(0), last)
                    yield
                efree[i] = [t]
                far_values(*late.pop(0), last)
                yield

            def far_values(hd, p, r, pairs, sc, tc, last):
                off = 0
                for s, c0, t0, n in pairs:
                    o = ob[p].ap[r:r + 64, P * t0:P * (t0 + n)]
                    t = mm(o, hv[:, 384 * s + 64 * hd:384 * s + 64 * hd + 64], sc.ap[:, off:off + P * n],
                           start=False, stop=last, w=[tc, thv], inc=True, skip=True)
                    off += P * n
                sc.free = [t]
                if last:
                    tok["ho", p] = t

            parts = [factors(64, g512)]
            yield
            parts.append(factors(32, g64))
            yield
            for h in (16, 8, 4, 0):
                yield from scores_near(parts.pop(0))
                parts.append(factors(h, g64) if h else base())
                yield
            yield from scores_near(parts.pop(0))
            parts.append(factors(128, g512))
            yield
            yield from scores_base(parts.pop(0))
            parts.append(factors(256, g512))
            yield
            yield from near_values()
            yield from far(parts.pop(0), False)
            yield from far(parts.pop(0), True)

        heads_bg.append(hgrn_steps())
        bs = [*m3.bufs, x5.next()]
        m3.i = 0
        tm4 = proj_tokens(bs, "win2", BV, 3, hh, hl, htok,
                          lambda k: advance(heads_bg) if k in (1, 4) else None)
        for m in range(4):
            t = act(hv[:, 384 * m:384 * m + 384], bs[m].ap[:, 0:384], w=[tm4[m], trc2, fence],
                    scale=rcol2[:, m:m + 1])
            bs[m].free = [t]
            thv.append(t)

        tu = []
        for t in range(3):
            b, tk_ = tile2(AU + P * t)
            z = zr.next()
            tz = tt(z.ap[:, 16:16 + T], b.ap, r3, ALU.mult, w=[tk_, z.free])
            b.free = [tz]
            u = c3(U3, t)
            cw = VEC["rg_cw"][0] + 4 * t
            tt_ = ts(u, z.ap[:, 16:16 + T], VECS[:, cw + 3:cw + 4], v("rg_cb", t), ALU.mult, ALU.add, [tz, fence])
            for j in range(3):
                tt_ = stt(u, z.ap[:, 13 + j:13 + j + T], VECS[:, cw + j:cw + j + 1], u, ALU.mult, ALU.add, [tt_])
            z.free = [tt_]
            tu.append(tt_)

        def rg_steps():
            tr_, ti_ = [], []
            for t in range(3):
                for g, dst, lst in ((0, A3, tr_), (1, B3, ti_)):
                    b = x5.next()
                    tm_ = mm(b.ap, RGW[:, P * (2 * t + g):P * (2 * t + g) + P], c3(U3, t),
                             w=[tu[t], trw, b.free], inc=True)
                    ta = act(c3(dst, t), b.ap, ACT.Tanh, [tm_, tsp["hb"], fence],
                             bias=SM[:, 33 + 3 * g + t:34 + 3 * g + t], scale=0.5)
                    b.free = [ta]
                    lst.append(ts(c3(dst, t), c3(dst, t), 0.5, 0.5, ALU.mult, ALU.add, [ta]))
                yield
            for t in range(3):
                a, bb, u, g = c3(A3, t), c3(B3, t), c3(U3, t), c3(G3, t)
                t1 = act(g, a, ACT.Tanh, [tr_[t], tsp["sp8"], fence], scale=SM[:, 30 + t:31 + t])
                t2 = act(a, a, ACT.Exp, [t1], scale=SM[:, 51 + t:52 + t])
                t3 = tt(bb, bb, u, ALU.mult, [ti_[t]])
                t4 = act(u, a, ACT.Square, [t2, t3])
                t4 = stt(g, u, 1.0, g, ALU.add, ALU.mult, [t4, t1])
                tr_[t], ti_[t] = [t2], [t3, t4]
                yield
            t = act(G3[:, :], G3[:, :], ACT.Sqrt, [ti_[0], ti_[1], ti_[2]])
            for i in range(3):
                t1 = tt(c3(B3, i), c3(B3, i), c3(G3, i), ALU.mult, [t])
                tok["rg", i] = scan(c3(U3, i), c3(A3, i), c3(B3, i), [t1, tr_[i]])
                yield

        gates_bg.append(rg_steps())

        YMH, YML = {}, {}
        ytok = {}

        txb = []
        for k in range(KD):
            t = act(xk(k), xk(k), w=[htok[k], ty[k]], scale=fg(k))
            txb.append(tt(xk(k), xk(k), r1, ALU.mult, [t, tr1], PO))

        scy = [at(f"scy{t}", [P, T], F32, place[f"scl{t}"])[:, :] for t in range(2)]
        scc = [at(f"scc{t}", [P, T], F32, place[f"sch{t}"])[:, :] for t in range(2)]
        cc, cz = [], []
        for t in range(2):
            b, tk_ = tile2(CC + P * t)
            t1 = tt(scc[t], b.ap, r6, ALU.mult, [tk_, tr6, fence])
            b.free = [t1]
            cc.append(t1)
        for t in range(2):
            b, tk_ = tile2(CV + P * t)
            z = zr.next()
            t1 = tt(z.ap[:, 16:16 + T], b.ap, scc[t], ALU.mult, [tk_, cc[t], z.free])
            b.free = [t1]
            y = scy[t]
            cw = VEC["sc_cw"][0] + 3 * t
            t1 = ts(y, z.ap[:, 16:16 + T], VECS[:, cw + 2:cw + 3], w=[t1, fence])
            for j in range(2):
                t1 = stt(y, z.ap[:, 14 + j:14 + j + T], VECS[:, cw + j:cw + j + 1], y, ALU.mult, ALU.add, [t1])
            z.free = [t1]
            cz.append(tt(y, y, r3, ALU.mult, [t1], PO))
        while gates_bg:
            tick()
        tgs = []
        for t in range(3):
            b, tk_ = tile2(BG + P * t)
            x_, g = c3(B3, t), c3(gs, t)
            t1 = tt(x_, b.ap, r3, ALU.mult, [tk_, tok["rg", t]])
            b.free = [t1]
            t2 = act(g, x_, ACT.Tanh, [t1, tq], scale=0.5)
            t1 = stt(g, g, 1.0, x_, ALU.add, ALU.mult, [t2])
            tgs.append(ts(g, g, 0.5, w=[t1]))
        a3g = []
        for t in range(3):
            b, tk_ = tile2(AG + P * t)
            g, a_, u = c3(G3, t), c3(A3, t), c3(U3, t)
            t0 = tok["rg", t]
            tz = tt(g, b.ap, r3, ALU.mult, [tk_, t0])
            b.free = [tz]
            t1 = act(a_, g, ACT.Square, [tz, t0])
            t1 = ts(a_, a_, 0.044715, 1.0, ALU.mult, ALU.add, [t1])
            t1 = tt(a_, a_, g, ALU.mult, [t1])
            t1 = act(a_, a_, ACT.Tanh, [t1], scale=0.7978845608028654)
            t1 = stt(g, a_, 1.0, g, ALU.add, ALU.mult, [t1])
            t1 = stt(u, u, 0.5, g, ALU.mult, ALU.mult, [t1])
            a3g.append(t1)
        while heads_bg:
            tick()
        win2_free = []
        hfree = [PE.last]
        rgh = [at(f"rgh{t}", [P, T], F32R, place["A3"] + 4 * T * t) for t in range(3)]
        rgl = [at(f"rgl{t}", [P, T], F32R, place["B3"] + 4 * T * t) for t in range(3)]
        hgh = [at(f"hgh{t}", [P, T], F32R, place["E0"] + 4 * T * t) for t in range(3)]
        hgl = [at(f"hgl{t}", [P, T], F32R, place["E1"] + 4 * T * t) for t in range(3)]
        mixh = {k: m[:, :] for k, m in zip((0, 1, 2, 3, 4, 5, 6, 7), [*rgh, *hgh, *sch])}
        mixl = {k: m[:, :] for k, m in zip((0, 1, 2, 3, 4, 5, 6, 7), [*rgl, *hgl, *scl])}

        def head_norms(items):
            tables(LNEXP)
            tq_ = {}
            for k, src, dst, sq, t, gate in items:
                tq_[k] = act(sq, src, ACT.Square, [t, hfree])
            yield
            for k, src, dst, sq, t, gate in items:
                bank = x4.next()
                tm_ = mm(bank.ap, bdones, sq, w=[tq_[k], bank.free], inc=True)
                t1 = act(sq, bank.ap, ACT.Ln, [tm_], bias=eps6, scale=1.0 / 64)
                bank.free = [t1]
                t1 = act(sq, sq, ACT.Exp, [t1], scale=-0.5)
                t1 = stt(dst, src, v("mix_gain", k), sq, ALU.mult, ALU.mult, [t1, t, hfree])
                if gate is not None:
                    t1 = tt(dst, dst, gate, ALU.mult, [t1, tgs])
                ytok[k] = split(dst, mixh[k], mixl[k], [t1, hfree, t], DV if k in (3, 4, 5) else PO)
                yield

        heads_bg.append(head_norms([(3 + p, ob[p].ap, c3(k3, p), c3(g64, p), tok["ho", p], c3(gs, p))
                                    for p in range(3)]))
        heads_bg.append(head_norms([(t, c3(U3, t), c3(U3, t), c3(G3, t), a3g[t], None) for t in range(3)]))
        for t in range(2):
            b, tk_ = tile2(CB + P * t)
            y = scy[t]
            t1 = tt(y, b.ap, y, ALU.mult, [tk_, cz[t]])
            b.free = [t1]
            heads_bg.append(head_norms([(6 + t, y, y, scc[t], t1, None)]))
        win2_free = [PE.last]

        def wout(b, d, ks, first, last, between=None):
            return proj(b.ap, "wout", P * d, mixh, mixl, ytok, b.free, ks, first=first, last=last, between=between)

        while len(heads_bg) > 2 or not all(k in ytok for k in (0, 1, 2, 3, 4, 5)):
            tick()
        wb = [m3.next() for _ in range(3)]
        for p in range(3):
            wout(wb[p], p, WK[:NW], True, False, tick)
        while heads_bg:
            tick()
        mix_free = [AC.last, DV.last, PO.last]

        main = Ring(pb)
        main.bufs = [*m3.bufs, *x5.bufs]

        def norm_stats(sqbufs, accb, rst, w0):
            state = {"t": None}

            def add(k, src, t):
                o = Buf(accb) if k == 0 else sqbufs.next()
                t1 = act(o.ap, src, ACT.Square, [t, o.free, *w0])
                if k:
                    t1 = tt(accb, accb, o.ap, ALU.add, [t1, state["t"]])
                    o.free = [t1]
                state["t"] = t1

            def end(bank):
                tables(LNEXP)
                t = mm(bank.ap, ones, accb, w=[state["t"], bank.free], inc=True)
                t = act(rst, bank.ap, ACT.Ln, [t, *w0], bias=eps6, scale=1.0 / 1024)
                bank.free = [t]
                return act(rst, rst, ACT.Exp, [t], scale=-0.5)

            return add, end

        rff = at("rff", [P, T], F32, 227264)[:, :]
        add, end = norm_stats(Ring([c3(g512, 0), c3(g512, 1)]), c3(g512, 2), rff, [mix_free, hfree])
        tx1 = []
        htok = []
        for d in range(8):
            b = wb[d] if d < 3 else main.next()
            t = wout(b, d, WK[NW:] if d < 3 else WK, d >= 3, True)
            if d == 2:
                main.i = 3
            t = tt(xk(d), b.ap, xk(d), ALU.add, [t, txb[d]])
            b.free = [t]
            tx1.append(t)
            htok.append(gain_split(xk(d), v("ffn_norm", d), hh[d], hl[d], [t, win2_free]))
            add(d, xk(d), t)
        fence2 = [AC.last, DV.last, PO.last, PE.last]

        a3 = Area(arena + 4 * KD * T)
        FH = [a3(f"fh{j}", T, F32R) for j in range(NPAIR)]
        FL = [a3(f"fl{j}", T, F32R) for j in range(NPAIR)]
        ffn_work = a3.p
        zf = [a3(f"zf{i}", T + 16) for i in range(4)]
        CVr = Ring([a3(f"cv{i}", T) for i in range(6)])
        assert a3.p <= 227264
        for b in CVr.bufs:
            b.free = fence2
        tzf = [DV(lambda e, z=z: e.memset(z[:, 0:16], 0.0), fence2) for z in zf]
        zfr = Ring(zf)
        for b in zfr.bufs:
            b.free = [tzf]
        ftok = []

        def conv_tile(col, cwi):
            b = main.next()
            t = proj(b.ap, "ffn_up", col, hh, hl, htok, b.free)
            z, o = zfr.next(), CVr.next()
            if cwi == 0:
                tok["ffn"] = end(main.next())
            tz = tt(z.ap[:, 16:16 + T], b.ap, rff, ALU.mult, w=[t, z.free, tok["ffn"]])
            cw = VEC["ffn_cw"][0] + 3 * cwi
            t = ts(o.ap, z.ap[:, 16:16 + T], VECS[:, cw + 2:cw + 3], w=[tz, o.free])
            b.free = [tz]
            for j in range(2):
                t = stt(o.ap, z.ap[:, 14 + j:14 + j + T], VECS[:, cw + j:cw + j + 1], o.ap, ALU.mult, ALU.add,
                        [t, tz])
            z.free = [t]
            return o, t

        for j in range(NPAIR):
            g, tg_ = conv_tile(P * j, j)
            th = CVr.next()
            t1 = act(th.ap, g.ap, ACT.Tanh, [tg_, th.free], scale=0.5)
            t1 = stt(g.ap, th.ap, 1.0, g.ap, ALU.add, ALU.mult, [t1])
            th.free = [t1]
            u, tu_ = conv_tile(2816 + P * j, NPAIR + j)
            t1 = stt(u.ap, u.ap, 0.5, g.ap, ALU.mult, ALU.mult, [tu_, t1])
            g.free = [t1]
            sp = split(u.ap, FH[j][:, :], FL[j][:, :], [t1, fence2])
            u.free = sp
            ftok.append(sp)
        up_done = [AC.last, DV.last, PO.last, PE.last]
        PR = at("PR", [P, 2 * T], F32, ffn_work)
        PH = at("PH", [P, 2 * T], F32R, ffn_work + 8 * T)
        PL = at("PL", [P, 2 * T], F32R, ffn_work + 16 * T)
        s_p = sem("s_p")
        tp_ = dma(SP, PR[:, :].rearrange("p (k t) -> p k t", k=2), pT.rearrange("(k p) t -> p k t", p=P), s_p,
                  up_done)
        psp = split(PR[:, :], PH[:, :], PL[:, :], [tp_, up_done], DV)
        tx2 = []
        gtok = []
        for d in range(8):
            b = main.next()
            for k0 in range(0, NPAIR, 8):
                n = min(8, NPAIR - k0)
                for k in range(k0, k0 + n):
                    hi, lo, parts, e_ = ws.take(("ffn_dn", k, P * d))
                    mm(b.ap, hi, FH[k][:, :], start=k == 0, stop=False, w=[b.free, parts[0], ftok[k]])
                    mm(b.ap, hi, FL[k][:, :], start=False, stop=False)
                    t = mm(b.ap, lo, FH[k][:, :], start=False, stop=k == NPAIR - 1, w=[parts[1]],
                           inc=e_ or k == NPAIR - 1)
                    if e_:
                        ws.done[ws.u] = t
            t = tt(xk(d), b.ap, xk(d), ALU.add, [t, tx1[d]])
            b.free = [t]
            tx2.append(t)
            gtok.append(split(xk(d), hh[d], hl[d], [t, up_done]))
        dn_free = [PE.last]
        a4 = Area(arena + 4 * KD * T)
        PP = [a4(f"pp{d}", T) for d in range(8)]
        t4r = Ring([a4(f"t4{i}", T) for i in range(4)])
        sq4 = Ring([a4(f"sq4{i}", T) for i in range(2)])
        acc4, rs4 = a4("acc4", T)[:, :], a4("rs4", T)[:, :]
        tpp = []
        ph = [c3(PH, k) for k in range(2)]
        pl = [c3(PL, k) for k in range(2)]
        for d in range(8):
            b = main.next()
            t = proj(b.ap, "ple_p", P * d, ph, pl, [psp, psp], b.free, range(2))
            t = act(PP[d][:, :], b.ap, w=[t, dn_free])
            b.free = [t]
            tpp.append(t)
        add, end = norm_stats(sq4, acc4, rs4, [dn_free])
        tx3 = []
        for d in range(8):
            b = main.next()
            t = proj(b.ap, "ple_g", P * d, hh, hl, gtok, b.free)
            x_ = t4r.next()
            t1 = act(x_.ap, b.ap, ACT.Tanh, [t, x_.free, dn_free], scale=0.5)
            b.free = [t1]
            t1 = stt(x_.ap, x_.ap, 1.0, PP[d][:, :], ALU.add, ALU.mult, [t1, tpp[d]])
            t1 = stt(xk(d), x_.ap, 0.5, xk(d), ALU.mult, ALU.add, [t1, tx2[d], gtok[d]])
            x_.free = [t1]
            add(d, xk(d), t1)
            tx3.append(act(PP[d][:, :], xk(d), w=[t1], scale=v("final2", d)))
        trs = end(main.next())
        s_o = [sem(f"s_o{i}") for i in range(2)]
        ends = {}
        for d in range(8):
            t = tt(PP[d][:, :], PP[d][:, :], rs4, ALU.mult, [trs, tx3[d]], PO if d in (2, 5) else DV)
            ends[d % 2] = dma((SP, AC)[d % 2], out[P * d:P * d + P, :], PP[d][:, :], s_o[d % 2], [t])
        SP.wait(list(ends.values()))
        assert ws.u == len(units) - 1 and ws.b == len(units[-1])

        block = ctx.enter_context(nc.Block())

        @block.sync
        def _(eng):
            SP.replay(eng)

        @block.scalar
        def _(eng):
            AC.replay(eng)

        @block.vector
        def _(eng):
            DV.replay(eng)

        @block.gpsimd
        def _(eng):
            PO.replay(eng)

        @block.tensor
        def _(eng):
            PE.replay(eng)


def constants():
    p = np.arange(P)[:, None]
    c = np.arange(T)[None, :]
    ident = np.eye(P, dtype=np.float32)
    ones = np.ones((P, P), np.float32)
    bd = np.kron(np.eye(2), np.ones((64, 64))).astype(np.float32)
    mask = np.where(p >= np.arange(P)[None, :], 0.0, NEG).astype(np.float32)
    da = np.where(p - (c - 384) >= 0, -(p - (c - 384)), NEG).astype(np.float32)
    cb = np.arange(256)[None, :]
    dist = p - cb + P
    db = np.where((dist >= 0) & (dist < P), -dist, NEG).astype(np.float32)
    m64 = np.broadcast_to((np.arange(T) % 64 != 0).astype(np.float32), (P, T))
    cst = np.concatenate([ident, ones, bd, mask, da, db, m64], 1).astype(np.float32)
    s = np.arange(P)[:, None]
    u8 = []
    for h in LEVELS:
        t = np.arange(P).reshape(-1, 2, h)[:, 1, :].ravel()[None, :]
        m = (s // (2 * h) == t // (2 * h)) & (s % (2 * h) < h)
        u8.append(np.tile(m, (1, 4)))
    t = np.arange(P)[None, :]
    u8.append(np.tile((s // 4 == t // 4) & (s <= t), (1, 4)))
    return np.ascontiguousarray(cst), np.ascontiguousarray(np.concatenate(u8, 1).astype(np.float32))


def kernel(**inputs):
    import numpy as _np
    import concourse.bacc as _bacc
    from concourse import mybir as _mybir
    from concourse.bass_utils import run_bass_kernel_spmd as _run

    g = {k: _np.asarray(a) for k, a in inputs.items()}
    heads = [h for t in range(4) for h in (t, t + 4)]
    perm = _np.concatenate([_np.arange(64 * h, 64 * h + 64) for h in heads])
    win = g["w_in"][0].copy()
    win[:, QB:QB + 512] = g["w_in"][0][:, QB + perm]
    win[:, GB:GB + 512] = g["w_in"][0][:, GB + perm]
    mats = {"win": win, "up_a": g["w_up_a"][0], "up_b": g["w_up_b"][0][perm], "up_c": g["w_up_c"][0],
            "wo": g["w_o"][0], "win2": g["w_in_2"][0], "wout": g["w_out_2"][0], "ffn_up": g["ffn_w_up_2"][0],
            "ffn_dn": g["ffn_w_down_2"][0], "ple_p": g["ple_w_proj_2"][0], "ple_g": g["ple_w_gate_2"][0]}
    wall = _np.concatenate([mats[n][P * k:P * k + P, c:c + w] for u in plan_units() for n, k, c, w in u], 1)

    def cols(a):
        return a.reshape(-1, P).T

    def rep(a):
        return _np.tile(a.reshape(1, -1), (P, 1))

    bf = _np.tile(g["b_forget"][0], P // 8).reshape(P, 1)
    cwr = g["rg_conv_w_2"][0].reshape(4, 3, P).transpose(2, 1, 0).reshape(P, 12)
    cws = g["sc_conv_w_2"][0].reshape(3, 2, P).transpose(2, 1, 0).reshape(P, 6)
    cwf = g["ffn_conv_w_2"][0].reshape(3, 44, P).transpose(2, 1, 0).reshape(P, 132)
    vec = _np.concatenate([
        cols(g["norm_gain"][0]), cols(g["final_gain"]), cols(g["norm_mix_gain_2"][0]), cols(g["subln_gain"][0]),
        rep(g["sinks"][0]), bf, rep(g["lambda_q1"][0]), rep(g["lambda_k1"][0]), rep(g["lambda_q2"][0]),
        rep(g["lambda_k2"][0]), cwr, cols(g["rg_conv_b_2"][0]), cols(g["rg_b_r_2"][0].ravel()),
        cols(g["rg_b_i_2"][0].ravel()), cols(g["rg_lambda_2"][0]), cols(g["hg_lower_bounds_2"][0]), cws,
        cols(g["mix_out_gain_2"][0]), cols(g["norm_ffn_gain_2"][0]), cwf, cols(g["final_norm_gain_2"])], 1)
    rgw = _np.zeros((P, 6 * P), _np.float32)
    for t in range(3):
        for j, n in enumerate(("rg_w_r_2", "rg_w_i_2")):
            for s in range(2):
                o = P * (2 * t + j) + 64 * s
                rgw[64 * s:64 * s + 64, o:o + 64] = g[n][0, 2 * t + s]
    cst, cu8 = constants()
    arrays = {"wall": wall, "xT": g["x"][0].T, "pT": g["p_2"][0, 0].T, "vec": vec, "cst": cst, "cu8": cu8,
              "rgw": rgw}
    nc = _bacc.Bacc("TRN2", target_bir_lowering=False, num_devices=1)
    aps = []
    for n, a in arrays.items():
        arrays[n] = _np.ascontiguousarray(a)
        aps.append(nc.dram_tensor(f"in_{n}", a.shape, _mybir.dt.from_np(a.dtype), kind="ExternalInput").ap())
    out = nc.dram_tensor("outT", (1024, T), _mybir.dt.float32, kind="ExternalOutput").ap()
    build(nc, *aps, out)
    r = _run(nc, [{f"in_{n}": a for n, a in arrays.items()}], core_ids=[0])
    return r.results[0]["outT"].T.reshape(1, T, 1024)
```

```python
import math
from contextlib import ExitStack

import numpy as np

import concourse.bass as bass
from concourse import mybir

F32 = mybir.dt.float32
F32R = mybir.dt.float32r
U8 = mybir.dt.uint8
ALU = mybir.AluOpType
ACT = mybir.ActivationFunctionType
AXX = mybir.AxisListType.X

P = 128
T = 512
KD = 8
BLK = 4
NEG = -1.0e30
LOWEST = -3.0e38
LEVELS = [4, 8, 16, 32]
MASKS = len(LEVELS) * 128 + 512
MIDDLE = 21.84
DEEP = 3
WK = [3, 4, 5, 0, 1, 2, 6, 7]
NPAIR = 22

QA, KA, VA, GA, QB, KB, VB, GB, QC, KC, VC, FC, GC, GM = (
    0, 512, 1024, 1536, 2048, 2560, 2688, 2816, 3328, 3840, 4352, 4864, 4872, 5384)
AU, AG, BQ, BF, BV, BG, CB, CC, CV = 0, 384, 768, 1152, 1536, 1920, 2304, 2560, 2816

VEC = {}


def _vec_table():
    at = 0
    for name, n in [("norm_gain", 8), ("final_gain", 8), ("mix_norm", 8), ("subln", 1), ("sinks", 8),
                    ("b_forget", 1), ("lam_vec", 256), ("rg_cw", 12), ("rg_cb", 3), ("rg_br", 3), ("rg_bi", 3),
                    ("rg_lam", 3), ("hg_lb", 3), ("sc_cw", 6), ("mix_gain", 8), ("ffn_norm", 8), ("ffn_cw", 132),
                    ("final2", 8)]:
        VEC[name] = (at, n)
        at += n
    return at


NVEC = _vec_table()


def plan_units():
    units = []

    def fm(name, col, width=P, nk=KD):
        units.append([(name, k, col, width) for k in range(nk)])

    def tm(name, col, nb):
        for k in range(KD):
            units.append([(name, k, col + P * e, P) for e in range(nb)])

    tm("win", KC, 4)
    for t in range(2):
        fm("win", QC + P * t)
    for k in range(KD):
        units.append([("win", k, VC + P * e, P) for e in range(4)] + [("win", k, FC, 8)])
    for t in range(2, 4):
        fm("win", QC + P * t)
    for c in (KA, QA):
        for t in range(4):
            fm("win", c + P * t)
    tm("win", VA, 4)
    fm("win", KB)
    fm("win", VB)
    for t in range(4):
        fm("win", QB + P * t)
    for t in range(4):
        fm("win", GC + P * t)
    for d in range(3):
        for j in range(3):
            fm("win", GM + 1024 * j + P * d)
    for c in (GA, GB):
        for t in range(4):
            fm("win", c + P * t)
    for d in range(8):
        if d >= 3:
            for j in range(3):
                fm("win", GM + 1024 * j + P * d)
        units.append([(n, k, P * d, P) for n in ("up_c", "up_a") for k in range(4)])
        units.append([("up_b", k, P * d, P) for k in range(4)])
    for d in range(2):
        fm("wo", P * d, nk=7)
    units.append([("wo", 7, P * d, P) for d in range(2)])
    for d in range(2, 8):
        fm("wo", P * d)
    for c in (BF, BQ):
        for t in range(3):
            fm("win2", c + P * t)
    tm("win2", BV, 3)
    for c, n in ((AU, 3), (CC, 2), (CV, 2), (BG, 3), (AG, 3), (CB, 2)):
        for t in range(n):
            fm("win2", c + P * t)
    for ks in (WK[:3], WK[3:6], WK[6:]):
        for d in range(3):
            units.append([("wout", k, P * d, P) for k in ks])
    for d in range(3, 8):
        units.append([("wout", k, P * d, P) for k in WK])
    for j in range(NPAIR):
        fm("ffn_up", P * j)
        fm("ffn_up", 2816 + P * j)
    for d in range(8):
        for k in range(0, NPAIR, 8):
            units.append([("ffn_dn", kk, P * d, P) for kk in range(k, min(k + 8, NPAIR))])
    units.append([("ple_p", k, P * d, P) for d in range(4) for k in range(2)])
    units.append([("ple_p", k, P * d, P) for d in range(4, 8) for k in range(2)])
    for d in range(8):
        fm("ple_g", P * d)
    return [u[i:i + n] for u in units for n in [len(u) if u[-1][3] < P else BLK] for i in range(0, len(u), n)]


class Queue:

    def __init__(self, sem):
        self.sem, self.n, self.items, self.seen = sem, 0, [], {}

    def wait(self, toks):
        for tok in toks:
            if isinstance(tok, list):
                self.wait(tok)
            elif tok is not None and self.seen.get(tok[0].name, 0) < tok[1]:
                self.seen[tok[0].name] = tok[1]
                self.items.append(tok)

    def __call__(self, fn, toks=(), inc=True):
        self.wait(toks)
        self.n += inc
        self.items.append((fn, inc))
        return (self.sem, self.n)

    @property
    def last(self):
        return (self.sem, self.n)

    def replay(self, eng):
        for a, b in self.items:
            if callable(a):
                ins = a(eng)
                if b is True:
                    ins.then_inc(self.sem, 1)
                elif b:
                    ins.then_inc(b, 16)
            else:
                eng.wait_ge(a, b)


class Buf:

    def __init__(self, ap):
        self.ap, self.free = ap, []


class Ring:
    def __init__(self, aps):
        self.bufs, self.i = [Buf(a[:, :]) for a in aps], 0

    def next(self):
        b = self.bufs[self.i % len(self.bufs)]
        self.i += 1
        return b


def build(nc, wall, xT, pT, vec, cst, cu8, rgw, out):
    units = plan_units()
    with ExitStack() as ctx:
        base = 16512
        place = {}

        def at(name, shape, dt, off):
            return nc.alloc_sbuf_tensor_at(name, shape, dt, offset=off)

        class Area:
            def __init__(self, start):
                self.p = start

            def __call__(self, name, cols, dt=F32, size=4):
                t = at(name, [P, cols], dt, self.p)
                place[name] = self.p
                self.p += (cols * size + 63) // 64 * 64
                assert self.p <= 229368, (name, self.p)
                return t

        NR, NS = 5, 6
        LOOK = 5
        ar = Area(base)
        raw = [ar(f"raw{i}", BLK * P + 8) for i in range(NR)]
        whi = [ar(f"whi{i}", BLK * P + 8, F32R) for i in range(NS)]
        wlo = [ar(f"wlo{i}", BLK * P + 8, F32R) for i in range(NS)]
        CST = ar("cst", 128 * 4 + 512 + 256 + 512)
        CU8 = ar("cu8", MASKS, U8, 1)
        VECS = ar("vecs", NVEC)
        SM = ar("sm", 96)
        HH = ar("HH", KD * T, F32R)
        HL = ar("HL", KD * T, F32R)
        arena = ar.p
        ident = CST[:, 0:128]
        ones = CST[:, 128:256]
        bdones = CST[:, 256:384]
        maskC = CST[:, 384:512]
        DA = CST[:, 512:1024]
        DB = CST[:, 1024:1280]
        m64 = CST[:, 1280:1792]

        def lvmask(l):
            return CU8[:, 128 * l:128 * l + 128]

        b4mask = CU8[:, 128 * len(LEVELS):MASKS]

        def v(name, i=0, n=1):
            o = VEC[name][0] + i
            return VECS[:, o:o + n]

        pb = [ctx.enter_context(nc.psum_tensor(f"pb{i}", [P, T], F32)) for i in range(8)]

        def sem(name):
            return ctx.enter_context(nc.semaphore(name))

        PE, AC, DV, PO, SP = (Queue(sem(n)) for n in ("s_pe", "s_ac", "s_dv", "s_po", "s_sp"))

        def act(o, i, f=ACT.Copy, w=(), bias=None, scale=1.0, accum=None):
            kw = {}
            if bias is not None:
                kw["bias"] = bias
            if accum is not None:
                kw["accum_out"] = accum
            return AC(lambda e: e.activation(o, i, f, scale=scale, **kw), w)

        def tables(name):
            AC(lambda e: e.preload_act_table_set(name), inc=False)

        LNEXP, EXPTANH = "natural_log_exp_and_others", "exp_and_others"

        def tt(o, a, b, op, w=(), q=None):
            return (q or DV)(lambda e: e.tensor_tensor(o, a, b, op), w)

        def ts(o, a, s1, s2=None, op0=ALU.mult, op1=None, w=(), q=None):
            if op1 is None:
                return (q or DV)(lambda e: e.tensor_scalar(o, a, s1, None, op0), w)
            return (q or DV)(lambda e: e.tensor_scalar(o, a, s1, s2, op0, op1), w)

        def stt(o, a, s, b, op0, op1, w=()):
            return DV(lambda e: e.scalar_tensor_tensor(out=o, in0=a, scalar=s, in1=b, op0=op0, op1=op1), w)

        def addmax(o, a, b, mx, w=()):
            return DV(lambda e: e.tensor_tensor_reduce(o, a, b, 1.0, LOWEST, ALU.add, ALU.max, mx), w)

        def recip(o, a, w=()):
            return DV(lambda e: e.reciprocal(o, a), w)

        def vcopy(o, a, w=(), q=None):
            return (q or DV)(lambda e: e.tensor_copy(o, a), w)

        def scan(o, d0, d1, w=()):
            return DV(lambda e: e.tensor_tensor_scan(o, d0, d1, 0.0, ALU.mult, ALU.add), w)

        def mm(o, l, r, start=True, stop=True, w=(), inc=False, skip=False):
            return PE(lambda e: e.matmul(o, l, r, start=start, stop=stop, skip_group_check=skip), w, inc)

        def tp(o, i, w=(), inc=False):
            return PE(lambda e: e.transpose(o, i, ident), w, inc)

        dma_n = {}

        def dma(q, o, i, s, w=()):
            q.wait(w)
            q.items.append((lambda e: e.dma_start(o, i), s))
            dma_n[s.name] = dma_n.get(s.name, 0) + 16
            return (s, dma_n[s.name])

        def split(src, hi, lo, w, q=None):
            a = act(hi, src, w=w)
            b = tt(lo, src, hi.bitcast(F32), ALU.subtract, [a, *w], q or PO)
            return [a, b]

        def gain_split(src, gain, hi, lo, w):
            a = act(hi, src, w=w, scale=gain)
            b = stt(lo, src, gain, hi.bitcast(F32), ALU.mult, ALU.subtract, [a, *w])
            return [a, b]

        s_raw = [sem(f"s_raw{i}") for i in range(NR)]
        offs = np.concatenate([[0], np.cumsum([sum(b[3] for b in u) for u in units])])

        class Stream:
            def __init__(self):
                self.loaded, self.done, self.parts = {}, {}, {}
                self.u, self.b, self.next_split = -1, 0, 0

            def load(self, u):
                if u < len(units):
                    n = int(offs[u + 1] - offs[u])
                    self.loaded[u] = dma(SP, raw[u % NR][:, 0:n], wall[:, int(offs[u]):int(offs[u + 1])],
                                         s_raw[u % NR], [self.parts.get(u - NR)])

            def prepare(self, upto):
                while self.next_split <= min(upto, len(units) - 1):
                    u = self.next_split
                    n = int(offs[u + 1] - offs[u])
                    self.parts[u] = split(raw[u % NR][:, 0:n], whi[u % NS][:, 0:n], wlo[u % NS][:, 0:n],
                                          [self.loaded[u], self.done.get(u - NS)])
                    self.load(u + NR)
                    self.next_split += 1

            def take(self, want, n=1):
                if self.u < 0 or self.b == len(units[self.u]):
                    self.u, self.b = self.u + 1, 0
                    self.prepare(self.u + LOOK)
                u = units[self.u]
                assert u[self.b][:3] == want, (u[self.b], want)
                o = sum(b[3] for b in u[:self.b])
                self.b += n
                e = sum(b[3] for b in u[:self.b])
                return whi[self.u % NS][:, o:e], wlo[self.u % NS][:, o:e], self.parts[self.u], self.b == len(u)

        ws = Stream()

        def proj(o, name, col, xh, xl, xtok, free, ks=range(KD), width=P, first=True, last=True, between=None):
            for i, k in enumerate(ks):
                hi, lo, parts, end = ws.take((name, k, col))
                hi, lo = hi[:, 0:width], lo[:, 0:width]
                mm(o, hi, xh[k], start=first and i == 0, stop=False, w=[free, parts[0], xtok[k]])
                mm(o, hi, xl[k], start=False, stop=False)
                t = mm(o, lo, xh[k], start=False, stop=last and i == len(ks) - 1, w=[parts[1]],
                       inc=end or i == len(ks) - 1)
                if end:
                    ws.done[ws.u] = t
                if between:
                    between(i)
            return t

        def proj_tokens(os, name, col, nb, xh, xl, xtok, between=None):
            toks = [None] * 4
            for k in range(KD):
                hi, lo, parts, end = ws.take((name, k, col), nb)
                for m in range(4):
                    xs = slice(P * m, P * m + P)
                    o = os[m].ap[:, 0:nb * P]
                    mm(o, xh[k][:, xs], hi, start=k == 0, stop=False, w=[os[m].free, parts, xtok[k]])
                    mm(o, xh[k][:, xs], lo, start=False, stop=False)
                    toks[m] = mm(o, xl[k][:, xs], hi, start=False, stop=k == KD - 1, inc=True)
                if end:
                    ws.done[ws.u] = toks[3]
                if between:
                    between(k)
            return toks

        s_c = [sem(f"s_c{i}") for i in range(4)]
        s_x = [sem(f"s_x{i}") for i in range(KD)]
        X = at("X", [P, KD * T], F32, arena)

        def xk(k):
            return X[:, T * k:T * k + T]

        tgain = dma(AC, VECS[:, 0:KD], vec[:, 0:KD], s_c[3])
        tables(LNEXP)
        xtok0 = []
        for k in range(KD):
            xtok0.append(dma(SP, xk(k), xT[P * k:P * k + P, :], s_x[k]))
            if k < NR:
                ws.load(k)
        tvec = dma(SP, VECS[:, KD:NVEC], vec[:, KD:NVEC], s_c[0])
        tcst = dma(SP, CST[:, :], cst, s_c[1])
        eps6 = SM[:, 0:1]
        eps5 = SM[:, 1:2]
        one = SM[:, 2:3]
        teps = [DV(lambda e: e.memset(eps6, 1e-6)), DV(lambda e: e.memset(eps5, 1e-5)),
                DV(lambda e: e.memset(one, 1.0))]

        hh = [HH[:, T * k:T * k + T] for k in range(KD)]
        hl = [HL[:, T * k:T * k + T] for k in range(KD)]

        main = Ring([b[:, :] for b in pb[0:4]])
        S = Ring([b[:, :] for b in pb[4:7]])
        TB = S
        YB = Ring([pb[7][:, :]])

        attention_banks = [*S.bufs, *YB.bufs]

        a1 = Area(arena)
        qA = [a1(f"qA{t}", T) for t in range(4)]
        kA = [a1(f"kA{t}", T) for t in range(4)]
        vA = [a1(f"vA{m}", T) for m in range(4)]
        qC = [a1(f"qC{t}", T) for t in range(4)]
        kC = [a1(f"kC{t}", T) for t in range(4)]
        vC = [a1(f"vC{m}", T) for m in range(4)]
        qB = [a1(f"qB{t}", T) for t in range(4)]
        kB = a1("kB", T)
        vB = a1("vB", T)
        exB = [a1(f"exB{t}", T, F32R) for t in range(4)]
        GMs = [a1(f"gms{i}", T) for i in range(9)]
        work0 = a1.p
        Pr = Ring([a1(f"P{i}", T) for i in range(6)])
        PTr = Ring([a1(f"PT{i}", T) for i in range(3)])
        Br = Ring([a1(f"B{i}", T) for i in range(2)])
        Nr = Ring([a1(f"N{i}", T) for i in range(4)])
        s_cw, s_n = sem("s_cw"), [sem(f"s_n{i}") for i in range(4)]
        Wr = Ring([a1(f"W{i}", T) for i in range(3)])
        STt = a1("stat", 8 * 8)
        Sr = Ring([STt[:, 8 * i:8 * i + 8] for i in range(8)])
        CQ = a1("CQ", 32)
        THr = Ring([a1(f"th{i}", T) for i in range(3)])
        cT = a1("cT", T)
        assert a1.p <= 229368
        MH = at("MH", [P, KD * T], F32R, work0)
        ML = at("ML", [P, KD * T], F32R, work0 + 4 * KD * T)
        mh = [MH[:, T * k:T * k + T] for k in range(KD)]
        ml = [ML[:, T * k:T * k + T] for k in range(KD)]
        assert work0 + 8 * KD * T <= place["stat"]

        MF = at("maskf", [P, MASKS], F32, place["gms4"])

        rst, rst8, rcol = qB[3][:, :], qB[2][:, :], SM[:, 56:60]
        acc, *sqs = (at(f"sq0{i}", [P, T], F32, place[f"exB{i}"])[:, :] for i in range(3))
        sqb = Ring(sqs)
        ptok = []
        tacc = None
        for k in range(KD):
            b = sqb.next() if k else Buf(acc)
            ptok.append(gain_split(xk(k), v("norm_gain", k), mh[k], ml[k], [xtok0[k], tgain]))
            if k <= LOOK:
                ws.prepare(k)
            t = tt(b.ap, xk(k), xk(k), ALU.mult, [xtok0[k], b.free])
            if k:
                tacc = tt(acc, acc, b.ap, ALU.add, [t, tacc])
                b.free = [tacc]
            else:
                tacc = t
        htok = []

        def first_norm():
            bank = TB.next()
            tables(LNEXP)
            t = mm(bank.ap, ones, acc, w=[tacc, tcst], inc=True)
            t = act(rst, bank.ap, ACT.Ln, [t, teps], bias=eps6, scale=1.0 / 1024)
            bank.free = [t]
            t = act(rst, rst, ACT.Exp, [t], scale=-0.5)
            t8 = ts(rst8, rst, 0.125, w=[t])
            return t, t8

        def norm_columns():
            bank = TB.next()
            for m in range(4):
                tm_ = mm(bank.ap[:, m:m + 1], rst[0:1, P * m:P * m + P], ones[0:1, 0:1], w=[trst, bank.free],
                         inc=m == 3)
            tc = vcopy(rcol, bank.ap[:, 0:4], [tm_])
            bank.free = [tc]
            return tc

        tmp = Ring([b.ap for b in sqb.bufs])

        def first_normed(ks):
            for k in ks:
                b = tmp.next()
                t1 = stt(b.ap, xk(k), v("norm_gain", k), rst, ALU.mult, ALU.mult, [trst, tacc, b.free])
                sp = split(b.ap, hh[k], hl[k], [t1])
                b.free = sp
                htok.append(sp)
            return [AC.last, DV.last, PO.last]

        background = []

        def step(n=1):
            for _ in range(n):
                while background:
                    try:
                        next(background[0])
                        break
                    except StopIteration:
                        background.pop(0)

        def drain_background():
            while background:
                step()

        def pipeline(us):
            n = len(us)
            us[0].pre()
            for i in range(n + DEEP + 3):
                if 0 <= i - DEEP < n:
                    us[i - DEEP].turn()
                if i + 1 < n:
                    us[i + 1].pre()
                if i < n:
                    us[i].scores()
                if 0 <= i - 1 < n:
                    us[i - 1].normal()
                if 0 <= i - DEEP - 1 < n:
                    us[i - DEEP - 1].values()
                if 0 <= i - DEEP - 3 < n:
                    us[i - DEEP - 3].late()
                yield

        class Unit:

            def pre(self):
                pass

            def late(self):
                pass

            def softmax(self, bank, tscore, bias, tbias, width, col, sink=None):
                st, p = self.st, Pr.next()
                t = addmax(p.ap[:, 0:width], bank.ap[:, 0:width], bias, st.ap[:, col:col + 1],
                           [tscore, tbias, p.free, st.free if col == 0 else None])
                bank.free = [t]
                self.addt = t
                nm = st.ap[:, col + 1:col + 2]
                if sink is None:
                    t = ts(nm, st.ap[:, col:col + 1], -1.0, w=[t])
                else:
                    t = ts(nm, st.ap[:, col:col + 1], sink, -1.0, ALU.max, ALU.mult, [t])
                t2 = act(p.ap[:, 0:width], p.ap[:, 0:width], ACT.Exp, [t], bias=nm,
                         accum=st.ap[:, col + 2:col + 3])
                return p, t2, t

            def turn(self):
                bank, self.pt = TB.next(), PTr.next()
                n = self.width // P
                for j in range(n):
                    t = tp(bank.ap[:, P * j:P * j + P], self.p.ap[:, P * j:P * j + P],
                           [self.tp, bank.free], inc=j == n - 1)
                self.p.free = [t]
                self.tpt = act(self.pt.ap[:, 0:self.width], bank.ap[:, 0:self.width], w=[t, self.pt.free])
                bank.free = [self.tpt]

        def finish_values(us, os, lhs, tv, last):
            n = us[0].width // P
            for j in range(n):
                for u, o, l in zip(us, os, lhs):
                    t = mm(o, l(j), u.pt.ap[:, P * j:P * j + P], start=j == 0, stop=j == n - 1,
                           w=[us[-1].tpt, u.tpt, tv, last], inc=j == n - 1)
            for u in us:
                u.pt.free = [t]
            return t

        tok = {}

        class UnitC(Unit):
            neg = {}

            def __init__(self, h, i):
                self.h, self.i, self.t, self.r = h, i, h // 2, 64 * (h % 2)
                self.width = P * (i + 1)

            def pre(self):
                if self.i == 2 or (self.t == 0 and self.i == 0):
                    h = self.h + 2 * (self.i // 2)
                    if h < 8:
                        nb = Nr.next()
                        UnitC.neg[h] = nb, dma(SP, nb.ap, scratch[h, :].partition_broadcast(P), s_n[(Nr.i - 1) % 4],
                                               [tok["cw"], nb.free])
                self.nb, self.tn = UnitC.neg[self.h]

            def scores(self):
                i, r = self.i, self.r
                bank = S.next()
                ts_ = mm(bank.ap[:, 0:self.width], qC[self.t][r:r + 64, P * i:P * i + P],
                         kC[self.t][r:r + 64, 0:self.width], w=[tok["qC"], tok["kC"], bank.free], inc=True)
                tok["scoreC", self.t] = ts_
                bb = Br.next()
                cq = CQ[:, 8 * i + self.h:8 * i + self.h + 1]
                tb = [stt(bb.ap[:, P * i:P * i + P], self.nb.ap[:, P * i:P * i + P], cq, maskC, ALU.add, ALU.add,
                          [self.tn, tok["cq"], bb.free])]
                if i:
                    tb.append(ts(bb.ap[:, 0:P * i], self.nb.ap[:, 0:P * i], cq, op0=ALU.add))
                self.nb.free = tb
                self.st = Sr.next()
                self.p, self.te, _ = self.softmax(bank, ts_, bb.ap[:, 0:self.width], tb, self.width, 0)
                bb.free = [self.addt]

            def normal(self):
                st = self.st.ap
                t = recip(st[:, 3:4], st[:, 2:3], [self.te])
                self.tp = ts(self.p.ap[:, 0:self.width], self.p.ap[:, 0:self.width], st[:, 3:4], w=[t])
                self.st.free = [self.tp]

            def values(self):
                if self.r == 0:
                    UnitC.pair = self
                    return
                i = self.i
                if i == 0:
                    UnitC.y = YB.next()
                y = UnitC.y
                us = [UnitC.pair, self]
                t = finish_values(us, [y.ap[u.r:u.r + 64, P * i:P * i + P] for u in us],
                                  [lambda j, u=u: vC[j][:, 64 * u.h:64 * u.h + 64] for u in us], tok["vC"], y.free)
                if i == 3:
                    tok["yC", self.t] = vcopy(qC[self.t][:, :], y.ap, [t, tok["scoreC", self.t]])
                    y.free = [tok["yC", self.t]]

        class UnitA(Unit):
            def __init__(self, h, i):
                self.h, self.i = h, i
                self.width = P * (i + 1)

            def pre(self):
                if self.i == 0:
                    UnitA.nb = Br.next()
                    UnitA.tn = ts(UnitA.nb.ap, DA, 2.0 ** (-2 * (self.h + 1)), w=[UnitA.nb.free])
                self.nb, self.tn = UnitA.nb, UnitA.tn

            def scores(self):
                i = self.i
                self.st = Sr.next()
                self.ps, self.tes = [], []
                for m in range(2):
                    r = 64 * m
                    bank = S.next()
                    t = mm(bank.ap[:, 0:self.width], qA[self.h][r:r + 64, P * i:P * i + P],
                           kA[self.h][r:r + 64, 0:self.width], w=[tok["qA"], tok["kA"], bank.free], inc=True)
                    tok["scoreA", self.h] = t
                    p, te, _ = self.softmax(bank, t, self.nb.ap[:, 384 - P * i:512], self.tn, self.width, 4 * m)
                    self.ps.append(p)
                    self.tes.append(te)
                self.nb.free = [self.addt]

            def normal(self):
                st, wd = self.st.ap, self.width
                p0, p1 = self.ps
                a = recip(st[:, 3:4], st[:, 2:3], [self.tes[0]])
                b = recip(st[:, 7:8], st[:, 6:7], [self.tes[1]])
                b = ts(p1.ap[:, 0:wd], p1.ap[:, 0:wd], st[:, 7:8], lam, ALU.mult, ALU.mult, [b, tok["lam"]])
                self.tp = stt(p0.ap[:, 0:wd], p0.ap[:, 0:wd], st[:, 3:4], p1.ap[:, 0:wd], ALU.mult, ALU.subtract,
                              [a, b])
                self.p = p0
                p1.free = [self.tp]
                self.st.free = [self.tp]

            def values(self):
                h, i = self.h, self.i
                if i == 0:
                    UnitA.y = YB.next()
                y = UnitA.y
                t = finish_values([self], [y.ap[:, P * i:P * i + P]], [lambda j: vA[j][:, P * h:P * h + P]],
                                  tok["vA"], y.free)
                if i == 3:
                    dst = qA[h][:, :]
                    t = vcopy(dst, y.ap, [t, tok["scoreA", h]])
                    y.free = [t]
                    self.sq = Wr.next()
                    self.tsq = act(self.sq.ap, dst, ACT.Square, [t, self.sq.free])

            def late(self):
                h = self.h
                if self.i == 3:
                    sq, ts_, dst = self.sq, self.tsq, qA[h][:, :]
                    bank = TB.next()
                    tables(LNEXP)
                    tm_ = mm(bank.ap, ones, sq.ap, w=[ts_, bank.free], inc=True)
                    t2 = act(sq.ap, bank.ap, ACT.Ln, [tm_], bias=eps5, scale=1.0 / 128)
                    bank.free = [t2]
                    t2 = act(sq.ap, sq.ap, ACT.Exp, [t2], scale=-0.5)
                    tok["yA", h] = stt(dst, dst, subg, sq.ap, ALU.mult, ALU.mult, [t2, tok["subg"]])
                    sq.free = [tok["yA", h]]

        class UnitB(Unit):
            def __init__(self, t, s, i):
                self.t, self.r, self.i, self.h = t, 64 * s, i, t + 4 * s
                UnitB.nb = {}
                self.j0 = max(i - 1, 0)
                self.width = P * (i + 1 - self.j0)

            def pre(self):
                if self.i == 0:
                    nb = Br.next()
                    UnitB.nb[self.r] = nb, ts(nb.ap[:, 0:256], DB, 2.0 ** -(self.h + 1), w=[nb.free])
                self.nb, self.tn = UnitB.nb[self.r]

            def scores(self):
                i, r = self.i, self.r
                self.st = Sr.next()
                bank = S.next()
                t = mm(bank.ap[:, 0:self.width], qB[self.t][r:r + 64, P * i:P * i + P],
                       kB[r:r + 64, P * self.j0:P * i + P], w=[tok["qB"], tok["kB"], bank.free], inc=True)
                tok["scoreB", self.t] = t
                self.p, self.te, tm_ = self.softmax(bank, t, self.nb.ap[:, 256 - self.width:256], self.tn,
                                                    self.width, 0, v("sinks", self.h))
                self.nb.free = [self.addt]
                st = self.st.ap
                self.te2 = act(st[:, 4:5], v("sinks", self.h), ACT.Exp, [tm_], bias=st[:, 1:2])

            def normal(self):
                st, wd = self.st.ap, self.width
                t = tt(st[:, 5:6], st[:, 2:3], st[:, 4:5], ALU.add, [self.te, self.te2])
                t = recip(st[:, 3:4], st[:, 5:6], [t])
                self.tp = ts(self.p.ap[:, 0:wd], self.p.ap[:, 0:wd], st[:, 3:4], w=[t])
                self.st.free = [self.tp]

            def values(self):
                if self.r == 0:
                    UnitB.pair = self
                    return
                i = self.i
                if i == 0:
                    UnitB.y = YB.next()
                y = UnitB.y
                us = [UnitB.pair, self]
                t = finish_values(us, [y.ap[u.r:u.r + 64, P * i:P * i + P] for u in us],
                                  [lambda j, u=u: vB[:, P * (u.j0 + j) + u.r:P * (u.j0 + j) + u.r + 64] for u in us],
                                  tok["vB"], y.free)
                if i == 3:
                    tok["yB", self.t] = vcopy(qB[self.t][:, :], y.ap, [t, tok["scoreB", self.t]])
                    y.free = [tok["yB", self.t]]

        def slot(i):
            if i in (2, 5, 7):
                step()

        lam, subg = SM[:, 8:9], SM[:, 9:10]
        lam_init = 0.8 - 0.6 * math.exp(-0.3 * 0)
        lv = VEC["lam_vec"][0]
        scr = THr.bufs[0].ap
        tl = []
        for j in range(2):
            tl.append(DV(lambda e, j=j: e.tensor_tensor_reduce(
                scr[:, 64 * j:64 * j + 64], VECS[:, lv + 128 * j:lv + 128 * j + 64],
                VECS[:, lv + 128 * j + 64:lv + 128 * j + 128], 1.0, 0.0, ALU.mult, ALU.add,
                SM[:, 10 + j:11 + j]), [tvec]))
        t = act(SM[:, 12:14], SM[:, 10:12], ACT.Exp, tl)
        t = tt(SM[:, 14:15], SM[:, 12:13], SM[:, 13:14], ALU.subtract, [t])
        tok["lam"] = ts(lam, SM[:, 14:15], lam_init, op0=ALU.add, w=[t])
        tok["subg"] = ts(subg, v("subln"), 1.0 - lam_init, w=[tvec])

        def fm_tile(col, dst, scale=None, on=None, w=()):
            b = main.next()
            t = proj(b.ap, "win", col, hh, hl, htok, b.free, between=slot)
            if on is DV:
                t = vcopy(dst, b.ap, [t, *w]) if scale is None else ts(dst, b.ap, scale, w=[t, *w])
            else:
                t = act(dst, b.ap, w=[t, *w], scale=scale or 1.0)
            b.free = [t]
            return t

        def first_tile(col, ring=None, between=None):
            b = (ring or main).next()
            return b, proj(b.ap, "win", col, mh, ml, ptok, b.free, between=between)

        bk = [main.next() for _ in range(4)]
        tkc = [None] * 4
        for k in range(KD):
            hi, lo, parts, end = ws.take(("win", k, KC), 4)
            for m in range(4):
                h_, l_ = hi[:, P * m:P * m + P], lo[:, P * m:P * m + P]
                mm(bk[m].ap, h_, mh[k], start=k == 0, stop=False, w=[bk[m].free, parts[0], ptok[k][0]])
                mm(bk[m].ap, h_, ml[k], start=False, stop=False, w=[ptok[k]])
                tkc[m] = mm(bk[m].ap, l_, mh[k], start=False, stop=k == KD - 1, w=[parts[1]], inc=True)
            ws.done[ws.u] = tkc[3]
        trst, trst8 = first_norm()
        for m in range(4):
            tok["kC"] = tt(kC[m][:, :], bk[m].ap, rst, ALU.mult, [tkc[m], trst8])
            bk[m].free = [tok["kC"]]
        def query_tile(t, ring=None, between=None):
            b, tk = first_tile(QC + P * t, ring, between)
            return lambda: queries(t, b, tk)

        def queries(t, b, tk):
            tok["qC"] = tt(qC[t][:, :], b.ap, rst8, ALU.mult, [tk, trst8])
            b.free = [tok["qC"]]

        scratch = nc.dram_tensor("c_sums", (8, T), F32, kind="Internal").ap()

        def forget_sums():
            b = S.next()
            for m in range(4):
                t = mm(b.ap[0:8, P * m:P * m + P], CQ[:, 8 * m:8 * m + 8], ident, w=[tfc, b.free], inc=m == 3)
            fx, fn, fa = (GMs[i][0:8, :] for i in range(3))
            t1 = tt(fx, b.ap[0:8, :], rst[0:8, :], ALU.mult, w=[t, trst])
            b.free = [t1]
            t1 = ts(fx, fx, VECS[0:8, VEC["b_forget"][0]:VEC["b_forget"][0] + 1], op0=ALU.add, w=[t1, tvec])
            t2 = ts(fn, fx, 0.0, op0=ALU.min, w=[t1])
            t3 = stt(fa, fn, -2.0, fx, ALU.mult, ALU.add, [t2])
            t4 = act(fa, fa, ACT.Exp, [t3], scale=-1.0)
            t4 = act(fa, fa, ACT.Ln, [t4, teps], bias=one[0:8, :])
            t5 = tt(fn, fn, fa, ALU.subtract, [t4])
            tok["c"] = scan(cT[0:8, :], ones[0:8, 0:1].to_broadcast([8, T]), fn, [t5])
            t5 = ts(fx, cT[0:8, :], -1.0, w=[tok["c"]])
            tok["cw"] = dma(SP, scratch, fx, s_cw, [t5])

        t0 = query_tile(0, S)
        trc = norm_columns()
        t0()
        query_tile(1, S)()
        bs = [main.next() for _ in range(4)]
        bf = [YB.next(), *(S.next() for _ in range(3))]
        tm4 = [None] * 4
        for k in range(KD):
            hi, lo, parts, end = ws.take(("win", k, VC), 5)
            for m in range(4):
                xs = slice(P * m, P * m + P)
                for x, w_, i in ((mh, hi, 0), (mh, lo, 1), (ml, hi, 2)):
                    for b, c in ((bs[m], slice(0, 256)), (bf[m], slice(256, 520))):
                        tm4[m] = mm(b.ap[:, 0:c.stop - c.start], x[k][:, xs], w_[:, c], start=k == 0 and i == 0,
                                    stop=k == KD - 1 and i == 2, w=[b.free, parts, ptok[k]] if i == 0 else (),
                                    inc=i == 2 and b is bf[m])
            ws.done[ws.u] = tm4[3]
            first_free = first_normed([k])
        tfc = [vcopy(CQ[:, 8 * m:8 * m + 8], bf[m].ap[:, 256:264], [tm4[m]]) for m in range(4)]
        for b, c in ((bs, slice(0, 256)), (bf, slice(256, 512))):
            for m in range(4):
                tok["vC"] = act(vC[m][:, c], b[m].ap[:, 0:256], w=[tm4[m], trc, tfc[m]], scale=rcol[:, m:m + 1])
                b[m].free = [tok["vC"], tfc[m]]
        query_tile(2, None, lambda k: forget_sums() if k == 5 else None)()
        b, tm4 = first_tile(QC + P * 3)
        queries(3, b, tm4)
        bank = TB.next()
        for m in range(4):
            tk = mm(bank.ap[:, 8 * m:8 * m + 8], cT[0:8, P * m:P * m + P], ident[0:8, 0:8],
                    w=[tok["c"], bank.free], inc=m == 3)
        tok["cq"] = vcopy(CQ[:, :], bank.ap[:, 0:32], [tk])
        bank.free = [tok["cq"]]
        work_free = [tm4]
        for r in (Pr, PTr, Br, Nr, Wr):
            for b in r.bufs:
                b.free = [work_free]
        background.append(pipeline([UnitC(2 * t + s, i) for t in range(4) for i in range(4) for s in range(2)]))

        xfree = [first_free, tok["qC"]]
        tcu8 = dma(SP, MF[:, :], cu8, s_c[2])
        for t in range(4):
            tok["kA"] = fm_tile(KA + P * t, kA[t][:, :], w=xfree)
        for t in range(4):
            tok["qA"] = fm_tile(QA + P * t, qA[t][:, :], 0.125, w=xfree)
        bs = [main.next() for _ in range(4)]
        tm4 = proj_tokens(bs, "win", VA, 4, hh, hl, htok, lambda k: step(1 + k % 2))
        for m in range(4):
            tok["vA"] = act(vA[m][:, :], bs[m].ap, w=[tm4[m]])
            bs[m].free = [tok["vA"]]
        background.append(pipeline([UnitA(h, i) for h in range(4) for i in range(4)]))
        tok["kB"] = fm_tile(KB, kB[:, :])
        vt = THr.next()
        t = fm_tile(VB, vt.ap, w=[tl])
        tvt = t
        for t in range(4):
            tok["qB"] = fm_tile(QB + P * t, qB[t][:, :], 0.125, w=xfree)
            if t == 0:
                bank = TB.next()
                for m in range(4):
                    t2 = tp(bank.ap[:, P * m:P * m + P], vt.ap[:, P * m:P * m + P], [tvt, bank.free], inc=m == 3)
                vt.free = [t2]
                tok["vB"] = act(vB[:, :], bank.ap, w=[t2])
                bank.free = [tok["vB"]]
        background.append(pipeline([UnitB(t, s, i) for t in range(4) for i in range(4) for s in range(2)]))

        def gate_tile(col, y, ty, hi, lo):
            b = main.next()
            t = proj(b.ap, "win", col, hh, hl, htok, b.free, between=slot)
            th = THr.next()
            t1 = act(th.ap, b.ap, ACT.Tanh, [t, th.free], scale=0.5)
            t1 = stt(th.ap, th.ap, 1.0, b.ap, ALU.add, ALU.mult, [t1])
            b.free = [t1]
            t1 = stt(th.ap, th.ap, 0.5, y, ALU.mult, ALU.mult, [t1, ty()])
            sp = split(th.ap, hi, lo, [t1])
            th.free = sp
            return sp

        def alias(name, like):
            return at(name, [P, T], F32R, place[like])

        ygh, ygl = {}, {}
        for t in range(4):
            ygh["c", t], ygl["c", t] = alias(f"ychi{t}", f"kC{t}"), alias(f"yclo{t}", f"qC{t}")
            ygh["a", t], ygl["a", t] = alias(f"yahi{t}", f"kA{t}"), alias(f"yalo{t}", f"qA{t}")
            ygh["b", t], ygl["b", t] = exB[t], alias(f"yblo{t}", f"qB{t}")
        ygt = {}

        def need(key):
            while key not in tok:
                step()
            return tok[key]

        for t in range(4):
            need(("yC", t))
            ygt["c", t] = gate_tile(GC + P * t, qC[t][:, :], lambda t=t: tok["yC", t], ygh["c", t][:, :],
                                    ygl["c", t][:, :])
        gmt = {}

        def gm_tile(d, j, buf, free=()):
            b = main.next()
            t = proj(b.ap, "win", GM + 1024 * j + P * d, hh, hl, htok, b.free, between=slot)
            gmt[d, j] = (act(buf, b.ap, ACT.Tanh, [t, *free], scale=0.5), buf)
            b.free = [gmt[d, j][0]]

        tcu8 = vcopy(CU8[:, :], MF[:, :], [tcu8], PO)
        for d in range(3):
            for j in range(3):
                gm_tile(d, j, GMs[3 * d + j][:, :], [tcu8])
        for t in range(4):
            need(("yA", t))
            ygt["a", t] = gate_tile(GA + P * t, qA[t][:, :], lambda t=t: tok["yA", t], ygh["a", t][:, :],
                                    ygl["a", t][:, :])
        for t in range(4):
            need(("yB", t))
            ygt["b", t] = gate_tile(GB + P * t, qB[t][:, :], lambda t=t: tok["yB", t], ygh["b", t][:, :],
                                    ygl["b", t][:, :])
        drain_background()
        att_free = [AC.last, DV.last, PE.last, PO.last]

        tsp = {}

        def rg_const():
            sl, nn = SM[:, 24:27], SM[:, 27:30]
            la = v("rg_lam", 0, 3)
            t = ts(nn, la, 0.0, op0=ALU.min, w=[tvec])
            t1 = stt(sl, nn, -2.0, la, ALU.mult, ALU.add, [t])
            t1 = act(sl, sl, ACT.Exp, [t1], scale=-1.0)
            t1 = act(sl, sl, ACT.Ln, [t1], bias=one)
            t1 = tt(sl, sl, nn, ALU.subtract, [t1])
            t1 = ts(SM[:, 30:33], sl, 8.0, w=[t1])
            tsp["sp8"] = [t1, ts(SM[:, 51:54], SM[:, 30:33], -1.0, w=[t1])]
            tsp["hb"] = ts(SM[:, 33:39], v("rg_br", 0, 6), 0.5)
            lb = v("hg_lb", 0, 3)
            t = tt(SM[:, 39:42], lb, lb, ALU.subtract)
            t = act(SM[:, 39:42], SM[:, 39:42], ACT.Exp, [t])
            t = recip(SM[:, 42:45], SM[:, 39:42], [t])
            t = tt(SM[:, 39:42], SM[:, 39:42], SM[:, 42:45], ALU.mult, [t])
            t = tt(SM[:, 45:48], SM[:, 39:42], SM[:, 39:42], ALU.subtract, [t])
            tsp["lb"] = ts(SM[:, 48:51], SM[:, 45:48], -1.0, 1.0, ALU.mult, ALU.add, [t])

        lbv, olb = SM[:, 45:48], SM[:, 48:51]

        rg_const()

        mtok = []
        Gr = Ring([g[:, :] for g in GMs])
        for d in range(8):
            if d >= 3:
                for j in range(3):
                    g = Gr.next()
                    gm_tile(d, j, g.ap, [g.free])
                    gmt[d, j] += (g,)
            else:
                for j in range(3):
                    gmt[d, j] += (Gr.next(),)
            prev = None
            for n, j in (("c", 2), ("a", 0), ("b", 1)):
                b = main.next()
                t = proj(b.ap, "up_" + n, P * d, [ygh[n, k][:, :] for k in range(4)],
                         [ygl[n, k][:, :] for k in range(4)], [ygt[n, k] for k in range(4)], b.free,
                         range(4))
                tg, gb, g = gmt[d, j]
                t = stt(gb, gb, 1.0, b.ap, ALU.add, ALU.mult, [t, tg])
                b.free = [t]
                if prev is not None:
                    t2 = tt(gb, gb, prev[0], ALU.add, [t, prev[1]])
                    prev[2].free = [t2]
                    t = t2
                prev = (gb, t, g)
            gb, t, g = prev
            a = act(mh[d], gb, w=[t, att_free], scale=0.5)
            l = stt(ml[d], gb, 0.5, mh[d].bitcast(F32), ALU.mult, ALU.subtract, [a])
            g.free = [a, l]
            mtok.append([a, l])
        up_free = [PE.last]
        s_x2 = [sem(f"s_xr{i}") for i in range(2)]
        xr = []
        for i in range(2):
            tok_ = dma(SP, X[:, 4 * T * i:4 * T * i + 4 * T].rearrange("p (k t) -> p k t", k=4),
                       xT[4 * P * i:4 * P * i + 4 * P, :].rearrange("(k p) t -> p k t", p=P), s_x2[i], up_free)
            xr += [tok_] * 4

        def c3(x, t):
            return x[:, T * t:T * t + T]

        a2 = Area(arena + 4 * KD * T)
        U3, A3, B3, G3 = (a2(n, 3 * T) for n in ("U3", "A3", "B3", "G3"))
        r1, r3, r6 = (a2(n, T)[:, :] for n in ("R1", "R3", "R6"))
        q3, k3, g64, g512 = (a2(n, 3 * T) for n in ("q3", "k3", "g64", "g512"))
        Es = [a2(f"E{i}", 3 * T) for i in range(2)]
        QH = [a2(f"QH{i}", 3 * T // 2) for i in range(2)]
        hv, gs = (a2(n, 3 * T) for n in ("hv", "gs"))
        ST = [a2(f"ST{p}", 2 * T) for p in range(3)]
        sch = [a2(f"sch{t}", T, F32R) for t in range(2)]
        scl = [a2(f"scl{t}", T, F32R) for t in range(2)]
        ZP = [a2(f"zp{i}", T + 16) for i in range(2)]
        offr = Ring([a2(f"off{i}", T) for i in range(2)] + [c3(g64, i) for i in range(2)])
        RGW = at("RGW", [P, 6 * P], F32, place["cst"] + 512 * 4)

        fg = lambda k: v("final_gain", k)
        gg = SM[:, 16:24]
        tgg = tt(gg, v("final_gain", 0, 8), v("mix_norm", 0, 8), ALU.mult, [tvec])
        acc1, acc2, r2 = c3(U3, 0), c3(U3, 1), c3(U3, 2)
        sq = Ring([c3(A3, i) for i in range(3)] + [c3(B3, i) for i in range(3)])
        w0 = [up_free, DV.last, AC.last, PO.last]
        ty, htok = [], []
        ta1 = ta2 = None
        b01 = [main.next() for _ in range(2)]
        for d in range(2):
            proj(b01[d].ap, "wo", P * d, mh, ml, mtok, b01[d].free, range(7), last=False)
        for d in range(8):
            if d < 2:
                b = b01[d]
                t = proj(b.ap, "wo", P * d, mh, ml, mtok, b.free, [7], first=False)
            else:
                b = main.next()
                t = proj(b.ap, "wo", P * d, mh, ml, mtok, b.free)
            t = tt(xk(d), b.ap, xk(d), ALU.add, [t, xr[d]])
            b.free = [t]
            ty.append(t)
            htok.append(gain_split(xk(d), gg[:, d:d + 1], hh[d], hl[d], [t, tgg, up_free]))
            o1, o2 = (Buf(acc1), Buf(acc2)) if d == 0 else (sq.next(), sq.next())
            t1 = act(o1.ap, xk(d), ACT.Square, [t, o1.free, w0])
            t2 = act(o2.ap, xk(d), ACT.Square, [t, o2.free, w0], scale=fg(d))
            if d:
                ta1 = tt(acc1, acc1, o1.ap, ALU.add, [t1, ta1])
                ta2 = tt(acc2, acc2, o2.ap, ALU.add, [t2, ta2])
                o1.free, o2.free = [ta1], [ta2]
            else:
                ta1, ta2 = t1, t2
        fence = [AC.last, DV.last, PO.last, PE.last]
        s_rw = sem("s_rw")
        trw = dma(SP, RGW[:, :], rgw, s_rw, fence)

        m3 = Ring([pb[i][:, :] for i in (0, 1, 2)])
        x5 = Ring([pb[i][:, :] for i in (3, 4, 5, 6, 7)])
        x4 = Ring([pb[i][:, :] for i in (3, 4)])
        ob = [Buf(pb[i][:, :]) for i in (5, 6, 7)]
        m3.bufs, x5.bufs = main.bufs[0:3], [main.bufs[3], *attention_banks]
        for i in range(2):
            x4.bufs[i] = x5.bufs[i]
        ob = x5.bufs[2:]

        heads_bg, gates_bg = [], []
        ticks = [0]

        def advance(gens):
            while gens:
                try:
                    next(gens[0])
                    return
                except StopIteration:
                    gens.pop(0)

        def tick(i=1):
            if i % 2:
                ticks[0] += 1
                if ticks[0] % 2:
                    advance(gates_bg)
                advance(heads_bg)

        def tile2(col, between=tick, ring=None):
            b = (ring or m3).next()
            return b, proj(b.ap, "win2", col, hh, hl, htok, b.free, between=between)

        def both_norms():
            bk1, bk2 = x5.next(), x5.next()
            tables(LNEXP)
            t1 = mm(bk1.ap, ones, acc1, w=[ta1, bk1.free], inc=True)
            t2 = mm(bk2.ap, ones, acc2, w=[ta2, bk2.free], inc=True)
            t = act(r1, bk1.ap, ACT.Ln, [t1, w0], bias=eps6, scale=1.0 / 1024)
            bk1.free = [t]
            tr1 = act(r1, r1, ACT.Exp, [t], scale=-0.5)
            t = tt(r3, r1, r1, ALU.mult, [tr1, w0])
            t = tt(r2, bk2.ap, r3, ALU.mult, [t, t2])
            bk2.free = [t]
            t = act(r2, r2, ACT.Ln, [t], bias=eps6, scale=1.0 / 1024)
            t = act(r2, r2, ACT.Exp, [t], scale=-0.5)
            tr = tt(r3, r1, r2, ALU.mult, [t])
            tr6 = tt(r6, r3, r3, ALU.mult, [tr], PO)
            return tr1, tr, tr6

        def both_columns():
            bank = x5.next()
            for m in range(4):
                tm_ = mm(bank.ap[:, m:m + 1], r3[0:1, P * m:P * m + P], ones[0:1, 0:1], w=[tr3, bank.free],
                         inc=m == 3)
            tc = vcopy(rcol2, bank.ap[:, 0:4], [tm_])
            bank.free = [tc]
            return tc

        rcol2 = SM[:, 60:64]
        tzp = [DV(lambda e, z=z: e.memset(z[:, 0:16], 0.0), fence) for z in ZP]
        zr = Ring(ZP)
        for b in zr.bufs:
            b.free = [tzp]
        tst = [PO(lambda e, s=s: e.memset(s[:, :], 0.0), fence) for s in ST]
        up_mid, down_mid = SM[:, 64:65], SM[:, 65:66]
        tmid = [PO(lambda e: e.memset(up_mid, MIDDLE)), PO(lambda e: e.memset(down_mid, -MIDDLE))]

        E3 = Es[0]
        tg = []
        pend = []
        for t in range(3):
            pend.append(tile2(BF + P * t, None))
            if t == 0:
                tr1, tr3, tr6 = both_norms()
        for t in range(3):
            b, tk_ = pend[t]
            e = c3(E3, t)
            t1 = tt(e, b.ap, r3, ALU.mult, [tk_, tr3, fence])
            b.free = [t1]
            tg.append(act(e, e, ACT.Exp, [t1], scale=-1.0))
        tq = []
        qt = Ring([c3(gs, i) for i in range(3)])
        for t in range(3):
            b, tk_ = tile2(BQ + P * t, None, x5)
            if t == 0:
                trc2 = both_columns()
            qt.bufs[t].free = tt(qt.bufs[t].ap, b.ap, r3, ALU.mult, [tk_, fence])
            b.free = [qt.bufs[t].free]
            e = c3(E3, t)
            t1 = ts(e, e, 1.0, op0=ALU.add, w=[tg[t]])
            t1 = recip(e, e, [t1])
            t1 = ts(e, e, olb[:, t:t + 1], lbv[:, t:t + 1], ALU.mult, ALU.add, [t1, tsp["lb"]])
            t2 = ts(c3(k3, t), e, -1.0, 1.0, ALU.mult, ALU.add, [t1, fence])
            t1 = ts(e, e, 2.0 ** -63, op0=ALU.max, w=[t1, t2])
            tg[t] = t1
        tlf, tG = tg, []

        def gates_steps():
            for t in range(3):
                e = c3(E3, t)
                tlf[t] = act(e, e, ACT.Ln, [tg[t]])
                tG.append(scan(c3(g64, t), m64, e, [tlf[t], fence]))
                tG.append(scan(c3(g512, t), ones[:, 0:1].to_broadcast([P, T]), e, [tlf[t], fence]))
            yield
            for t in range(3):
                x_, q_ = qt.bufs[t], c3(q3, t)
                t2 = act(q_, x_.ap, ACT.Tanh, [x_.free, fence], scale=0.5)
                t1 = stt(q_, q_, 1.0, x_.ap, ALU.add, ALU.mult, [t2])
                tq.append(ts(q_, q_, 0.5 * 0.125, w=[t1]))
            yield

        heads_bg.append(gates_steps())
        thv = []

        def blocks(x, h):
            return x[:, :].rearrange("p (b two r) -> p b two r", two=2, r=h)

        def hgrn_steps():
            merged = [[t] for t in tst]
            efree = [[tG], []]
            nth = [0]

            def factors(h, src):
                i = nth[0] % 2
                nth[0] += 1
                E, qh = Es[i], QH[i]
                g, d = blocks(src, h), blocks(E, h)
                nb = 3 * T // (2 * h)
                mid = g[:, :, 0, h - 1:h].to_broadcast([P, nb, h])
                w = [tG, efree[i], fence]
                t1 = tt(d[:, :, 0, :], mid, g[:, :, 0, :], ALU.subtract, w)
                t2 = tt(d[:, :, 1, :], g[:, :, 1, :], mid, ALU.subtract, w)
                t = act(E[:, :], E[:, :], ACT.Exp, [t1, t2])
                k_ = blocks(k3, h)
                tk_ = tt(d[:, :, 0, :], d[:, :, 0, :], k_[:, :, 0, :], ALU.mult, [t], PO if nth[0] > 2 else DV)
                qv = qh[:, :].rearrange("p (b r) -> p b r", r=h)
                tq_ = tt(qv, blocks(q3, h)[:, :, 1, :], d[:, :, 1, :], ALU.mult, [t, tq, efree[i], fence])
                return h, i, [tk_, tq_]

            def base():
                i = nth[0] % 2
                nth[0] += 1
                E = Es[i]
                g = g64[:, :].rearrange("p (b r) -> p b r", r=4)
                d = E[:, :].rearrange("p (b r) -> p b r", r=4)
                mid = g[:, :, 1:2].to_broadcast([P, 3 * P, 4])
                t = tt(d, g, mid, ALU.subtract, [tG, efree[i]])
                t1 = act(g64[:, :], E[:, :], ACT.Exp, [t, tmid], bias=up_mid)
                t2 = act(E[:, :], E[:, :], ACT.Exp, [t, t1, tmid], bias=down_mid, scale=-1.0)
                tq_ = tt(g64[:, :], g64[:, :], q3[:, :], ALU.mult, [t1, tq])
                tk_ = tt(E[:, :], E[:, :], k3[:, :], ALU.mult, [t2], PO)
                return 0, i, [tk_, tq_]

            def scores_64(part):
                h, i, tf = part
                E, qv = Es[i], QH[i]
                for hd in range(6):
                    p, r = hd // 2, 64 * (hd % 2)
                    bank = x5.next()
                    for m in range(4):
                        x0 = T * p + P * m
                        t = mm(bank.ap[0:64, 64 * m:64 * m + 64], E[r:r + 64, x0:x0 + 64],
                               qv[r:r + 64, x0 // 2:x0 // 2 + 64], w=[tf, bank.free], inc=m == 3)
                    dst = ST[p][0:64, T * (hd % 2):T * (hd % 2) + T].rearrange("p (m t) -> p m t", m=4)[:, :, 64:128]
                    tc = act(dst, bank.ap[0:64, 0:256].rearrange("p (m t) -> p m t", m=4), w=[t, tst[p]])
                    merged[p] = [tc, *merged[p]]
                    bank.free = [tc]
                    if hd % 2:
                        yield
                efree[i] = [t]

            def scores_near(part):
                h, i, tf = part
                l = LEVELS.index(h)
                E, qv = Es[i], QH[i]
                for hd in range(6):
                    p, r = hd // 2, 64 * (hd % 2)
                    bank = x5.next()
                    for m in range(4):
                        for u in range(2):
                            x0 = T * p + P * m + 64 * u
                            t = mm(bank.ap[64 * u:64 * u + 64, 32 * m:32 * m + 32], E[r:r + 64, x0:x0 + 64],
                                   qv[r:r + 64, x0 // 2:x0 // 2 + 32], w=[tf, bank.free], inc=m == 3)
                    for u in range(2):
                        rows = slice(64 * u, 64 * u + 64)
                        dst = ST[p][rows, T * (hd % 2):T * (hd % 2) + T].rearrange(
                            "p (m u b two r) -> p m u b two r", u=2, m=4, two=2, r=h)[:, :, u, :, 1, :]
                        msk = lvmask(l)[rows, :].rearrange("p (m b r) -> p m b r", m=4, r=h)
                        src = bank.ap[rows, 0:128].rearrange("p (m b r) -> p m b r", m=4, r=h)
                        tc = DV(lambda e, dst=dst, msk=msk, src=src: e.copy_predicated(dst, msk, src),
                                [t, merged[p], tcu8])
                    merged[p] = [tc]
                    bank.free = [tc]
                    if hd % 2:
                        yield
                efree[i] = [t]

            def scores_base(part):
                _, i, tf = part
                E = Es[i]
                for hd in range(6):
                    p, r = hd // 2, 64 * (hd % 2)
                    bank = x5.next()
                    for m in range(4):
                        x0 = T * p + P * m
                        t = mm(bank.ap[:, P * m:P * m + P], E[r:r + 64, x0:x0 + P], g64[r:r + 64, x0:x0 + P],
                               w=[tf, bank.free], inc=m == 3)
                    dst = ST[p][:, T * (hd % 2):T * (hd % 2) + T]
                    tc = DV(lambda e, dst=dst, src=bank.ap: e.copy_predicated(dst, b4mask, src),
                            [t, merged[p], tcu8])
                    merged[p] = [tc]
                    bank.free = [tc]
                    yield
                efree[i] = [t]

            def near_values():
                for p in range(3):
                    for m in range(4):
                        for r in (0, 64):
                            hd = 2 * p + r // 64
                            t = mm(ob[p].ap[r:r + 64, P * m:P * m + P],
                                   hv[:, 384 * m + 64 * hd:384 * m + 64 * hd + 64],
                                   ST[p][:, T * (hd % 2) + P * m:T * (hd % 2) + P * m + P], start=m == 0,
                                   stop=False, w=[merged[p], thv, ob[p].free], inc=m == 3, skip=True)
                    yield

            def far(part, last):
                h, i, tf = part
                E, qv = Es[i], QH[i]
                pairs = [(0, 0, 2, 2), (1, 0, 2, 2)] if h == 256 else [(0, 0, 1, 1), (2, 1, 3, 1)]
                late = []
                for hd in range(6):
                    p, r = hd // 2, 64 * (hd % 2)
                    x0 = T * p
                    bank = x4.next()
                    off = 0
                    for s, c0, t0, n in pairs:
                        t = mm(bank.ap[:, off:off + P * n], E[r:r + 64, x0 + P * s:x0 + P * s + P],
                               qv[r:r + 64, x0 // 2 + P * c0:x0 // 2 + P * (c0 + n)], w=[tf, bank.free],
                               inc=True)
                        off += P * n
                    sc = offr.next()
                    tc = act(sc.ap[:, 0:off], bank.ap[:, 0:off], w=[t, sc.free, fence])
                    bank.free = [tc]
                    late.append((hd, sc, tc))
                    if len(late) > 2:
                        far_values(p - 1, late[0:2], pairs, last)
                        late = late[2:]
                    yield
                efree[i] = [t]
                far_values(2, late, pairs, last)
                yield

            def far_values(p, both, pairs, last):
                off = 0
                for s, c0, t0, n in pairs:
                    for hd, sc, tc in both:
                        r = 64 * (hd % 2)
                        t = mm(ob[p].ap[r:r + 64, P * t0:P * (t0 + n)], hv[:, 384 * s + 64 * hd:384 * s + 64 * hd + 64],
                               sc.ap[:, off:off + P * n], start=False, stop=last, w=[both[0][2], both[1][2], thv],
                               inc=True, skip=True)
                    off += P * n
                for hd, sc, tc in both:
                    sc.free = [t]
                if last:
                    tok["ho", p] = t

            parts = [factors(64, g512)]
            yield
            parts.append(factors(32, g64))
            yield
            for h in (16, 8, 4, 0):
                yield from (scores_64 if h == 16 else scores_near)(parts.pop(0))
                parts.append(factors(h, g64) if h else base())
                yield
                if not h:
                    yield
            yield from scores_near(parts.pop(0))
            parts.append(factors(128, g512))
            yield
            yield
            yield from scores_base(parts.pop(0))
            parts.append(factors(256, g512))
            yield
            for b, o in zip(offr.bufs[2:], range(2)):
                b.free = efree
            yield
            yield
            yield from near_values()
            yield
            yield from far(parts.pop(0), False)
            yield from far(parts.pop(0), True)

        heads_bg.append(hgrn_steps())
        bs = [x5.next() for _ in range(4)]
        tm4 = proj_tokens(bs, "win2", BV, 3, hh, hl, htok,
                          lambda k: advance(heads_bg) if k in (0, 1, 3, 6) else None)
        for m in range(4):
            t = act(hv[:, 384 * m:384 * m + 384], bs[m].ap[:, 0:384], w=[tm4[m], trc2, fence],
                    scale=rcol2[:, m:m + 1])
            bs[m].free = [t]
            thv.append(t)

        tu = []
        for t in range(3):
            b, tk_ = tile2(AU + P * t, tick if t else None)
            z = zr.next()
            tz = tt(z.ap[:, 16:16 + T], b.ap, r3, ALU.mult, w=[tk_, z.free])
            b.free = [tz]
            u = c3(U3, t)
            cw = VEC["rg_cw"][0] + 4 * t
            tt_ = ts(u, z.ap[:, 16:16 + T], VECS[:, cw + 3:cw + 4], v("rg_cb", t), ALU.mult, ALU.add, [tz, fence])
            for j in range(3):
                tt_ = stt(u, z.ap[:, 13 + j:13 + j + T], VECS[:, cw + j:cw + j + 1], u, ALU.mult, ALU.add, [tt_])
            z.free = [tt_]
            tu.append(tt_)

        def rg_steps():
            tr_, ti_ = [], []
            for t in range(3):
                for g, dst, lst in ((0, A3, tr_), (1, B3, ti_)):
                    b = x5.next()
                    tm_ = mm(b.ap, RGW[:, P * (2 * t + g):P * (2 * t + g) + P], c3(U3, t),
                             w=[tu[t], trw, b.free], inc=True)
                    ta = act(c3(dst, t), b.ap, ACT.Tanh, [tm_, tsp["hb"], fence],
                             bias=SM[:, 33 + 3 * g + t:34 + 3 * g + t], scale=0.5)
                    b.free = [ta]
                    lst.append(ts(c3(dst, t), c3(dst, t), 0.5, 0.5, ALU.mult, ALU.add, [ta]))
                yield
            for t in range(3):
                a, bb, u, g = c3(A3, t), c3(B3, t), c3(U3, t), c3(G3, t)
                t1 = act(g, a, ACT.Tanh, [tr_[t], tsp["sp8"], fence], scale=SM[:, 30 + t:31 + t])
                t2 = act(a, a, ACT.Exp, [t1], scale=SM[:, 51 + t:52 + t])
                t3 = tt(bb, bb, u, ALU.mult, [ti_[t]])
                t4 = act(u, a, ACT.Square, [t2, t3])
                t4 = stt(g, u, 1.0, g, ALU.add, ALU.mult, [t4, t1])
                tr_[t], ti_[t] = [t2], [t3, t4]
                yield
            t = act(G3[:, :], G3[:, :], ACT.Sqrt, [ti_[0], ti_[1], ti_[2]])
            tables(EXPTANH)
            for i in range(3):
                t1 = tt(c3(B3, i), c3(B3, i), c3(G3, i), ALU.mult, [t])
                tok["rg", i] = scan(c3(U3, i), c3(A3, i), c3(B3, i), [t1, tr_[i]])
                yield

        gates_bg.append(rg_steps())

        YMH, YML = {}, {}
        ytok = {}

        txb = []

        def residual():
            k = len(txb)
            t = act(xk(k), xk(k), w=[htok[k], ty[k]], scale=fg(k))
            txb.append(tt(xk(k), xk(k), r1, ALU.mult, [t, tr1], PO))


        scy = [at(f"scy{t}", [P, T], F32, place[f"scl{t}"])[:, :] for t in range(2)]
        scc = [at(f"scc{t}", [P, T], F32, place[f"sch{t}"])[:, :] for t in range(2)]
        cc, cz = [], []
        for t in range(2):
            b, tk_ = tile2(CC + P * t)
            t1 = tt(scc[t], b.ap, r6, ALU.mult, [tk_, tr6, fence])
            b.free = [t1]
            cc.append(t1)
            residual()
        for t in range(2):
            b, tk_ = tile2(CV + P * t)
            z = zr.next()
            t1 = tt(z.ap[:, 16:16 + T], b.ap, scc[t], ALU.mult, [tk_, cc[t], z.free])
            b.free = [t1]
            y = scy[t]
            cw = VEC["sc_cw"][0] + 3 * t
            t1 = ts(y, z.ap[:, 16:16 + T], VECS[:, cw + 2:cw + 3], w=[t1, fence])
            for j in range(2):
                t1 = stt(y, z.ap[:, 14 + j:14 + j + T], VECS[:, cw + j:cw + j + 1], y, ALU.mult, ALU.add, [t1])
            z.free = [t1]
            cz.append(tt(y, y, r3, ALU.mult, [t1], PO))
            residual()
        while gates_bg:
            tick()
        tgs = []
        for t in range(3):
            b, tk_ = tile2(BG + P * t)
            x_, g = c3(B3, t), c3(gs, t)
            t1 = tt(x_, b.ap, r3, ALU.mult, [tk_, tok["rg", t]])
            b.free = [t1]
            t2 = act(g, x_, ACT.Tanh, [t1, tq], scale=0.5)
            t1 = stt(g, g, 1.0, x_, ALU.add, ALU.mult, [t2])
            tgs.append(ts(g, g, 0.5, w=[t1]))
            residual()
        a3g = []
        for t in range(3):
            b, tk_ = tile2(AG + P * t)
            if len(txb) < KD:
                residual()
            g, a_, u = c3(G3, t), c3(A3, t), c3(U3, t)
            t0 = tok["rg", t]
            tz = tt(g, b.ap, r3, ALU.mult, [tk_, t0])
            b.free = [tz]
            t1 = act(a_, g, ACT.Square, [tz, t0])
            t1 = ts(a_, a_, 0.044715, 1.0, ALU.mult, ALU.add, [t1])
            t1 = tt(a_, a_, g, ALU.mult, [t1])
            t1 = act(a_, a_, ACT.Tanh, [t1], scale=0.7978845608028654)
            t1 = stt(g, a_, 1.0, g, ALU.add, ALU.mult, [t1])
            t1 = stt(u, u, 0.5, g, ALU.mult, ALU.mult, [t1])
            a3g.append(t1)
        while heads_bg:
            tick()
        win2_free = []
        hfree = [PE.last]
        rgh = [at(f"rgh{t}", [P, T], F32R, place["A3"] + 4 * T * t) for t in range(3)]
        rgl = [at(f"rgl{t}", [P, T], F32R, place["B3"] + 4 * T * t) for t in range(3)]
        hgh = [at(f"hgh{t}", [P, T], F32R, place["E0"] + 4 * T * t) for t in range(3)]
        hgl = [at(f"hgl{t}", [P, T], F32R, place["E1"] + 4 * T * t) for t in range(3)]
        mixh = {k: m[:, :] for k, m in zip((0, 1, 2, 3, 4, 5, 6, 7), [*rgh, *hgh, *sch])}
        mixl = {k: m[:, :] for k, m in zip((0, 1, 2, 3, 4, 5, 6, 7), [*rgl, *hgl, *scl])}

        def head_norms(items):
            for i in range(len(items) + 1):
                if i < len(items):
                    k, src, dst, sq, t, tsq, gate = items[i]
                    bank = x4.next()
                    tm_ = mm(bank.ap, bdones, sq, w=[tsq, bank.free], inc=True)
                    t1 = act(sq, bank.ap, ACT.Ln, [tm_], bias=eps6, scale=1.0 / 64)
                    bank.free = [t1]
                    tf = act(sq, sq, ACT.Exp, [t1], scale=-0.5)
                if i:
                    k_, src_, dst_, sq_, t_, tf_, gate_ = last
                    t1 = stt(dst_, src_, v("mix_gain", k_), sq_, ALU.mult, ALU.mult, [tf_, t_, hfree])
                    if gate_ is not None:
                        t1 = tt(dst_, dst_, gate_, ALU.mult, [t1, tgs])
                    ytok[k_] = split(dst_, mixh[k_], mixl[k_], [t1, hfree, t_], DV if k_ in (3, 4, 5) else PO)
                last = (k, src, dst, sq, t, tf, gate)
                yield

        def norm_steps():
            tables(LNEXP)
            th_ = [act(c3(g64, p), ob[p].ap, ACT.Square, [tok["ho", p], hfree]) for p in range(3)]
            yield
            tr_ = [act(c3(G3, t), c3(U3, t), ACT.Square, [a3g[t]]) for t in range(3)]
            yield
            yield
            yield from head_norms([(3 + p, ob[p].ap, c3(k3, p), c3(g64, p), tok["ho", p], th_[p], c3(gs, p))
                                   for p in range(3)]
                                  + [(t, c3(U3, t), c3(U3, t), c3(G3, t), a3g[t], tr_[t], None) for t in range(3)])

        sc_items = []

        heads_bg.append(norm_steps())
        for t in range(2):
            b, tk_ = tile2(CB + P * t)
            y = scy[t]
            t1 = tt(y, b.ap, y, ALU.mult, [tk_, cz[t]])
            b.free = [t1]
            sc_items.append((6 + t, y, y, scc[t], t1, act(scc[t], y, ACT.Square, [t1]), None))
        def later(gen):
            yield
            yield from gen

        heads_bg.append(later(head_norms(sc_items)))
        win2_free = [PE.last]

        def wout(b, d, ks, first, last, between=None):
            return proj(b.ap, "wout", P * d, mixh, mixl, ytok, b.free, ks, first=first, last=last, between=between)

        wb = [m3.next() for _ in range(3)]
        for ks in (WK[:3], WK[3:6]):
            while not all(k in ytok for k in ks):
                tick()
            for d in range(3):
                wout(wb[d], d, ks, ks[0] == 3, False, lambda i: tick())
        while heads_bg:
            tick()
        mix_free = [AC.last, DV.last, PO.last]

        main = Ring(pb)
        main.bufs = [*m3.bufs, *x5.bufs]

        def norm_stats(sqbufs, accb, rst, w0):
            state = {"t": None}
            last = KD - 1

            def add(k, src, t):
                o = Buf(accb) if k == 0 else sqbufs.next()
                t1 = act(o.ap, src, ACT.Square, [t, o.free, *w0])
                if k == last:
                    state["last"] = o.ap, t1
                    return
                if k:
                    t1 = tt(accb, accb, o.ap, ALU.add, [t1, state["t"]])
                    o.free = [t1]
                state["t"] = t1
                return t1

            def end(bank):
                tables(LNEXP)
                mm(bank.ap, ones, accb, stop=False, w=[state["t"], bank.free])
                t = mm(bank.ap, ones, state["last"][0], start=False, w=[state["last"][1]], inc=True)
                t = act(rst, bank.ap, ACT.Ln, [t, *w0], bias=eps6, scale=1.0 / 1024)
                bank.free = [t]
                return act(rst, rst, ACT.Exp, [t], scale=-0.5)

            return add, end

        rff = at("rff", [P, T], F32, 227264)[:, :]
        add, end = norm_stats(Ring([c3(g512, 0), c3(g512, 1)]), c3(g512, 2), rff, [mix_free, hfree])
        tx1 = []
        htok = []
        for d in range(8):
            b = wb[d] if d < 3 else main.next()
            t = wout(b, d, WK[6:] if d < 3 else WK, d >= 3, True)
            if d == 2:
                main.i = 3
            t = tt(xk(d), b.ap, xk(d), ALU.add, [t, txb[d]])
            b.free = [t]
            tx1.append(t)
            htok.append(gain_split(xk(d), v("ffn_norm", d), hh[d], hl[d], [t, win2_free]))
            add(d, xk(d), t)
        fence2 = [AC.last, DV.last, PO.last, PE.last]

        a3 = Area(arena + 4 * KD * T)
        FH = [a3(f"fh{j}", T, F32R) for j in range(NPAIR)]
        FL = [a3(f"fl{j}", T, F32R) for j in range(NPAIR)]
        ffn_work = a3.p
        zf = [a3(f"zf{i}", T + 16) for i in range(4)]
        CVr = Ring([a3(f"cv{i}", T) for i in range(6)])
        assert a3.p <= 227264
        for b in CVr.bufs:
            b.free = fence2
        tzf = [DV(lambda e, z=z: e.memset(z[:, 0:16], 0.0), fence2) for z in zf]
        zfr = Ring(zf)
        for b in zfr.bufs:
            b.free = [tzf]
        ftok = []

        def conv_tile(col, cwi):
            b = main.next()
            t = proj(b.ap, "ffn_up", col, hh, hl, htok, b.free)
            z, o = zfr.next(), CVr.next()
            if cwi == 0:
                tok["ffn"] = end(main.next())
            tz = tt(z.ap[:, 16:16 + T], b.ap, rff, ALU.mult, w=[t, z.free, tok["ffn"]])
            cw = VEC["ffn_cw"][0] + 3 * cwi
            t = ts(o.ap, z.ap[:, 16:16 + T], VECS[:, cw + 2:cw + 3], w=[tz, o.free])
            b.free = [tz]
            for j in range(2):
                t = stt(o.ap, z.ap[:, 14 + j:14 + j + T], VECS[:, cw + j:cw + j + 1], o.ap, ALU.mult, ALU.add,
                        [t, tz])
            z.free = [t]
            return o, t

        for j in range(NPAIR):
            g, tg_ = conv_tile(P * j, j)
            th = CVr.next()
            t1 = act(th.ap, g.ap, ACT.Tanh, [tg_, th.free], scale=0.5)
            t1 = stt(g.ap, th.ap, 1.0, g.ap, ALU.add, ALU.mult, [t1])
            th.free = [t1]
            u, tu_ = conv_tile(2816 + P * j, NPAIR + j)
            t1 = stt(u.ap, u.ap, 0.5, g.ap, ALU.mult, ALU.mult, [tu_, t1])
            g.free = [t1]
            sp = split(u.ap, FH[j][:, :], FL[j][:, :], [t1, fence2])
            u.free = sp
            ftok.append(sp)
        up_done = [AC.last, DV.last, PO.last, PE.last]
        PR = at("PR", [P, 2 * T], F32, ffn_work)
        PH = at("PH", [P, 2 * T], F32R, ffn_work + 8 * T)
        PL = at("PL", [P, 2 * T], F32R, ffn_work + 16 * T)
        s_p = sem("s_p")
        tp_ = dma(SP, PR[:, :].rearrange("p (k t) -> p k t", k=2), pT.rearrange("(k p) t -> p k t", p=P), s_p,
                  up_done)
        psp = split(PR[:, :], PH[:, :], PL[:, :], [tp_, up_done], DV)
        tx2 = []
        gtok = []
        for d in range(8):
            b = main.next()
            for k0 in range(0, NPAIR, 8):
                n = min(8, NPAIR - k0)
                for k in range(k0, k0 + n):
                    hi, lo, parts, e_ = ws.take(("ffn_dn", k, P * d))
                    mm(b.ap, hi, FH[k][:, :], start=k == 0, stop=False, w=[b.free, parts[0], ftok[k]])
                    mm(b.ap, hi, FL[k][:, :], start=False, stop=False)
                    t = mm(b.ap, lo, FH[k][:, :], start=False, stop=k == NPAIR - 1, w=[parts[1]],
                           inc=e_ or k == NPAIR - 1)
                    if e_:
                        ws.done[ws.u] = t
            t = tt(xk(d), b.ap, xk(d), ALU.add, [t, tx1[d]])
            b.free = [t]
            tx2.append(t)
            gtok.append(split(xk(d), hh[d], hl[d], [t, up_done]))
        dn_free = [PE.last]
        a4 = Area(arena + 4 * KD * T)
        PPA = a4("PP", KD * T)
        PP = [PPA[:, T * d:T * d + T] for d in range(8)]
        t4r = Ring([a4(f"t4{i}", T) for i in range(4)])
        sq4 = Ring([a4(f"sq4{i}", T) for i in range(2)])
        acc4, rs4 = a4("acc4", T)[:, :], a4("rs4", T)[:, :]
        tpp = []
        ph = [c3(PH, k) for k in range(2)]
        pl = [c3(PL, k) for k in range(2)]
        for d in range(8):
            b = main.next()
            t = proj(b.ap, "ple_p", P * d, ph, pl, [psp, psp], b.free, range(2))
            t = act(PP[d], b.ap, w=[t, dn_free])
            b.free = [t]
            tpp.append(t)
        add, end = norm_stats(sq4, acc4, rs4, [dn_free])

        def embed(b, d, t, c):
            n = c.stop - c.start
            x_ = t4r.next()
            y = x_.ap[:, 0:n]
            t1 = act(y, b.ap[:, 0:n], ACT.Tanh, [t, x_.free, dn_free], scale=0.5)
            b.free = [t1]
            t1 = stt(y, y, 1.0, PP[d][:, c], ALU.add, ALU.mult, [t1, tpp[d]])
            t1 = stt(xk(d)[:, c], y, 0.5, xk(d)[:, c], ALU.mult, ALU.add, [t1, tx2[d], gtok[d]])
            x_.free = [t1]
            return t1

        tx3 = []
        for d in range(6):
            b = main.next()
            t = proj(b.ap, "ple_g", P * d, hh, hl, gtok, b.free)
            t1 = embed(b, d, t, slice(0, T))
            tacc4 = add(d, xk(d), t1)
            tx3.append(act(PP[d], xk(d), w=[t1], scale=v("final2", d)))
        last = {}
        for d in (6, 7):
            for k in range(KD):
                last[d, k] = ws.take(("ple_g", k, P * d))
        sq67 = [b.ap for b in sq4.bufs]
        sq67_free = [b.free for b in sq4.bufs]
        s_o = [sem(f"s_o{i}") for i in range(2)]
        ends = {}
        H = T // 2
        cs = [slice(0, H), slice(H, T)]
        tx67, tsq = {}, {}

        def half_tile(half, d):
            c, b = cs[half], main.next()
            for k in range(KD):
                hi, lo, parts, _ = last[d, k]
                mm(b.ap[:, 0:H], hi, hh[k][:, c], start=k == 0, stop=False, w=[b.free, parts, gtok[k]])
                mm(b.ap[:, 0:H], hi, hl[k][:, c], start=False, stop=False)
                t = mm(b.ap[:, 0:H], lo, hh[k][:, c], start=False, stop=k == KD - 1, inc=k == KD - 1)
            return b, t

        def half_embed(half, d, b, t):
            c = cs[half]
            t1 = tx67[half, d] = embed(b, d, t, c)
            tsq[half, d] = act(sq67[d - 6][:, c], xk(d)[:, c], ACT.Square, [t1, sq67_free[d - 6]])

        def half_out(half, pool):
            c, b = cs[half], main.next()
            tables(LNEXP)
            mm(b.ap[:, 0:H], ones, acc4[:, c], stop=False, w=[tacc4, b.free])
            mm(b.ap[:, 0:H], ones, sq67[0][:, c], start=False, stop=False, w=[tsq[half, 6]])
            t = mm(b.ap[:, 0:H], ones, sq67[1][:, c], start=False, w=[tsq[half, 7]], inc=True)
            t = act(rs4[:, c], b.ap[:, 0:H], ACT.Ln, [t], bias=eps6, scale=1.0 / 1024)
            b.free = [t]
            trs = act(rs4[:, c], rs4[:, c], ACT.Exp, [t], scale=-0.5)
            for g in range(4):
                tg_ = []
                for d in (2 * g, 2 * g + 1):
                    if d > 5:
                        tg_.append(stt(PP[d][:, c], xk(d)[:, c], v("final2", d), rs4[:, c], ALU.mult, ALU.mult,
                                       [trs, tx67[half, d]]))
                    else:
                        tg_.append(tt(PP[d][:, c], PP[d][:, c], rs4[:, c], ALU.mult, [trs, tx3[d]],
                                      PO if d in pool else DV))
                ends[g % 2] = dma(SP, out[2 * P * g:2 * P * g + 2 * P, c].rearrange("(k p) t -> p k t", p=P),
                                  PPA[:, 2 * T * g:2 * T * g + 2 * T].rearrange("p (k t) -> p k t", k=2)[:, :, c],
                                  s_o[g % 2], tg_)

        for d in (6, 7):
            half_embed(0, d, *half_tile(0, d))
        b6, t6 = half_tile(1, 6)
        half_out(0, (0, 1, 3, 5))
        tables(EXPTANH)
        half_embed(1, 6, b6, t6)
        half_embed(1, 7, *half_tile(1, 7))
        half_out(1, (3, 5))
        SP.wait(list(ends.values()))
        assert ws.u == len(units) - 1 and ws.b == len(units[-1])

        block = ctx.enter_context(nc.Block())

        @block.sync
        def _(eng):
            SP.replay(eng)

        @block.scalar
        def _(eng):
            AC.replay(eng)

        @block.vector
        def _(eng):
            DV.replay(eng)

        @block.gpsimd
        def _(eng):
            PO.replay(eng)

        @block.tensor
        def _(eng):
            PE.replay(eng)


def constants():
    p = np.arange(P)[:, None]
    c = np.arange(T)[None, :]
    ident = np.eye(P, dtype=np.float32)
    ones = np.ones((P, P), np.float32)
    bd = np.kron(np.eye(2), np.ones((64, 64))).astype(np.float32)
    mask = np.where(p >= np.arange(P)[None, :], 0.0, NEG).astype(np.float32)
    da = np.where(p - (c - 384) >= 0, -(p - (c - 384)), NEG).astype(np.float32)
    cb = np.arange(256)[None, :]
    dist = p - cb + P
    db = np.where((dist >= 0) & (dist < P), -dist, NEG).astype(np.float32)
    m64 = np.broadcast_to((np.arange(T) % 64 != 0).astype(np.float32), (P, T))
    cst = np.concatenate([ident, ones, bd, mask, da, db, m64], 1).astype(np.float32)
    s = np.arange(P)[:, None]
    u8 = []
    for h in LEVELS:
        t = np.arange(64).reshape(-1, 2, h)[:, 1, :].ravel()[None, :]
        m = (s % 64 // (2 * h) == t // (2 * h)) & (s % (2 * h) < h)
        u8.append(np.tile(m, (1, 4)))
    t = np.arange(P)[None, :]
    u8.append(np.tile((s // 4 == t // 4) & (s <= t), (1, 4)))
    return np.ascontiguousarray(cst), np.ascontiguousarray(np.concatenate(u8, 1).astype(np.float32))


def kernel(**inputs):
    import numpy as _np
    import concourse.bacc as _bacc
    from concourse import mybir as _mybir
    from concourse.bass_utils import run_bass_kernel_spmd as _run

    g = {k: _np.asarray(a) for k, a in inputs.items()}
    heads = [h for t in range(4) for h in (t, t + 4)]
    perm = _np.concatenate([_np.arange(64 * h, 64 * h + 64) for h in heads])
    win = g["w_in"][0].copy()
    win[:, QB:QB + 512] = g["w_in"][0][:, QB + perm]
    win[:, GB:GB + 512] = g["w_in"][0][:, GB + perm]
    mats = {"win": win, "up_a": g["w_up_a"][0], "up_b": g["w_up_b"][0][perm], "up_c": g["w_up_c"][0],
            "wo": g["w_o"][0], "win2": g["w_in_2"][0], "wout": g["w_out_2"][0], "ffn_up": g["ffn_w_up_2"][0],
            "ffn_dn": g["ffn_w_down_2"][0], "ple_p": g["ple_w_proj_2"][0], "ple_g": g["ple_w_gate_2"][0]}
    wall = _np.concatenate([mats[n][P * k:P * k + P, c:c + w] for u in plan_units() for n, k, c, w in u], 1)

    def cols(a):
        return a.reshape(-1, P).T

    def rep(a):
        return _np.tile(a.reshape(1, -1), (P, 1))

    bf = _np.tile(g["b_forget"][0], P // 8).reshape(P, 1)
    cwr = g["rg_conv_w_2"][0].reshape(4, 3, P).transpose(2, 1, 0).reshape(P, 12)
    cws = g["sc_conv_w_2"][0].reshape(3, 2, P).transpose(2, 1, 0).reshape(P, 6)
    cwf = g["ffn_conv_w_2"][0].reshape(3, 44, P).transpose(2, 1, 0).reshape(P, 132)
    vec = _np.concatenate([
        cols(g["norm_gain"][0]), cols(g["final_gain"]), cols(g["norm_mix_gain_2"][0]), cols(g["subln_gain"][0]),
        rep(g["sinks"][0]), bf, rep(g["lambda_q1"][0]), rep(g["lambda_k1"][0]), rep(g["lambda_q2"][0]),
        rep(g["lambda_k2"][0]), cwr, cols(g["rg_conv_b_2"][0]), cols(g["rg_b_r_2"][0].ravel()),
        cols(g["rg_b_i_2"][0].ravel()), cols(g["rg_lambda_2"][0]), cols(g["hg_lower_bounds_2"][0]), cws,
        cols(g["mix_out_gain_2"][0]), cols(g["norm_ffn_gain_2"][0]), cwf, cols(g["final_norm_gain_2"])], 1)
    rgw = _np.zeros((P, 6 * P), _np.float32)
    for t in range(3):
        for j, n in enumerate(("rg_w_r_2", "rg_w_i_2")):
            for s in range(2):
                o = P * (2 * t + j) + 64 * s
                rgw[64 * s:64 * s + 64, o:o + 64] = g[n][0, 2 * t + s]
    cst, cu8 = constants()
    arrays = {"wall": wall, "xT": g["x"][0].T, "pT": g["p_2"][0, 0].T, "vec": vec, "cst": cst, "cu8": cu8,
              "rgw": rgw}
    nc = _bacc.Bacc("TRN2", target_bir_lowering=False, num_devices=1)
    aps = []
    for n, a in arrays.items():
        arrays[n] = _np.ascontiguousarray(a)
        aps.append(nc.dram_tensor(f"in_{n}", a.shape, _mybir.dt.from_np(a.dtype), kind="ExternalInput").ap())
    out = nc.dram_tensor("outT", (1024, T), _mybir.dt.float32, kind="ExternalOutput").ap()
    build(nc, *aps, out)
    r = _run(nc, [{f"in_{n}": a for n, a in arrays.items()}], core_ids=[0])
    return r.results[0]["outT"].T.reshape(1, T, 1024)
```
